# Optimizing a Trainium2 kernel written in Bass

```python
import math
import jax, jax.numpy as jnp
from jax import lax
import numpy as np

D_MODEL = 1024
BATCH = 1
SEQ = 256
DEPTH = 1

CHUNK = 64
HEAD_DIM = 64
N_Q_HEADS = 16
N_KV_HEADS = 2
Q_PER_KV = N_Q_HEADS // N_KV_HEADS
WINDOW = 128
WINDOW_CHUNKS = WINDOW // CHUNK
KEYS_PER_BLOCK = WINDOW_CHUNKS * CHUNK
ATTN_WIDTH = N_Q_HEADS * HEAD_DIM
KV_WIDTH = N_KV_HEADS * HEAD_DIM
LRU_WIDTH = D_MODEL
LRU_BLOCKS = 16
LRU_BLOCK_DIM = LRU_WIDTH // LRU_BLOCKS
CONV_WIDTH = 4
LRU_C = 8.0
N_EXPERTS = 32
TOP_K = 4
D_FF = D_MODEL
SWIGLU_ALPHA = 1.702
SWIGLU_LIMIT = 7.0
EXPERT_BLOCK = 256
RMS_EPS = 1e-6
N_MOD = 6
SPLITS = (ATTN_WIDTH, KV_WIDTH, KV_WIDTH, LRU_WIDTH, LRU_WIDTH, D_MODEL, D_MODEL)
PROJ_WIDTH = sum(SPLITS)
SPLIT_POINTS = tuple(int(v) for v in np.cumsum(SPLITS)[:-1])

kernel_name = "hybrid_swa_rglru_moe_block"

def rms_norm(x, g):
    xf = x.astype(jnp.float32)
    y = xf * lax.rsqrt(jnp.mean(xf * xf, axis=-1, keepdims=True) + RMS_EPS) * g.astype(jnp.float32)
    return y.astype(x.dtype)

def alibi_slopes(n_heads):
    return 2.0 ** (-8.0 * jnp.arange(1, n_heads + 1, dtype=jnp.float32) / n_heads)

def sliding_window_attention(q, k, v, sinks):
    B, S, _ = q.shape
    nC = S // CHUNK
    q = q.reshape(B, nC, CHUNK, N_KV_HEADS, Q_PER_KV, HEAD_DIM)
    k = k.reshape(B, nC, CHUNK, N_KV_HEADS, HEAD_DIM)
    v = v.reshape(B, nC, CHUNK, N_KV_HEADS, HEAD_DIM)

    def band(t):
        parts = [jnp.pad(t, ((0, 0), (p, 0), (0, 0), (0, 0), (0, 0)))[:, :nC]
                 for p in range(WINDOW_CHUNKS - 1, -1, -1)]
        return jnp.concatenate(parts, axis=2)

    kb, vb = band(k), band(v)
    scores = jnp.einsum('bnqgrd,bnkgd->bngrqk', q, kb).astype(jnp.float32) / math.sqrt(HEAD_DIM)
    qi = jnp.arange(CHUNK)[:, None]
    kj = jnp.arange(KEYS_PER_BLOCK)[None, :]
    dist = jnp.abs(qi + (WINDOW_CHUNKS - 1) * CHUNK - kj).astype(jnp.float32)
    slopes = alibi_slopes(N_Q_HEADS).reshape(N_KV_HEADS, Q_PER_KV)
    scores = scores - slopes[:, :, None, None] * dist
    key_chunk_back = WINDOW_CHUNKS - 1 - jnp.arange(KEYS_PER_BLOCK) // CHUNK
    valid = jnp.arange(nC)[:, None] >= key_chunk_back[None, :]
    scores = jnp.where(valid[None, :, None, None, None, :], scores, -jnp.inf)
    sink = sinks.astype(jnp.float32).reshape(N_KV_HEADS, Q_PER_KV)[None, None, :, :, None, None]
    m = jnp.maximum(jnp.max(scores, axis=-1, keepdims=True), sink)
    p = jnp.exp(scores - m)
    probs = p / (jnp.sum(p, axis=-1, keepdims=True) + jnp.exp(sink - m))
    out = jnp.einsum('bngrqk,bnkgd->bnqgrd', probs.astype(vb.dtype), vb)
    return out.reshape(B, S, ATTN_WIDTH)

def causal_depthwise_conv(x, w, b):
    S = x.shape[1]
    xp = jnp.pad(x, ((0, 0), (CONV_WIDTH - 1, 0), (0, 0)))
    y = b
    for j in range(CONV_WIDTH):
        y = y + w[j] * xp[:, j:j + S]
    return y

def rg_lru(x, w_a, b_a, w_x, b_x, lam):
    B, S, _ = x.shape
    xb = x.reshape(B, S, LRU_BLOCKS, LRU_BLOCK_DIM)
    r = jax.nn.sigmoid(jnp.einsum('bshi,hij->bshj', xb, w_a) + b_a).reshape(B, S, LRU_WIDTH)
    i = jax.nn.sigmoid(jnp.einsum('bshi,hij->bshj', xb, w_x) + b_x).reshape(B, S, LRU_WIDTH)
    log_a = -LRU_C * r.astype(jnp.float32) * jax.nn.softplus(-lam.astype(jnp.float32))
    a = jnp.exp(log_a)
    u = jnp.sqrt(-jnp.expm1(2.0 * log_a)) * (i * x).astype(jnp.float32)

    def combine(lhs, rhs):
        a1, b1 = lhs
        a2, b2 = rhs
        return a1 * a2, a2 * b1 + b2

    _, h = lax.associative_scan(combine, (a, u), axis=1)
    return h.astype(x.dtype)

def token_mixer(u, w_in, b_in, w_conv, b_conv, w_rg_a, b_rg_a, w_rg_x, b_rg_x, lru_lambda,
                attn_sinks, w_br_attn, w_br_lru, w_mix_out):
    proj = u @ w_in + b_in
    q, k, v, x_lru, g_lru_branch, gate_attn, gate_lru = jnp.split(proj, SPLIT_POINTS, axis=-1)
    y_attn = sliding_window_attention(q, k, v, attn_sinks) @ w_br_attn
    h = rg_lru(causal_depthwise_conv(x_lru, w_conv, b_conv), w_rg_a, b_rg_a, w_rg_x, b_rg_x, lru_lambda)
    y_lru = (h * jax.nn.gelu(g_lru_branch)) @ w_br_lru
    merged = jax.nn.sigmoid(gate_attn) * y_attn + jax.nn.sigmoid(gate_lru) * y_lru
    return merged @ w_mix_out

def moe_ffn(hid, w_router, b_router, w_up, b_up, w_down, b_down):
    B, S, D = hid.shape
    N = B * S
    NA = N * TOP_K
    t = hid.reshape(N, D)
    logits = (t @ w_router + b_router).astype(jnp.float32)
    top_logit, top_e = lax.top_k(logits, TOP_K)
    gate = jax.nn.softmax(top_logit, axis=-1)
    e_flat = top_e.reshape(NA)
    order = jnp.argsort(e_flat).astype(jnp.int32)
    sorted_e = e_flat[order]
    counts = jnp.bincount(e_flat, length=N_EXPERTS)
    padded = (counts + EXPERT_BLOCK - 1) // EXPERT_BLOCK * EXPERT_BLOCK
    start = jnp.cumsum(counts) - counts
    pad_end = jnp.cumsum(padded)
    pad_start = pad_end - padded
    dest = pad_start[sorted_e] + (jnp.arange(NA) - start[sorted_e])
    n_blocks = -(-NA // EXPERT_BLOCK) + N_EXPERTS
    P = n_blocks * EXPERT_BLOCK
    row_assign = jnp.full((P,), NA, jnp.int32).at[dest].set(order)
    row_token = row_assign // TOP_K
    block_e = jnp.minimum(jnp.searchsorted(pad_end, jnp.arange(n_blocks) * EXPERT_BLOCK, side='right'),
                          N_EXPERTS - 1).astype(jnp.int32)
    t_pad = jnp.concatenate([t, jnp.zeros((1, D), t.dtype)], axis=0)

    def expert_block(args):
        blk, e = args
        tok = lax.dynamic_slice(row_token, (blk * EXPERT_BLOCK,), (EXPERT_BLOCK,))
        hu = t_pad[tok] @ w_up[e] + b_up[e]
        x_glu = jnp.minimum(hu[:, 0::2], SWIGLU_LIMIT)
        x_lin = jnp.clip(hu[:, 1::2], -SWIGLU_LIMIT, SWIGLU_LIMIT)
        act = x_glu * jax.nn.sigmoid(SWIGLU_ALPHA * x_glu) * (x_lin + 1.0)
        return act @ w_down[e] + b_down[e]

    rows = lax.map(expert_block, (jnp.arange(n_blocks, dtype=jnp.int32), block_e)).reshape(P, D)
    gate_ext = jnp.concatenate([gate.reshape(NA), jnp.zeros((1,), jnp.float32)])
    w_rows = gate_ext[row_assign].astype(rows.dtype)
    y = jax.ops.segment_sum(rows * w_rows[:, None], row_token, num_segments=N + 1)[:N]
    return y.reshape(B, S, D)

def setup_inputs(seed: int = 0) -> dict:
    key = jax.random.key(seed)
    ks = iter(jax.random.split(key, 32))
    L, D = DEPTH, D_MODEL

    def nrm(shape, scale):
        return scale * jax.random.normal(next(ks), shape, jnp.float32)

    x = nrm((BATCH, SEQ, D), 1.0)
    c = nrm((BATCH, D), 1.0)
    w_ada = nrm((L, D, N_MOD * D), D ** -0.5)
    b_ada = nrm((L, N_MOD * D), 0.02)
    g_pre_mix = 1.0 + nrm((L, D), 0.05)
    g_post_mix = 1.0 + nrm((L, D), 0.05)
    w_in = nrm((L, D, PROJ_WIDTH), D ** -0.5)
    b_in = nrm((L, PROJ_WIDTH), 0.02)
    w_conv = nrm((L, CONV_WIDTH, LRU_WIDTH), CONV_WIDTH ** -0.5)
    b_conv = nrm((L, LRU_WIDTH), 0.02)
    w_rg_a = nrm((L, LRU_BLOCKS, LRU_BLOCK_DIM, LRU_BLOCK_DIM), LRU_BLOCK_DIM ** -0.5)
    b_rg_a = nrm((L, LRU_BLOCKS, LRU_BLOCK_DIM), 0.02)
    w_rg_x = nrm((L, LRU_BLOCKS, LRU_BLOCK_DIM, LRU_BLOCK_DIM), LRU_BLOCK_DIM ** -0.5)
    b_rg_x = nrm((L, LRU_BLOCKS, LRU_BLOCK_DIM), 0.02)
    a0 = jax.random.uniform(next(ks), (L, LRU_WIDTH), jnp.float32, 0.9, 0.999)
    lru_lambda = jnp.log(a0) - jnp.log1p(-a0)
    attn_sinks = nrm((L, N_Q_HEADS), 0.5)
    w_br_attn = nrm((L, ATTN_WIDTH, D), ATTN_WIDTH ** -0.5)
    w_br_lru = nrm((L, LRU_WIDTH, D), LRU_WIDTH ** -0.5)
    w_mix_out = nrm((L, D, D), D ** -0.5)
    g_pre_moe = 1.0 + nrm((L, D), 0.05)
    g_post_moe = 1.0 + nrm((L, D), 0.05)
    w_router = nrm((L, D, N_EXPERTS), D ** -0.5)
    b_router = nrm((L, N_EXPERTS), 0.01)
    w_up = nrm((L, N_EXPERTS, D, 2 * D_FF), D ** -0.5)
    b_up = nrm((L, N_EXPERTS, 2 * D_FF), 0.02)
    w_down = nrm((L, N_EXPERTS, D_FF, D), D_FF ** -0.5)
    b_down = nrm((L, N_EXPERTS, D), 0.02)
    return {"x": x, "c": c, "w_ada": w_ada, "b_ada": b_ada,
            "g_pre_mix": g_pre_mix, "g_post_mix": g_post_mix, "w_in": w_in, "b_in": b_in,
            "w_conv": w_conv, "b_conv": b_conv, "w_rg_a": w_rg_a, "b_rg_a": b_rg_a,
            "w_rg_x": w_rg_x, "b_rg_x": b_rg_x, "lru_lambda": lru_lambda, "attn_sinks": attn_sinks,
            "w_br_attn": w_br_attn, "w_br_lru": w_br_lru, "w_mix_out": w_mix_out,
            "g_pre_moe": g_pre_moe, "g_post_moe": g_post_moe, "w_router": w_router, "b_router": b_router,
            "w_up": w_up, "b_up": b_up, "w_down": w_down, "b_down": b_down}

def reference(x, c, w_ada, b_ada, g_pre_mix, g_post_mix, w_in, b_in, w_conv, b_conv,
              w_rg_a, b_rg_a, w_rg_x, b_rg_x, lru_lambda, attn_sinks, w_br_attn, w_br_lru, w_mix_out,
              g_pre_moe, g_post_moe, w_router, b_router, w_up, b_up, w_down, b_down):
    c_act = jax.nn.silu(c)
    for l in range(DEPTH):
        mod = c_act @ w_ada[l] + b_ada[l]
        shift1, scale1, gate1, shift2, scale2, gate2 = jnp.split(mod[:, None, :], N_MOD, axis=-1)
        u = rms_norm(x, g_pre_mix[l]) * (1.0 + scale1) + shift1
        y = token_mixer(u, w_in[l], b_in[l], w_conv[l], b_conv[l], w_rg_a[l], b_rg_a[l],
                        w_rg_x[l], b_rg_x[l], lru_lambda[l], attn_sinks[l],
                        w_br_attn[l], w_br_lru[l], w_mix_out[l])
        x = x + gate1 * rms_norm(y, g_post_mix[l])
        u = rms_norm(x, g_pre_moe[l]) * (1.0 + scale2) + shift2
        y = moe_ffn(u, w_router[l], b_router[l], w_up[l], b_up[l], w_down[l], b_down[l])
        x = x + gate2 * rms_norm(y, g_post_moe[l])
    return x


_drawn_inputs = setup_inputs


def setup_inputs(seed=0):
    import zlib

    import numpy as np

    out = dict(_drawn_inputs(seed))
    spreads = {}
    factors = {'b_rg_a': 10.785,
     'b_rg_x': 4.599,
     'b_up': 6.095,
     'b_down': 8.0,
     'attn_sinks': 3.193,
     'b_router': 2.833}
    for name, (base, spread) in spreads.items():
        noise = np.random.default_rng([zlib.crc32(name.encode()), seed]).standard_normal(out[name].shape)
        drawn = base * np.exp(spread * noise) if base else spread * noise
        out[name] = __import__('jax').numpy.asarray(drawn.astype(out[name].dtype))
    for name, factor in factors.items():
        out[name] = (out[name] * factor).astype(out[name].dtype)
    return out
```

```python
from contextlib import ExitStack

import concourse.bass as bass
from concourse import mybir

F32 = mybir.dt.float32
I32 = mybir.dt.int32
ALU = mybir.AluOpType
ACT = mybir.ActivationFunctionType
AX = mybir.AxisListType.X

P = 128
D = 1024
KT = D // P
S = 256
TH = S // P
HEADS, HD, CHUNK = 16, 64, 64
KEYS = 3 * CHUNK
E = 32
TOPK = 4
CAP = 64
ITEMS = 48
EPS = 1e-6
ALPHA, LIMIT = 1.702, 7.0
MASKED = 1e30
BIG = 8192.0
NEG_SLOPE8 = [-8.0 * 2.0 ** (-8.0 * (h + 1) / HEADS) for h in range(HEADS)]

T_K, T_V, T_X, T_G, T_GA, T_GL, T_END = 8, 9, 10, 18, 26, 34, 42
C_BIN, C_BCONV, C_WCONV, C_BA, C_BX, C_LAM, C_END = 0, 42, 50, 82, 90, 98, 106
L_ADA0, L_IN, L_ADA12, L_ATTN, L_LRU, L_MIX, L_END = 0, 4, 15, 23, 25, 27, 29
BAYS = 4
T_S, T_PT, T_PV, T_RI = 18, 20, 21, 20
LRU_SMALL = -0.85


def hybrid_block(nc, x, c, w_ada, b_ada, g_pre_mix, g_post_mix, w_in, b_in, w_conv, b_conv, w_rg_a, b_rg_a,
                 w_rg_x, b_rg_x, lru_lambda, attn_sinks, w_br_attn, w_br_lru, w_mix_out, g_pre_moe, g_post_moe,
                 w_router, b_router, w_up, b_up, w_down, b_down, out, mod_dram):
    with ExitStack() as ctx:
        def sb(name, shape, dt=F32):
            return ctx.enter_context(nc.sbuf_tensor(name, shape, dt))

        def sem(name):
            return ctx.enter_context(nc.semaphore(name))

        ring = sb("ring", [P, 12, 2048])
        bay = [ring[:, 2 * b:2 * b + 2, :].rearrange("p s n -> p (s n)") for b in range(BAYS)]
        xcT, rT, iT, eT = [ring[:, 8 + j, :].rearrange("p (k t) -> p k t", k=KT) for j in range(4)]

        x_tok = sb("x_tok", [P, TH, D])
        page_u = sb("page_u", [P, 2048])
        page_q = sb("page_q", [P, 2048])
        page_x = sb("page_x", [P, KT, 3 + S])
        page_g = sb("page_g", [P, 2048])
        page_ga = sb("page_ga", [P, 2048])
        page_gl = sb("page_gl", [P, 2048])
        page_a = sb("page_a", [P, 2048])
        page_n = sb("page_n", [P, 2048])
        tiles = lambda page: page[:, :].rearrange("p (k t) -> p k t", k=KT)
        halves = lambda page: page[:, :].rearrange("p (h d) -> p h d", h=TH)
        uT, qT, geluT, gaT, glT, attnT = map(tiles, (page_u, page_q, page_g, page_ga, page_gl, page_a))
        zT = tiles(page_n)
        xn = halves(page_n)
        hT = page_x[:, :, 3:3 + S]
        y_tok, u2 = halves(page_q), halves(page_g)
        u2T = tiles(page_u)
        y_acc = y_tok
        scale2_b, shift2_b = page_a[:, 0:D], page_a[:, D:2 * D]
        gate1_b, gate2_b = page_ga[:, 0:D], page_ga[:, D:2 * D]
        b_up_sb = page_gl[:, :]

        ident = sb("ident", [P, P])
        before = sb("before", [P, P])
        ones = sb("ones", [P, P])
        bd_a = sb("bd_a", [P, KT, P])
        bd_x = sb("bd_x", [P, KT, P])
        vec_rows = page_a[0:C_END, 512:512 + P]
        cols = sb("cols", [P, C_END])
        c_col = sb("c_col", [P, KT])
        c_sig = sb("c_sig", [P, KT])
        c_act = sb("c_act", [P, KT])
        c_rep = sb("c_rep", [P, KT, 32])
        mod_add = sb("mod_add", [P, 3, 512])
        mod_mul = sb("mod_mul", [P, 3, 512])
        mod_one = sb("mod_one", [P, 3])
        ab_rows = page_a[0:16, 768:768 + P]
        ab = sb("ab", [P, 16])
        stat = sb("stat", [P, 16])
        kz = sb("kz", [P, 4, CHUNK + S])
        v_tok = sb("v_tok", [P, TH, P])
        v_prev = sb("v_prev", [CHUNK, P])
        bv_b = sb("bv_b", [P, P])
        sinks_b = sb("sinks_b", [P, HEADS])
        sink8 = sb("sink8", [P, HEADS])
        dist_i = page_a[:, 0:TH * KEYS].bitcast(I32).rearrange("p (h k) -> p h k", h=TH)
        dist = sb("dist", [P, TH, KEYS])
        sc = sb("sc", [P, 2, TH, KEYS])
        soft = sb("soft", [P, 2, 8, TH])
        pT = sb("pT", [P, 2, 3, P])
        neg8sp = sb("neg8sp", [P, KT])
        sp_t = sb("sp_t", [P, 6, KT])
        def carve(flat):
            at = [0]

            def take(*shape, rows=P, dt=F32):
                n = 1
                for w in shape:
                    n *= w
                part = flat[0:rows, at[0]:at[0] + n]
                at[0] += n
                assert at[0] <= flat.shape[1]
                if dt != F32:
                    part = part.bitcast(dt)
                return part.rearrange("p (a b) -> p a b", a=shape[0]) if len(shape) == 2 else part
            return take

        of_x = carve(page_x[:, :, :].rearrange("p k t -> p (k t)"))
        of_kz = carve(kz[:, :, :].rearrange("p k t -> p (k t)"))
        of_sc = carve(sc[:, :, :, :].rearrange("p a b c -> p (a b c)"))
        w_router_sb = of_x(KT, E)
        b_down_sb = of_x(D, rows=E)
        lg, gt, eq, eq_n, mask, gate, posm = (of_x(TH, E) for _ in range(7))
        top8 = of_x(TH, 8)
        allow = of_x(TH, 4)
        b_router_b = sb("b_router_b", [P, E])
        gateT = of_kz(S, rows=E)
        posT = of_kz(S, rows=E)
        iota_i = of_kz(TH, P, dt=I32)
        iota_s = of_kz(TH, P)
        iota_n = of_kz(ITEMS, rows=E)
        item_t = of_kz(2, ITEMS, rows=E)
        w_target = sb("w_target", [E, 2])
        blocks = sb("blocks", [E, 8])
        item_sel = sb("item_sel", [P, ITEMS])
        item_off = of_kz(ITEMS, rows=E)
        pos_item = sb("pos_item", [P, TH, ITEMS])
        gate_item = sb("gate_item", [P, TH, ITEMS])
        tab = sb("tab", [1, 96], I32)
        oh = of_sc(TH, CAP)
        ohg = of_sc(TH, P)
        ohg_h = of_sc(TH, P)
        bsel = of_sc(CAP)
        xgT = bd_a[:, 0:4, :].rearrange("p a b -> p (a b)").rearrange("p (k s) -> p k s", k=KT)
        actT = bd_a[:, 4:8, :].rearrange("p a b -> p (a b)")
        glu = bd_x[:, 0:4, :].rearrange("p a b -> p (a b)")
        lin = bd_x[:, 4:8, :].rearrange("p a b -> p (a b)")
        sig = mod_add[:, 0, :]
        act_sb = mod_add[:, 1, :]
        rows = mod_add[:, 2, :]
        ohgT = mod_mul[:, 0, 0:S]
        scrap = halves(page_n)

        bank = [ctx.enter_context(nc.psum_tensor(f"bank{i}", [P, 512], F32)) for i in range(8)]
        proj = [bank[j][:, 0:256] for j in range(2)]

        small_in = sem("small_in")
        late_in = sem("late_in")
        x_in = sem("x_in")
        bay_in = [sem(f"bay_in{b}") for b in range(BAYS)]
        load_used = sem("load_used")
        consts = sem("consts")
        g_chain = sem("g_chain")
        v_chain = sem("v_chain")
        a_chain = sem("a_chain")
        route_in = sem("route_in")
        numbers = sem("numbers")
        c_ready = sem("c_ready")
        csig_ready = sem("csig_ready")
        xn_ready = sem("xn_ready")
        sq_ready = sem("sq_ready")
        mean_ready = sem("mean_ready")
        root_ready = sem("root_ready")
        xT_done = sem("xT_done")
        cols_ps = sem("cols_ps")
        cols_ready = sem("cols_ready")
        mod_done = sem("mod_done")
        mod_vec = sem("mod_vec")
        mod_out = sem("mod_out")
        ab_in = sem("ab_in")
        ab_ps = sem("ab_ps")
        ab_ready = sem("ab_ready")
        uT_ready = sem("uT_ready")
        proj_done = sem("proj_done")
        proj_evac = sem("proj_evac")
        v_evac = sem("v_evac")
        kz_ready = sem("kz_ready")
        s_done = sem("s_done")
        negm_ready = sem("negm_ready")
        exp_done = sem("exp_done")
        p_ready = sem("p_ready")
        pt_done = sem("pt_done")
        pt_ready = sem("pt_ready")
        pv_done = sem("pv_done")
        attn_ready = sem("attn_ready")
        xc_ready = sem("xc_ready")
        ri_done = sem("ri_done")
        ri_ready = sem("ri_ready")
        lam_exp = sem("lam_exp")
        lam_in = sem("lam_in")
        log_a = sem("log_a")
        a_tab = sem("a_tab")
        lru_w = sem("lru_w")
        lru_root = sem("lru_root")
        hg_ready = sem("hg_ready")
        br_done = sem("br_done")
        br_evac = sem("br_evac")
        merged = sem("merged")
        mix_done = sem("mix_done")
        mix_evac = sem("mix_evac")
        rows_b_in = sem("rows_b_in")
        sq1_ready = sem("sq1_ready")
        sq2_ready = sem("sq2_ready")
        x1_ready = sem("x1_ready")
        sq3_ready = sem("sq3_ready")
        yacc_done = sem("yacc_done")
        u2_ready = sem("u2_ready")
        u2T_done = sem("u2T_done")
        u2T_ready = sem("u2T_ready")
        lg_done = sem("lg_done")
        top_ready = sem("top_ready")
        gexp_ready = sem("gexp_ready")
        mask_ready = sem("mask_ready")
        pos_done = sem("pos_done")
        posm_ready = sem("posm_ready")
        posT_done = sem("posT_done")
        posT_ready = sem("posT_ready")
        blocks_ready = sem("blocks_ready")
        cum_done = sem("cum_done")
        sel_ready = sem("sel_ready")
        item_done = sem("item_done")
        tab_ready = sem("tab_ready")
        b_up_in = sem("b_up_in")
        yinit_done = sem("yinit_done")
        yinit_ready = sem("yinit_ready")
        w_slot = [sem(f"w_slot{k}") for k in range(12)]
        slot_used = [sem(f"slot_used{k}") for k in range(12)]
        oh_ready = sem("oh_ready")
        ohg_half = sem("ohg_half")
        ohg_ready = sem("ohg_ready")
        bsel_ready = sem("bsel_ready")
        gather_done = sem("gather_done")
        xg_ready = sem("xg_ready")
        ohgT_done = sem("ohgT_done")
        ohgT_ready = sem("ohgT_ready")
        glu_ready = sem("glu_ready")
        lin_ready = sem("lin_ready")
        gl_ready = sem("gl_ready")
        sig_ready = sem("sig_ready")
        act_ready = sem("act_ready")
        actT_done = sem("actT_done")
        actT_ready = sem("actT_ready")
        rows_ready = sem("rows_ready")
        comb_done = sem("comb_done")
        y_added = sem("y_added")
        out_done = sem("out_done")

        x_v = x.rearrange("b (h p) d -> (b p) h d", p=P)
        out_v = out.rearrange("b (h p) d -> (b p) h d", p=P)
        ada_v = w_ada.rearrange("l (p k) (m n) -> (l m) p k n", k=KT, m=3)
        in_v = w_in.rearrange("l (k p) n -> (l p) k n", p=P)
        square_v = {n: w.rearrange("l (k p) (c n) -> (l c) p k n", p=P, c=2)
                    for n, w in (("attn", w_br_attn), ("lru", w_br_lru), ("mix", w_mix_out))}
        up_v = w_up.rearrange("l e (k p) f -> (l e) p k f", p=P)
        down_v = w_down.rearrange("l e (q a p) f -> (l e) p q a f", p=P, a=2)
        mod_v = mod_dram.rearrange("(m j) n -> j m n", j=4)
        row = lambda v: v.rearrange("l (k p) -> (l k) p", p=P)

        def loads():
            res = []
            for m in range(3):
                for b in range(4):
                    res.append((bay[len(res) % BAYS].rearrange("p (k n) -> p k n", k=2),
                                ada_v[m, :, 2 * b:2 * b + 2, :]))
                if m == 0:
                    for g in range(11):
                        w = min(512, T_END * P - 512 * g)
                        dst = bay[len(res) % BAYS].rearrange("p (k n) -> p k n", k=KT)[:, :, 0:w]
                        res.append((dst, in_v[:, :, 512 * g:512 * g + w]))
            for n in ("attn", "lru", "mix"):
                for half in range(2):
                    res.append((bay[len(res) % BAYS].rearrange("p (k n) -> p k n", k=KT), square_v[n][half]))
            return res

        plan = loads()
        assert len(plan) == L_END
        block = ctx.enter_context(nc.Block())

        @block.sync
        def _(sp):
            for n, (dst, src) in enumerate(plan):
                if n >= BAYS:
                    sp.wait_ge(load_used, n - BAYS + 1)
                sp.dma_start(dst, src).then_inc(bay_in[n % BAYS], 16)
            for n in (1, 2, 3, 0):
                b = n
                last = max(q for q in range(L_END) if q % BAYS == b)
                sp.wait_ge(load_used, last + 1)
                for k in (2 * b, 2 * b + 1):
                    sp.dma_start(ring[:, k, :], up_v[0, :, k, :]).then_inc(w_slot[k], 16)
            sp.wait_ge(hg_ready, 1)
            for q in range(4):
                sp.dma_start(ring[:, 8 + q, :].rearrange("p (a f) -> p a f", a=2),
                             down_v[0, :, q, :, :]).then_inc(w_slot[8 + q], 16)
            sp.wait_ge(tab_ready, 1)
            with sp.Fori(1, E) as e:
                ahead = sp.value_load(tab[0:1, bass.ds(e, 1)], min_val=1, max_val=ITEMS)
                for k in range(KT):
                    sp.wait_ge(slot_used[k], ahead)
                    sp.dma_start(ring[:, k, :], up_v[bass.ds(e, 1), :, k, :].rearrange("e p f -> (e p) f"))\
                      .then_inc(w_slot[k], 16)
                for q in range(4):
                    sp.wait_ge(slot_used[8 + q], ahead)
                    sp.dma_start(ring[:, 8 + q, :].rearrange("p (a f) -> p a f", a=2),
                                 down_v[bass.ds(e, 1), :, q, :, :].rearrange("e p a f -> (e p) a f"))\
                      .then_inc(w_slot[8 + q], 16)

        @block.gpsimd
        def _(g):
            done = [0]

            def link(ins):
                done[0] += 1
                ins.then_inc(g_chain, 1)
                g.wait_ge(g_chain, done[0])

            link(g.memset(ident[:, :], 0.0))
            g.affine_select(out=ident[:, :], in_=ident[:, :], compare_op=ALU.not_equal, fill=1.0, base=0,
                            pattern=[[-1, P]], channel_multiplier=1).then_inc(consts, 1)
            g.memset(ones[:, :], 1.0).then_inc(consts, 1)
            link(g.memset(mod_add[:, :, :], 0.0))
            link(g.memset(mod_mul[:, :, :], 1.0))
            g.dma_start(mod_add[0:P:32, :, :], b_ada.rearrange("l (m j n) -> (l j) m n", m=3, j=4)).then_inc(late_in, 16)
            for j, m, gain in ((2, 0, g_pre_mix), (0, 1, g_post_mix), (0, 2, g_pre_moe), (2, 2, g_post_moe)):
                g.dma_start(mod_mul[32 * j:32 * j + 33:32, m, :], gain.rearrange("l (a n) -> (l a) n", a=2))\
                 .then_inc(late_in, 16)
            link(g.memset(mod_one[:, :], 0.0))
            link(g.memset(mod_one[64:128, 0:1], 1.0))
            g.memset(mod_one[0:64, 2:3], 1.0).then_inc(consts, 1)
            for bd, w in ((bd_a, w_rg_a), (bd_x, w_rg_x)):
                link(g.memset(bd[:, :, :], 0.0))
                pair = w.rearrange("l (k two) i j -> two (l i) k j", two=2)
                for f in range(2):
                    g.dma_start(bd[64 * f:64 * f + 64, :, 64 * f:64 * f + 64], pair[f]).then_inc(late_in, 16)
            g.memset(kz[:, :, :], 0.0).then_inc(consts, 1)
            g.memset(page_x[:, :, 0:3], 0.0).then_inc(consts, 1)
            link(g.memset(before[:, :], 1.0))
            g.affine_select(out=before[:, :], in_=before[:, :], compare_op=ALU.is_gt, fill=0.0, base=0,
                            pattern=[[1, P]], channel_multiplier=-1).then_inc(consts, 1)
            link(g.iota(dist_i[:, :, :], pattern=[[0, TH], [-1, KEYS]], base=CHUNK, channel_multiplier=1))
            g.tensor_copy(dist[:, :, :], dist_i[:, :, :]).then_inc(consts, 1)
            g.memset(item_sel[:, :], 0.0).then_inc(consts, 1)

            g.wait_ge(attn_ready, HEADS // 2)
            link(g.iota(iota_i[:, :, :], pattern=[[0, TH], [0, 2], [1, CAP]], base=0, channel_multiplier=0))
            link(g.tensor_copy(iota_s[:, :, :], iota_i[:, :, :]))
            link(g.iota(iota_i[0:E, 0, 0:ITEMS], pattern=[[1, ITEMS]], base=0, channel_multiplier=0))
            link(g.tensor_copy(iota_n[:, :], iota_i[0:E, 0, 0:ITEMS]))
            link(g.iota(iota_i[0:E, 1, 0:2], pattern=[[0, 2]], base=16, channel_multiplier=16))
            g.tensor_copy(w_target[:, :], iota_i[0:E, 1, 0:2]).then_inc(numbers, 1)
            def pick_bias(i):
                return g.tensor_copy(bsel, item_sel[:, bass.ds(i, 1)].to_broadcast([P, CAP]))

            g.wait_ge(tab_ready, 1)
            n_items = g.value_load(tab[0:1, E:E + 1], min_val=E, max_val=ITEMS - 1)
            pick_bias(0).then_inc(bsel_ready, 1)
            with g.Fori(0, n_items) as i:
                g.wait_ge(slot_used[7], i + 1)
                pick_bias(i + 1).then_inc(bsel_ready, 1)

        @block.scalar
        def _(a):
            a.dma_start(x_tok[:, :, :], x_v).then_inc(x_in, 16)
            a.dma_start(c_col[:, :], c.rearrange("b (p k) -> (b p) k", k=KT)).then_inc(small_in, 16)
            for r0, src in ((C_BIN, row(b_in)), (C_BCONV, row(b_conv)),
                            (C_WCONV, w_conv.rearrange("l j (k p) -> (l j k) p", p=P)),
                            (C_BA, b_rg_a.rearrange("l (k a) j -> (l k) (a j)", a=2)),
                            (C_BX, b_rg_x.rearrange("l (k a) j -> (l k) (a j)", a=2)), (C_LAM, row(lru_lambda))):
                a.dma_start(vec_rows[r0:r0 + src.shape[0], :], src).then_inc(small_in, 16)
            a.dma_start(bv_b[:, :], b_in[:, T_V * P:T_V * P + P].to_broadcast([P, P])).then_inc(small_in, 16)
            a.dma_start(sinks_b[:, :], attn_sinks.to_broadcast([P, HEADS])).then_inc(small_in, 16)
            a.dma_start(b_router_b[:, :], b_router.to_broadcast([P, E])).then_inc(small_in, 16)
            n_small = 16 * 10

            def root(s, o):
                a.wait_ge(mean_ready, s // 4 + 1)
                a.activation(stat[:, o:o + 2], stat[:, o:o + 2], ACT.Sqrt).then_inc(root_ready, 1)

            a.wait_ge(small_in, n_small)
            a.activation(c_sig[:, :], c_col[:, :], ACT.Sigmoid).then_inc(csig_ready, 1)
            a.wait_ge(x_in, 16)
            for h in range(TH):
                a.activation(page_g[:, D * h:D * h + D], x_tok[:, h, :], ACT.Square,
                             accum_out=stat[:, h:h + 1]).then_inc(sq_ready, 1)
            root(0, 2)
            a.wait_ge(cols_ready, 1)
            a.wait_ge(lam_in, 1)
            a.activation(sp_t[:, 0, :], sp_t[:, 1, :], ACT.Exp).then_inc(lam_exp, 1)
            a.wait_ge(mod_vec, 1)
            a.dma_start(mod_v[:, 0, :], mod_add[0:P:32, 0, :]).then_inc(mod_out, 16)
            a.wait_ge(mod_out, 16)
            a.dma_start(ab_rows[:, :], mod_dram[0:4, :].rearrange("m (r p) -> (m r) p", p=P)).then_inc(ab_in, 16)
            a.wait_ge(xT_done, 1)
            a.wait_ge(ab_ready, 1)
            for k in range(KT):
                a.activation(uT[:, k, :], bank[4 + k // 2][:, 256 * (k % 2):256 * (k % 2) + 256], ACT.Identity,
                             bias=ab[:, k:k + 1], scale=ab[:, 8 + k:9 + k]).then_inc(uT_ready, 1)

            def evac(t):
                a.wait_ge(proj_done, t + 1)
                src, bias = proj[t % 2], cols[:, C_BIN + t:C_BIN + t + 1]
                if t < T_K:
                    ins = a.activation(qT[:, t, :], src, ACT.Identity, bias=bias)
                elif t == T_K:
                    a.wait_ge(consts, 8)
                    for f in range(2):
                        half = slice(64 * f, 64 * f + 64)
                        ins = a.activation(kz[half, 3 * f, CHUNK:CHUNK + S], src[half, :], ACT.Identity,
                                           bias=cols[half, C_BIN + t:C_BIN + t + 1])
                        if f == 0:
                            ins.then_inc(kz_ready, 1)
                elif t < T_G:
                    ins = a.activation(page_x[:, t - T_X, 3:3 + S], src, ACT.Identity, bias=bias)
                elif t < T_GA:
                    ins = a.activation(geluT[:, t - T_G, :], src, ACT.Gelu_apprx_tanh, bias=bias)
                elif t < T_GL:
                    ins = a.activation(gaT[:, t - T_GA, :], src, ACT.Sigmoid, bias=bias)
                else:
                    ins = a.activation(glT[:, t - T_GL, :], src, ACT.Sigmoid, bias=bias)
                ins.then_inc(proj_evac, 1)

            for t in range(T_END):
                if t != T_V:
                    evac(t)
                h = t - T_S
                if 0 <= h < HEADS:
                    a.wait_ge(negm_ready, h + 1)
                    for m in range(TH):
                        a.activation(sc[:, h % 2, m, :], sc[:, h % 2, m, :], ACT.Exp, scale=0.125,
                                     bias=soft[:, h % 2, 1, m:m + 1], accum_out=soft[:, h % 2, 2, m:m + 1])\
                         .then_inc(exp_done, 1)
                    a.activation(soft[:, h % 2, 3, :], soft[:, h % 2, 6, :], ACT.Exp).then_inc(exp_done, 1)
                h = t - T_PT
                if 0 <= h < HEADS:
                    a.wait_ge(pt_done, h + 1)
                    a.activation(pT[:, h % 2, 0:2, :].rearrange("p a b -> p (a b)"), bank[3][:, 0:256],
                                 ACT.Copy).then_inc(pt_ready, 1)
                    a.activation(pT[0:CHUNK, h % 2, 2, :], bank[3][0:CHUNK, 256:384], ACT.Copy).then_inc(pt_ready, 1)
                h = t - T_PV
                if 0 <= h < HEADS and h % 2:
                    a.wait_ge(pv_done, h + 1)
                    a.activation(attnT[:, h // 2, :], bank[4][:, 0:256], ACT.Copy).then_inc(attn_ready, 1)
                k = t - T_RI
                if 0 <= k < KT:
                    a.wait_ge(ri_done, k + 1)
                    a.activation(rT[:, k, :], bank[5 + k % 2][:, 0:256], ACT.Sigmoid,
                                 bias=cols[:, C_BA + k:C_BA + k + 1]).then_inc(ri_ready, 1)
                    a.activation(iT[:, k, :], bank[5 + k % 2][:, 256:512], ACT.Sigmoid,
                                 bias=cols[:, C_BX + k:C_BX + k + 1]).then_inc(ri_ready, 1)
            for half in range(2):
                ks = slice(4 * half, 4 * half + 4)
                a.wait_ge(log_a, half + 1)
                a.activation(zT[:, ks, :], rT[:, ks, :], ACT.Exp).then_inc(a_tab, 1)
                a.wait_ge(lru_w, half + 1)
                a.activation(zT[:, ks, :], zT[:, ks, :], ACT.Sqrt, scale=-1.0).then_inc(lru_root, 1)
            a.wait_ge(mod_vec, 3)
            a.dma_start(mod_v[:, 1:3, :], mod_add[0:P:32, 1:3, :]).then_inc(mod_out, 16)
            a.wait_ge(mod_out, 32)
            a.wait_ge(merged, KT)
            a.wait_ge(br_evac, 2 * KT)
            a.wait_ge(br_done, 2 * KT)
            for dst, r in ((gate1_b, 4), (shift2_b, 6), (scale2_b, 8), (gate2_b, 10)):
                a.dma_start(dst, mod_dram[r:r + 2, :].rearrange("(o r) n -> o (r n)", o=1).to_broadcast([P, D]))\
                 .then_inc(rows_b_in, 16)

            a.wait_ge(hg_ready, 1)
            a.dma_start(w_router_sb, w_router.rearrange("l (k p) e -> (l p) k e", p=P)).then_inc(route_in, 16)
            a.dma_start(b_down_sb, b_down.rearrange("l e d -> (l e) d")).then_inc(route_in, 16)

            for h in range(TH):
                a.wait_ge(mix_done, 2 * h + 2)
                for cc in range(2):
                    a.activation(y_tok[:, h, 512 * cc:512 * cc + 512], bank[2 * h + cc][:, :], ACT.Copy)\
                     .then_inc(mix_evac, 1)
                a.wait_ge(mix_evac, 2 * h + 2)
                a.activation(scrap[:, h, :], y_tok[:, h, :], ACT.Square,
                             accum_out=stat[:, 4 + h:5 + h]).then_inc(sq1_ready, 1)
            root(4, 6)
            for h in range(TH):
                a.wait_ge(x1_ready, h + 1)
                a.wait_ge(sq1_ready, TH)
                a.activation(y_tok[:, h, :], x_tok[:, h, :], ACT.Square,
                             accum_out=stat[:, 8 + h:9 + h]).then_inc(sq2_ready, 1)
            root(8, 10)
            a.wait_ge(mix_evac, 4)
            a.wait_ge(br_evac, 2 * KT)
            a.wait_ge(mix_done, 4)
            a.dma_start(b_up_sb[0:E, :], b_up.rearrange("l e f -> (l e) f")).then_inc(b_up_in, 16)
            for k in range(KT):
                a.wait_ge(u2T_done, k // 2 + 1)
                a.activation(u2T[:, k, :], bank[4 + k // 2][:, 256 * (k % 2):256 * (k % 2) + 256], ACT.Copy)\
                 .then_inc(u2T_ready, 1)
            a.wait_ge(top_ready, 1)
            for h in range(TH):
                a.activation(gate[:, h, :], lg[:, h, :], ACT.Exp, bias=allow[:, h, 2:3]).then_inc(gexp_ready, 1)

            a.wait_ge(tab_ready, 1)
            n_items = a.value_load(tab[0:1, E:E + 1], min_val=E, max_val=ITEMS - 1)
            with a.Fori(0, n_items) as i:
                a.wait_ge(glu_ready, i + 1)
                a.activation(sig, glu, ACT.Sigmoid, scale=ALPHA).then_inc(sig_ready, 1)
                a.wait_ge(actT_done, i + 1)
                a.activation(actT, bank[3][:, :], ACT.Copy).then_inc(actT_ready, 1)
                a.wait_ge(slot_used[11], i + 1)
                a.activation(rows, bank[4][:, :], ACT.Copy).then_inc(rows_ready, 1)
            for h in range(TH):
                a.wait_ge(yacc_done, h + 1)
                a.activation(scrap[:, h, :], y_acc[:, h, :], ACT.Square,
                             accum_out=stat[:, 12 + h:13 + h]).then_inc(sq3_ready, 1)
            root(12, 14)
            for h in range(TH):
                a.wait_ge(x1_ready, TH + h + 1)
                a.dma_start(out_v[:, h, :], x_tok[:, h, :]).then_inc(out_done, 16)
            a.wait_ge(out_done, 16 * TH)

        @block.tensor
        def _(pe):
            def landed(n):
                pe.wait_ge(bay_in[n % BAYS], 16 * (n // BAYS + 1))

            pe.wait_ge(consts, 1)
            pe.wait_ge(small_in, 16 * 10)
            pe.transpose(bank[2][:, 0:C_END], vec_rows[:, :], ident[0:C_END, 0:C_END]).then_inc(cols_ps, 1)
            pe.wait_ge(xn_ready, TH)
            for k in range(KT):
                for h in range(TH):
                    ins = pe.transpose(bank[4 + k // 2][:, 256 * (k % 2) + P * h:256 * (k % 2) + P * h + P],
                                       xn[:, h, P * k:P * k + P], ident[:, :])
            ins.then_inc(xT_done, 1)

            def modulation(m, first):
                for b in range(4):
                    landed(first + b)
                    w = bay[(first + b) % BAYS].rearrange("p (k n) -> p k n", k=2)
                    for k in (0, 1):
                        for j in range(4):
                            ins = pe.matmul(bank[7][32 * j:32 * j + 32, :], c_rep[:, 2 * b + k, :],
                                            w[:, k, 512 * j:512 * j + 512], start=(b == 0 and k == 0),
                                            stop=(b == 3 and k == 1), tile_position=(0, 32 * j))
                    ins.then_inc(load_used, 1)

            pe.wait_ge(c_ready, 1)
            for b in range(4):
                landed(b)
                w = bay[b].rearrange("p (k n) -> p k n", k=2)
                for k in (0, 1):
                    for j in range(4):
                        ins = pe.matmul(bank[3][32 * j:32 * j + 32, :], c_rep[:, 2 * b + k, :],
                                        w[:, k, 512 * j:512 * j + 512], start=(b == 0 and k == 0),
                                        stop=(b == 3 and k == 1), tile_position=(0, 32 * j))
                ins.then_inc(load_used, 1)
            pe.wait_ge(ab_in, 16)
            pe.wait_ge(cols_ready, 1)
            pe.transpose(bank[2][:, 0:16], ab_rows[:, :], ident[0:16, 0:16]).then_inc(ab_ps, 1)

            def column_tile(t):
                n = L_IN + t // 4
                if t % 4 == 0:
                    landed(n)
                if t == 0:
                    pe.wait_ge(uT_ready, KT)
                if t - 2 == T_V:
                    pe.wait_ge(v_evac, 3)
                elif t >= 2:
                    pe.wait_ge(proj_evac, t - 1 if t - 2 < T_V else t - 2)
                w = bay[n % BAYS].rearrange("p (k n) -> p k n", k=KT)[:, :, P * (t % 4):P * (t % 4) + P]
                if t == T_V:
                    for m in range(TH):
                        for k in range(KT):
                            pe.matmul(proj[t % 2][:, P * m:P * m + P], uT[:, k, P * m:P * m + P], w[:, k, :],
                                      start=(k == 0), stop=(k == KT - 1))
                    for k in range(KT):
                        ins = pe.matmul(bank[2][0:CHUNK, 0:P], uT[:, k, CHUNK:P], w[:, k, :],
                                        start=(k == 0), stop=(k == KT - 1))
                else:
                    for k in range(KT):
                        ins = pe.matmul(proj[t % 2], w[:, k, :], uT[:, k, :], start=(k == 0), stop=(k == KT - 1))
                ins.then_inc(proj_done, 1)

            def scores(h):
                kv, f = h // 8, h % 2
                if h == 0:
                    pe.wait_ge(v_evac, 3)
                    pe.wait_ge(kz_ready, 3)
                    pe.wait_ge(proj_evac, T_K + 1)
                else:
                    pe.wait_ge(negm_ready, h)
                for m in range(TH):
                    ins = pe.matmul(bank[2][:, KEYS * m:KEYS * m + KEYS], qT[:, h // 2, P * m:P * m + P],
                                    kz[:, 2 * kv + f, P * m:P * m + KEYS], start=True, stop=True)
                ins.then_inc(s_done, 1)

            def turn_probs(h):
                pe.wait_ge(p_ready, h + 1)
                if h >= 1:
                    pe.wait_ge(pt_ready, 2 * h)
                for m in range(TH):
                    pe.transpose(bank[3][:, P * m:P * m + P], sc[:, h % 2, m, CHUNK:KEYS], ident[:, :])
                pe.transpose(bank[3][0:CHUNK, 2 * P:3 * P], sc[:, h % 2, 1, 0:CHUNK], ident[:, :])\
                  .then_inc(pt_done, 1)

            def values(h):
                kv, f = h // 8, h % 2
                pe.wait_ge(pt_ready, 2 * h + 2)
                if h >= 2:
                    pe.wait_ge(attn_ready, h // 2)
                o, v = bank[4][64 * f:64 * f + 64, :], slice(64 * kv, 64 * kv + 64)
                pe.matmul(o[:, 0:P], v_tok[:, 0, v], pT[:, h % 2, 0, :], start=True, stop=True)
                pe.matmul(o[:, P:2 * P], v_tok[:, 1, v], pT[:, h % 2, 1, :], start=True, stop=False)
                pe.matmul(o[:, P:2 * P], v_prev[:, v], pT[0:CHUNK, h % 2, 2, :], start=False, stop=True)\
                  .then_inc(pv_done, 1)

            def lru_gates(k):
                pe.wait_ge(xc_ready, k + 1)
                if k == 0:
                    pe.wait_ge(late_in, 16 * 9)
                if k >= 2:
                    pe.wait_ge(ri_ready, 2 * (k - 1))
                ps = bank[5 + k % 2]
                pe.matmul(ps[:, 0:256], bd_a[:, k, :], xcT[:, k, :], start=True, stop=True)
                pe.matmul(ps[:, 256:512], bd_x[:, k, :], xcT[:, k, :], start=True, stop=True).then_inc(ri_done, 1)

            for t in range(T_END):
                column_tile(t)
                if t % 4 == 3 or t == T_END - 1:
                    pe.wait_ge(proj_done, t + 1)
                    pe.nop().then_inc(load_used, 1)
                if 0 <= t - T_S < HEADS:
                    scores(t - T_S)
                if 0 <= t - T_PT < HEADS:
                    turn_probs(t - T_PT)
                if 0 <= t - T_PV < HEADS:
                    values(t - T_PV)
                if 0 <= t - T_RI < KT:
                    lru_gates(t - T_RI)

            modulation(1, L_ADA12)
            pe.wait_ge(load_used, L_ADA12 + 4)
            pe.nop().then_inc(mod_done, 1)
            pe.wait_ge(mod_vec, 2)
            modulation(2, L_ADA12 + 4)
            pe.wait_ge(load_used, L_ADA12 + 8)
            pe.nop().then_inc(mod_done, 1)

            def branch(first, src, base):
                for d in range(KT):
                    n = first + d // 4
                    if d % 4 == 0:
                        landed(n)
                    q = base + d
                    if q >= 2:
                        pe.wait_ge(br_evac, q - 1)
                    elif q == 0:
                        pe.wait_ge(proj_evac, T_END - 1)
                    w = bay[n % BAYS].rearrange("p (k n) -> p k n", k=KT)[:, :, P * (d % 4):P * (d % 4) + P]
                    for k in range(KT):
                        ins = pe.matmul(proj[q % 2], w[:, k, :], src[:, k, :], start=(k == 0), stop=(k == KT - 1))
                    ins.then_inc(br_done, 1)
                    if d % 4 == 3:
                        pe.wait_ge(br_done, q + 1)
                        pe.nop().then_inc(load_used, 1)

            pe.wait_ge(attn_ready, HEADS // 2)
            branch(L_ATTN, attnT, 0)
            pe.wait_ge(hg_ready, 1)
            branch(L_LRU, geluT, KT)
            pe.wait_ge(merged, KT)
            for cc in range(2):
                landed(L_MIX + cc)
            for h in range(TH):
                for cc in range(2):
                    w = bay[(L_MIX + cc) % BAYS].rearrange("p (k n) -> p k n", k=KT)
                    for k in range(KT):
                        ins = pe.matmul(bank[2 * h + cc][:, :], glT[:, k, P * h:P * h + P], w[:, k, :],
                                        start=(k == 0), stop=(k == KT - 1))
                    ins.then_inc(mix_done, 1)
            pe.wait_ge(mix_done, 4)
            pe.nop().then_inc(load_used, 1)
            pe.nop().then_inc(load_used, 1)

            for k in range(KT):
                if k == 0:
                    pe.wait_ge(u2_ready, TH)
                for h in range(TH):
                    ins = pe.transpose(bank[4 + k // 2][:, 256 * (k % 2) + P * h:256 * (k % 2) + P * h + P],
                                       u2[:, h, P * k:P * k + P], ident[:, :])
                if k % 2:
                    ins.then_inc(u2T_done, 1)
            pe.wait_ge(mix_evac, 4)
            pe.wait_ge(route_in, 32)
            for h in range(TH):
                for k in range(KT):
                    if h == 0:
                        pe.wait_ge(u2T_ready, k + 1)
                    ins = pe.matmul(bank[0][:, E * h:E * h + E], u2T[:, k, P * h:P * h + P], w_router_sb[:, k, :],
                                    start=(k == 0), stop=(k == KT - 1))
            ins.then_inc(lg_done, 1)
            pe.wait_ge(mask_ready, 1)
            pe.wait_ge(consts, 8)
            pe.matmul(bank[1][:, 0:E], before[:, :], mask[:, 0, :], start=True, stop=True)
            pe.matmul(bank[1][:, E:2 * E], before[:, :], mask[:, 1, :], start=True, stop=False)
            pe.matmul(bank[1][:, E:2 * E], ones[:, :], mask[:, 0, :], start=False, stop=True)
            pe.matmul(bank[2][0:E, 0:2], mask[:, 0, :], ones[:, 0:2], start=True, stop=False)
            pe.matmul(bank[2][0:E, 0:2], mask[:, 1, :], ones[:, 0:2], start=False, stop=True).then_inc(pos_done, 1)
            pe.wait_ge(posm_ready, 2)
            for h in range(TH):
                pe.transpose(bank[3][0:E, P * h:P * h + P], posm[:, h, :], ident[:, :])
            for h in range(TH):
                ins = pe.transpose(bank[3][0:E, S + P * h:S + P * h + P], gate[:, h, :], ident[:, :])
            ins.then_inc(posT_done, 1)
            pe.wait_ge(blocks_ready, 1)
            pe.matmul(bank[2][0:E, 4:6], before[0:E, 0:E], blocks[:, 0:2], start=True, stop=True)
            pe.matmul(bank[2][0:1, 8:8 + E + 2], blocks[:, 0:1], before[0:E, 0:E + 2], start=True, stop=True)\
              .then_inc(cum_done, 1)
            pe.wait_ge(sel_ready, 1)
            pe.wait_ge(posT_ready, 2)
            for h in range(TH):
                pe.matmul(bank[1][:, 64 + ITEMS * h:64 + ITEMS * h + ITEMS], posT[:, P * h:P * h + P],
                          item_sel[0:E, :], start=True, stop=False)
                pe.matmul(bank[1][:, 64 + ITEMS * h:64 + ITEMS * h + ITEMS], ones[0:E, :], item_off[:, :],
                          start=False, stop=True)
            for h in range(TH):
                pe.matmul(bank[1][:, 160 + ITEMS * h:160 + ITEMS * h + ITEMS], gateT[:, P * h:P * h + P],
                          item_sel[0:E, :], start=True, stop=True)
            pe.matmul(bank[2][0:1, 64:64 + ITEMS], w_target[:, 0:1], item_sel[0:E, :], start=True, stop=True)\
              .then_inc(item_done, 1)
            pe.wait_ge(u2T_ready, KT)
            for h in range(TH):
                for cc in range(2):
                    ins = pe.matmul(bank[4 + 2 * h + cc][:, :], gateT[:, P * h:P * h + P],
                                    b_down_sb[:, 512 * cc:512 * cc + 512], start=True, stop=True)
            ins.then_inc(yinit_done, 1)

            def gather():
                for k in range(KT):
                    for h in range(TH):
                        ins = pe.matmul(bank[2][:, CAP * k:CAP * k + CAP], u2[:, h, P * k:P * k + P], oh[:, h, :],
                                        start=(h == 0), stop=(h == TH - 1))
                ins.then_inc(gather_done, 1)

            def combine(h):
                for cc in range(2):
                    half = slice(64 * cc, 64 * cc + 64)
                    ins = pe.matmul(bank[6 + cc][:, :], ohgT[half, P * h:P * h + P], rows[half, :],
                                    start=True, stop=True)
                ins.then_inc(comb_done, 1)

            pe.wait_ge(tab_ready, 1)
            n_items = pe.value_load(tab[0:1, E:E + 1], min_val=E, max_val=ITEMS - 1)
            pe.wait_ge(oh_ready, 1)
            gather()
            pe.wait_ge(yinit_ready, 4)
            pe.wait_ge(b_up_in, 16 + 3)
            with pe.Fori(0, n_items) as i:
                w_landed = pe.value_load(tab[0:1, bass.ds(i + 48, 1)], min_val=16, max_val=16 * E)
                pe.wait_ge(xg_ready, i + 1)
                pe.wait_ge(bsel_ready, i + 1)
                for cc in range(4):
                    f = cc // 2
                    pe.matmul(bank[cc % 2][64 * f:64 * f + 64, :], bsel[:, :], b_up_sb[:, 512 * cc:512 * cc + 512],
                              start=True, stop=False, skip_group_check=True)
                for k in range(KT):
                    pe.wait_ge(w_slot[k], w_landed)
                    for cc in (0, 2, 1, 3):
                        f = cc // 2
                        ins = pe.matmul(bank[cc % 2][64 * f:64 * f + 64, :], xgT[:, k, :],
                                        ring[:, k, 512 * cc:512 * cc + 512], start=False, stop=(k == KT - 1),
                                        skip_group_check=True)
                    ins.then_inc(slot_used[k], 1)
                    if k == 2:
                        pe.wait_ge(rows_ready, i + 1)
                        pe.wait_ge(ohgT_ready, i + 1)
                        pe.wait_ge(y_added, 2 * i + 1)
                        combine(0)
                    if k == 4:
                        pe.wait_ge(y_added, 2 * i + 2)
                        combine(1)
                pe.wait_ge(ohg_ready, i + 1)
                for h in range(TH):
                    ins = pe.transpose(bank[5][:, P * h:P * h + P], ohg[:, h, :], ident[:, :])
                ins.then_inc(ohgT_done, 1)
                pe.wait_ge(oh_ready, i + 2)
                gather()
                pe.wait_ge(act_ready, i + 1)
                for j in range(4):
                    ins = pe.transpose(bank[3][:, P * j:P * j + P], act_sb[:, P * j:P * j + P], ident[:, :])
                ins.then_inc(actT_done, 1)
                pe.wait_ge(actT_ready, i + 1)
                for j in range(KT):
                    q = 8 + j // 2
                    if j % 2 == 0:
                        pe.wait_ge(w_slot[q], w_landed)
                    off = P * (j % 4) + CAP * (j // 4)
                    for cc in range(2):
                        ins = pe.matmul(bank[4][64 * cc:64 * cc + 64, :], actT[:, off:off + CAP],
                                        ring[:, q, D * (j % 2) + 512 * cc:D * (j % 2) + 512 * cc + 512],
                                        start=(j == 0), stop=(j == KT - 1))
                    if j % 2:
                        ins.then_inc(slot_used[q], 1)
            pe.wait_ge(rows_ready, n_items + 1)
            pe.wait_ge(ohgT_ready, n_items + 1)
            pe.wait_ge(y_added, 2 * n_items + 1)
            combine(0)
            pe.wait_ge(yacc_done, 1)
            combine(1)

        @block.vector
        def _(v):
            done = [0]

            def link(ins):
                done[0] += 1
                ins.then_inc(v_chain, 1)
                v.wait_ge(v_chain, done[0])

            stt = v.scalar_tensor_tensor

            def rstd(s, o):
                v.tensor_scalar(stat[:, o:o + 2], stat[:, s:s + 2], 1.0 / D, EPS, ALU.mult, ALU.add)\
                 .then_inc(mean_ready, 1)
                v.wait_ge(root_ready, s // 4 + 1)
                link(v.reciprocal(stat[:, o:o + 2], stat[:, o:o + 2]))

            v.wait_ge(csig_ready, 1)
            link(v.tensor_tensor(c_act[:, :], c_col[:, :], c_sig[:, :], ALU.mult))
            v.tensor_copy(c_rep[:, :, :], c_act[:, :].rearrange("p (k o) -> p k o", o=1).to_broadcast([P, KT, 32]))\
             .then_inc(c_ready, 1)
            v.wait_ge(sq_ready, TH)
            rstd(0, 2)
            for h in range(TH):
                v.tensor_scalar(xn[:, h, :], x_tok[:, h, :], stat[:, 2 + h:3 + h], None, ALU.mult).then_inc(xn_ready, 1)
            v.wait_ge(cols_ps, 1)
            v.tensor_copy(cols[:, :], bank[2][:, 0:C_END]).then_inc(cols_ready, 1)
            v.wait_ge(cols_ready, 1)
            v.wait_ge(consts, 8)
            dist_f = dist[:, :, :].rearrange("p m k -> p (m k)")
            link(stt(out=dist_f, in0=dist_f, scalar=-1.0, in1=dist_f, op0=ALU.mult, op1=ALU.max))
            link(v.memset(dist[0:64, :, 2 * CHUNK:KEYS], MASKED))
            link(v.memset(dist[64:128, :, 0:CHUNK], MASKED))
            link(v.memset(dist[:, 0, 0:CHUNK], MASKED))
            link(v.tensor_scalar(sink8[:, :], sinks_b[:, :], 8.0, None, ALU.mult))
            lam = cols[:, C_LAM:C_LAM + KT]
            z, w, y, y2, acc, pos = (sp_t[:, j, :] for j in range(6))
            stt(out=w, in0=lam, scalar=-1.0, in1=lam, op0=ALU.mult, op1=ALU.min).then_inc(lam_in, 1)
            v.wait_ge(lam_exp, 1)
            link(v.tensor_scalar(pos, lam, -1.0, 0.0, ALU.mult, ALU.max))
            link(v.tensor_scalar(w, z, 2.0, None, ALU.add))
            link(v.reciprocal(w, w))
            link(v.tensor_tensor(y, z, w, ALU.mult))
            link(v.tensor_tensor(y2, y, y, ALU.mult))
            link(v.tensor_scalar(acc, y2, 1.0 / 15, 1.0 / 13, ALU.mult, ALU.add))
            for n in (11, 9, 7, 5, 3, 1):
                link(v.tensor_tensor(acc, acc, y2, ALU.mult))
                link(v.tensor_scalar(acc, acc, 1.0 / n, None, ALU.add))
            link(v.tensor_tensor(acc, acc, y, ALU.mult))
            link(stt(out=acc, in0=acc, scalar=2.0, in1=pos, op0=ALU.mult, op1=ALU.add))
            link(v.tensor_scalar(neg8sp[:, :], acc, -8.0, None, ALU.mult))

            def mod_group(m, ps):
                link(stt(out=mod_add[:, m, :], in0=ps, scalar=mod_one[:, m:m + 1], in1=mod_add[:, m, :],
                         op0=ALU.add, op1=ALU.add))
                v.tensor_tensor(mod_add[:, m, :], mod_add[:, m, :], mod_mul[:, m, :], ALU.mult).then_inc(mod_vec, 1)

            v.wait_ge(late_in, 16 * 9)
            v.wait_ge(load_used, 4)
            mod_group(0, bank[3][:, :])
            v.wait_ge(ab_ps, 1)
            v.tensor_copy(ab[:, :], bank[2][:, 0:16]).then_inc(ab_ready, 1)

            v.wait_ge(proj_evac, T_K + 1)
            v.wait_ge(kz_ready, 1)
            v.tensor_copy(kz[64:128, 1, CHUNK:CHUNK + S], kz[0:64, 0, CHUNK:CHUNK + S]).then_inc(kz_ready, 1)
            v.tensor_copy(kz[0:64, 2, CHUNK:CHUNK + S], kz[64:128, 3, CHUNK:CHUNK + S]).then_inc(kz_ready, 1)
            v.wait_ge(proj_done, T_V + 1)
            for m in range(TH):
                v.tensor_tensor(v_tok[:, m, :], proj[T_V % 2][:, P * m:P * m + P], bv_b[:, :], ALU.add)\
                 .then_inc(v_evac, 1)
            v.tensor_tensor(v_prev[:, :], bank[2][0:CHUNK, 0:P], bv_b[0:CHUNK, :], ALU.add).then_inc(v_evac, 1)

            for k in range(KT):
                v.wait_ge(proj_evac, T_X + k)
                tap = lambda j: (page_x[:, k, j:j + S], cols[:, C_WCONV + 8 * j + k:C_WCONV + 8 * j + k + 1])
                src, wj = tap(0)
                link(v.tensor_scalar(xcT[:, k, :], src, wj, cols[:, C_BCONV + k:C_BCONV + k + 1], ALU.mult, ALU.add))
                for j in (1, 2, 3):
                    src, wj = tap(j)
                    ins = stt(out=xcT[:, k, :], in0=src, scalar=wj, in1=xcT[:, k, :], op0=ALU.mult, op1=ALU.add)
                    if j < 3:
                        link(ins)
                    else:
                        ins.then_inc(xc_ready, 1)

            def soften(h):
                b = h % 2
                v.wait_ge(s_done, h + 1)
                if h >= 2:
                    v.wait_ge(pt_done, h - 1)
                link(stt(out=sc[:, b, :, :].rearrange("p m k -> p (m k)"),
                         in0=dist[:, :, :].rearrange("p m k -> p (m k)"), scalar=NEG_SLOPE8[h],
                         in1=bank[2][:, 0:TH * KEYS], op0=ALU.mult, op1=ALU.add))
                link(v.tensor_reduce(soft[:, b, 0, :], sc[:, b, :, :], AX, ALU.max))
                link(v.tensor_scalar(soft[:, b, 1, :], soft[:, b, 0, :], sink8[:, h:h + 1], -0.125, ALU.max, ALU.mult))
                v.tensor_scalar(soft[:, b, 6, :], soft[:, b, 1, :], sinks_b[:, h:h + 1], None, ALU.add)\
                 .then_inc(negm_ready, 1)

            def normalise(h):
                b = h % 2
                v.wait_ge(exp_done, 3 * h + 3)
                link(v.tensor_tensor(soft[:, b, 4, :], soft[:, b, 2, :], soft[:, b, 3, :], ALU.add))
                link(v.reciprocal(soft[:, b, 5, :], soft[:, b, 4, :]))
                for m in range(TH):
                    ins = v.tensor_scalar(sc[:, b, m, :], sc[:, b, m, :], soft[:, b, 5, m:m + 1], None, ALU.mult)
                    if m == 0:
                        link(ins)
                    else:
                        ins.then_inc(p_ready, 1)

            for h in range(HEADS + 1):
                if h < HEADS:
                    soften(h)
                if h >= 1:
                    normalise(h - 1)

            v.wait_ge(ri_ready, 2 * KT)
            for half in range(2):
                ks = slice(4 * half, 4 * half + 4)
                la, e, zz, ii, xx = rT[:, ks, :], eT[:, ks, :], zT[:, ks, :], iT[:, ks, :], xcT[:, ks, :]
                v.tensor_tensor(la, la, neg8sp[:, ks].rearrange("p (k o) -> p k o", o=1).to_broadcast([P, 4, S]),
                                ALU.mult).then_inc(log_a, 1)
                v.wait_ge(log_a, half + 1)
                yy = page_x[:, ks, 3:3 + S]
                v.wait_ge(proj_evac, T_G)
                link(v.tensor_scalar(yy, la, 0.125, None, ALU.mult))
                link(v.tensor_scalar(e, yy, 1.0 / 120, None, ALU.mult))
                for coef in (1.0 / 24, 1.0 / 6, 0.5, 1.0):
                    link(stt(out=e, in0=e, scalar=coef, in1=yy, op0=ALU.add, op1=ALU.mult))
                for _ in range(3):
                    link(stt(out=e, in0=e, scalar=2.0, in1=e, op0=ALU.add, op1=ALU.mult))
                v.wait_ge(a_tab, half + 1)
                link(v.tensor_scalar(zz, zz, -1.0, None, ALU.add))
                link(v.tensor_scalar(la, la, LRU_SMALL, None, ALU.is_lt))
                link(v.copy_predicated(e, la.bitcast(I32), zz))
                v.tensor_scalar(la, e, 2.0, None, ALU.add).then_inc(v_chain, 1)
                done[0] += 1
                v.wait_ge(v_chain, done[0])
                v.tensor_tensor(zz, la, e, ALU.mult).then_inc(lru_w, 1)
                link(v.tensor_tensor(ii, ii, xx, ALU.mult))
                link(v.tensor_scalar(e, e, 1.0, None, ALU.add))
                v.wait_ge(lru_root, half + 1)
                link(v.tensor_tensor(ii, ii, zz, ALU.mult))
                for k in range(4 * half, 4 * half + 4):
                    link(v.tensor_tensor_scan(hT[:, k, :], eT[:, k, :], iT[:, k, :], 0.0, ALU.mult, ALU.add))
                ins = v.tensor_tensor(geluT[:, ks, :], geluT[:, ks, :], hT[:, ks, :], ALU.mult)
                if half == 0:
                    v.wait_ge(proj_evac, T_GA - 1)
                    link(ins)
                else:
                    ins.then_inc(hg_ready, 1)
            v.wait_ge(mod_done, 1)
            mod_group(1, bank[7][:, :])
            v.wait_ge(mod_done, 2)
            mod_group(2, bank[7][:, :])

            v.wait_ge(proj_evac, T_END - 1)
            for q in range(2 * KT):
                v.wait_ge(br_done, q + 1)
                page, d = (gaT, q) if q < KT else (glT, q - KT)
                v.tensor_tensor(page[:, d, :], page[:, d, :], proj[q % 2], ALU.mult).then_inc(br_evac, 1)
                if q >= KT:
                    v.wait_ge(br_evac, q + 1)
                    v.tensor_tensor(glT[:, d, :], glT[:, d, :], gaT[:, d, :], ALU.add).then_inc(merged, 1)

            v.wait_ge(sq1_ready, TH)
            rstd(4, 6)
            v.wait_ge(rows_b_in, 64)
            for h in range(TH):
                link(stt(out=scrap[:, h, :], in0=y_tok[:, h, :], scalar=stat[:, 6 + h:7 + h], in1=gate1_b,
                         op0=ALU.mult, op1=ALU.mult))
                v.tensor_tensor(x_tok[:, h, :], x_tok[:, h, :], scrap[:, h, :], ALU.add).then_inc(x1_ready, 1)
            v.wait_ge(sq2_ready, TH)
            rstd(8, 10)
            for h in range(TH):
                link(stt(out=u2[:, h, :], in0=x_tok[:, h, :], scalar=stat[:, 10 + h:11 + h], in1=scale2_b,
                         op0=ALU.mult, op1=ALU.mult))
                v.tensor_tensor(u2[:, h, :], u2[:, h, :], shift2_b, ALU.add).then_inc(u2_ready, 1)

            v.wait_ge(lg_done, 1)
            for h in range(TH):
                link(v.tensor_tensor(lg[:, h, :], bank[0][:, E * h:E * h + E], b_router_b[:, :], ALU.add))
            for h in range(TH):
                link(v.max(top8[:, h, :], lg[:, h, :]))
            for h in range(TH):
                ins = v.tensor_scalar(allow[:, h, 2:3], top8[:, h, 0:1], -1.0, None, ALU.mult)
                if h == 0:
                    link(ins)
                else:
                    ins.then_inc(top_ready, 1)
            for h in range(TH):
                fourth = top8[:, h, TOPK - 1:TOPK]
                link(v.tensor_scalar(gt[:, h, :], lg[:, h, :], fourth, None, ALU.is_gt))
                link(v.tensor_scalar(eq[:, h, :], lg[:, h, :], fourth, None, ALU.is_equal))
                link(v.tensor_tensor_scan(eq_n[:, h, :], ones[:, 0:E], eq[:, h, :], 0.0, ALU.mult, ALU.add))
                link(v.tensor_reduce(allow[:, h, 0:1], gt[:, h, :], AX, ALU.add))
                link(v.tensor_scalar(allow[:, h, 1:2], allow[:, h, 0:1], -1.0, float(TOPK), ALU.mult, ALU.add))
                link(v.tensor_scalar(eq_n[:, h, :], eq_n[:, h, :], allow[:, h, 1:2], None, ALU.is_le))
                link(v.tensor_tensor(eq[:, h, :], eq[:, h, :], eq_n[:, h, :], ALU.mult))
                ins = v.tensor_tensor(mask[:, h, :], gt[:, h, :], eq[:, h, :], ALU.add)
                if h == 0:
                    link(ins)
                else:
                    ins.then_inc(mask_ready, 1)
            v.wait_ge(mask_ready, 1)
            v.wait_ge(gexp_ready, TH)
            link(v.tensor_tensor(gate[:, :, :], gate[:, :, :], mask[:, :, :], ALU.mult))
            link(v.tensor_reduce(allow[:, :, 0], gate[:, :, :], AX, ALU.add))
            link(v.reciprocal(allow[:, :, 1], allow[:, :, 0]))
            for h in range(TH):
                ins = v.tensor_scalar(gate[:, h, :], gate[:, h, :], allow[:, h, 1:2], None, ALU.mult)
                if h == 0:
                    link(ins)
                else:
                    ins.then_inc(posm_ready, 1)
            v.wait_ge(pos_done, 1)
            flat = lambda t: t[:, :, :].rearrange("p h e -> p (h e)")
            link(stt(out=flat(posm), in0=bank[1][:, 0:2 * E], scalar=BIG, in1=flat(mask), op0=ALU.add, op1=ALU.mult))
            v.tensor_scalar(flat(posm), flat(posm), -BIG, None, ALU.add).then_inc(posm_ready, 1)
            link(v.tensor_copy(blocks[:, 4:6], bank[2][0:E, 0:2]))
            link(v.tensor_scalar(blocks[:, 0:2], blocks[:, 4:6], float(CAP), 1.0, ALU.is_gt, ALU.add))
            link(stt(out=blocks[:, 0:2], in0=blocks[:, 4:6], scalar=2.0 * CAP, in1=blocks[:, 0:2],
                     op0=ALU.is_gt, op1=ALU.add))
            stt(out=blocks[:, 0:2], in0=blocks[:, 4:6], scalar=3.0 * CAP, in1=blocks[:, 0:2],
                op0=ALU.is_gt, op1=ALU.add).then_inc(blocks_ready, 1)
            v.wait_ge(blocks_ready, 1)
            v.wait_ge(posT_done, 1)
            v.tensor_copy(posT[:, :], bank[3][0:E, 0:S]).then_inc(posT_ready, 1)
            v.tensor_copy(gateT[:, :], bank[3][0:E, S:2 * S]).then_inc(posT_ready, 1)
            v.wait_ge(cum_done, 1)
            link(v.tensor_copy(blocks[:, 2:4], bank[2][0:E, 4:6]))
            link(v.tensor_tensor(blocks[:, 6:8], blocks[:, 2:4], blocks[:, 0:2], ALU.add))
            v.wait_ge(numbers, 1)
            link(v.tensor_scalar(item_t[:, 0, :], iota_n[:, :], blocks[:, 2:3], None, ALU.is_ge))
            link(v.tensor_scalar(item_t[:, 1, :], iota_n[:, :], blocks[:, 6:7], None, ALU.is_lt))
            link(v.tensor_tensor(item_sel[0:E, :], item_t[:, 0, :], item_t[:, 1, :], ALU.mult))
            link(v.tensor_scalar(item_t[:, 0, :], iota_n[:, :], blocks[:, 2:3], -float(CAP), ALU.subtract, ALU.mult))
            stt(out=item_off[:, :], in0=item_t[:, 0, :], scalar=BIG, in1=item_sel[0:E, :],
                op0=ALU.add, op1=ALU.mult).then_inc(sel_ready, 1)
            v.wait_ge(item_done, 1)
            link(v.tensor_scalar(pos_item[:, :, :].rearrange("p h i -> p (h i)"), bank[1][:, 64:64 + TH * ITEMS],
                                 -BIG, None, ALU.add))
            link(v.tensor_copy(gate_item[:, :, :].rearrange("p h i -> p (h i)"), bank[1][:, 160:160 + TH * ITEMS]))
            link(v.tensor_copy(tab[:, 0:E + 2], bank[2][0:1, 8:8 + E + 2]))
            v.tensor_copy(tab[:, 48:96], bank[2][0:1, 64:64 + ITEMS]).then_inc(tab_ready, 1)
            v.wait_ge(yinit_done, 1)
            for h in range(TH):
                for cc in range(2):
                    v.tensor_copy(y_acc[:, h, 512 * cc:512 * cc + 512], bank[4 + 2 * h + cc][:, :])\
                     .then_inc(yinit_ready, 1)
            v.wait_ge(mix_done, 4)
            for r in range(E, P, 32):
                v.memset(page_gl[r:r + 32, :], 0.0).then_inc(b_up_in, 1)
            v.memset(rows, 0.0).then_inc(rows_ready, 1)
            v.memset(ohgT, 0.0).then_inc(ohgT_ready, 1)
            v.wait_ge(yinit_ready, 4)
            v.memset(lin[:, 0:1], 0.0).then_inc(y_added, 1)
            v.wait_ge(tab_ready, 1)
            v.wait_ge(y_added, 1)
            n_items = v.value_load(tab[0:1, E:E + 1], min_val=E, max_val=ITEMS - 1)

            def add_half(h, n):
                v.wait_ge(comb_done, n)
                for cc in range(2):
                    part = y_acc[:, h, 512 * cc:512 * cc + 512]
                    ins = v.tensor_tensor(part, part, bank[6 + cc][:, :], ALU.add)
                return ins

            def same_slot(dst, width, i):
                return v.tensor_tensor(dst, iota_s[:, :, 0:width],
                                       pos_item[:, :, bass.ds(i, 1)].to_broadcast([P, TH, width]), ALU.is_equal)

            same_slot(oh, CAP, 0).then_inc(oh_ready, 1)
            v.wait_ge(gather_done, 1)
            v.tensor_copy(xgT.rearrange("p k s -> p (k s)"), bank[2][:, :]).then_inc(xg_ready, 1)
            two = lambda b, o: b[:, o:512:2]
            with v.Fori(0, n_items) as i:
                same_slot(oh, CAP, i + 1).then_inc(oh_ready, 1)
                same_slot(ohg_h, P, i).then_inc(ohg_half, 1)
                v.wait_ge(ohg_half, i + 1)
                v.tensor_tensor(ohg, ohg_h, gate_item[:, :, bass.ds(i, 1)].to_broadcast([P, TH, P]), ALU.mult)\
                 .then_inc(ohg_ready, 1)
                for h in range(TH):
                    add_half(h, 2 * i + h + 1).then_inc(y_added, 1)
                v.wait_ge(slot_used[7], i + 1)
                for b in range(2):
                    ins = v.tensor_scalar(glu[:, 256 * b:256 * b + 256], two(bank[b], 0), LIMIT, None, ALU.min)
                ins.then_inc(glu_ready, 1)
                for b in range(2):
                    ins = v.tensor_scalar(lin[:, 256 * b:256 * b + 256], two(bank[b], 1), LIMIT, -LIMIT,
                                          ALU.min, ALU.max)
                ins.then_inc(lin_ready, 1)
                v.wait_ge(glu_ready, i + 1)
                v.wait_ge(lin_ready, i + 1)
                stt(out=lin, in0=lin, scalar=1.0, in1=glu, op0=ALU.add, op1=ALU.mult).then_inc(gl_ready, 1)
                v.wait_ge(gl_ready, i + 1)
                v.wait_ge(sig_ready, i + 1)
                v.tensor_tensor(act_sb, lin, sig, ALU.mult).then_inc(act_ready, 1)
                v.wait_ge(ohgT_done, i + 1)
                v.tensor_copy(ohgT, bank[5][:, 0:S]).then_inc(ohgT_ready, 1)
                v.wait_ge(gather_done, i + 2)
                v.tensor_copy(xgT.rearrange("p k s -> p (k s)"), bank[2][:, :]).then_inc(xg_ready, 1)
            for h in range(TH):
                add_half(h, 2 * n_items + h + 1).then_inc(yacc_done, 1)
            v.wait_ge(sq3_ready, TH)
            rstd(12, 14)
            for h in range(TH):
                link(stt(out=y_acc[:, h, :], in0=y_acc[:, h, :], scalar=stat[:, 14 + h:15 + h], in1=gate2_b,
                         op0=ALU.mult, op1=ALU.mult))
                v.tensor_tensor(x_tok[:, h, :], x_tok[:, h, :], y_acc[:, h, :], ALU.add).then_inc(x1_ready, 1)


_INS = ["x", "c", "w_ada", "b_ada", "g_pre_mix", "g_post_mix", "w_in", "b_in", "w_conv", "b_conv", "w_rg_a", "b_rg_a",
        "w_rg_x", "b_rg_x", "lru_lambda", "attn_sinks", "w_br_attn", "w_br_lru", "w_mix_out", "g_pre_moe",
        "g_post_moe", "w_router", "b_router", "w_up", "b_up", "w_down", "b_down"]
_OUTS = [((1, S, D), "float32")]


def kernel(**inputs):
    import numpy as _np
    import concourse.bacc as _bacc
    from concourse import mybir as _mybir
    from concourse.bass_utils import run_bass_kernel_spmd as _run

    nc = _bacc.Bacc("TRN2", target_bir_lowering=False, num_devices=1)
    arrays, args = {}, []
    for name in _INS:
        a = _np.ascontiguousarray(inputs[name])
        arrays[f"in_{name}_dram"] = a
        args.append(nc.dram_tensor(f"in_{name}_dram", a.shape, _mybir.dt.from_np(a.dtype), kind="ExternalInput").ap())
    for i, (shape, dtype) in enumerate(_OUTS):
        dt = _mybir.dt.from_np(_np.dtype(dtype))
        args.append(nc.dram_tensor(f"out_{i}_dram", shape, dt, kind="ExternalOutput").ap())
    args.append(nc.dram_tensor("mod_dram", (12, 512), _mybir.dt.float32, kind="Internal").ap())
    hybrid_block(nc, *args)
    r = _run(nc, [arrays], core_ids=[0])
    return r.results[0]["out_0_dram"]
```

```python
from contextlib import ExitStack

import concourse.bass as bass
from concourse import mybir

F32 = mybir.dt.float32
BF16 = mybir.dt.bfloat16
I32 = mybir.dt.int32
ALU = mybir.AluOpType
ACT = mybir.ActivationFunctionType
AX = mybir.AxisListType.X

P = 128
D = 1024
KT = D // P
S = 256
TH = S // P
HEADS, HD, CHUNK = 16, 64, 64
KEYS = 3 * CHUNK
E = 32
TOPK = 4
CAP = 64
ITEMS = 48
EPS = 1e-6
ALPHA, LIMIT = 1.702, 7.0
MASKED = 1e30
BIG = 8192.0
NEG_SLOPE8 = [-8.0 * 2.0 ** (-8.0 * (h + 1) / HEADS) for h in range(HEADS)]

T_K, T_V, T_X, T_G, T_GA, T_GL, T_END = 8, 9, 10, 18, 26, 34, 42
C_BIN, C_BCONV, C_WCONV, C_BA, C_BX, C_LAM, C_END = 0, 42, 50, 82, 90, 98, 106
L_ADA0, L_IN, L_ATTN, L_LRU, L_MIX, L_END = 0, 4, 23, 25, 27, 29
IN_GROUPS = 11
RIDE = 3
BAYS = 4
T_S, T_PT, T_PV, T_RI = 18, 20, 21, 20
LRU_SMALL = -0.85


def hybrid_block(nc, x, c, w_ada, b_ada, g_pre_mix, g_post_mix, w_in, b_in, w_conv, b_conv, w_rg_a, b_rg_a,
                 w_rg_x, b_rg_x, lru_lambda, attn_sinks, w_br_attn, w_br_lru, w_mix_out, g_pre_moe, g_post_moe,
                 w_router, b_router, w_up, b_up, w_down, b_down, out):
    with ExitStack() as ctx:
        def sb(name, shape, dt=F32):
            return ctx.enter_context(nc.sbuf_tensor(name, shape, dt))

        def sem(name):
            return ctx.enter_context(nc.semaphore(name))

        ring = sb("ring", [P, 12, 2048])
        bay = [ring[:, 2 * b:2 * b + 2, :].rearrange("p s n -> p (s n)") for b in range(BAYS)]
        xcT, rT, iT, eT = [ring[:, 8 + j, :].rearrange("p (k t) -> p k t", k=KT) for j in range(4)]

        x_tok = sb("x_tok", [P, TH, D])
        page_u = sb("page_u", [P, 2048])
        page_q = sb("page_q", [P, 2048])
        page_x = sb("page_x", [P, KT, 3 + S])
        page_g = sb("page_g", [P, 2048])
        page_ga = sb("page_ga", [P, 2048])
        page_gl = sb("page_gl", [P, 2048])
        page_a = sb("page_a", [P, 2048])
        page_n = sb("page_n", [P, 2048])
        tiles = lambda page: page[:, :].rearrange("p (k t) -> p k t", k=KT)
        halves = lambda page: page[:, :].rearrange("p (h d) -> p h d", h=TH)
        uT, qT, geluT, gaT, glT, attnT = map(tiles, (page_u, page_q, page_g, page_ga, page_gl, page_a))
        zT = tiles(page_n)
        xn = halves(page_n)
        hT = page_x[:, :, 3:3 + S]
        y_acc, u2 = halves(page_q), halves(page_g)
        u2T = tiles(page_u)
        scale2_b, shift2_b = page_a[:, 0:D], page_a[:, D:2 * D]
        gate1_b, gate2_b = page_n[:, 0:D], page_n[:, D:2 * D]
        b_up_raw = page_u[0:E, :]

        ident = sb("ident", [P, P])
        before = sb("before", [P, P])
        ones = sb("ones", [P, P])
        bd_a = sb("bd_a", [P, KT, P])
        bd_x = sb("bd_x", [P, KT, P])
        vec_rows = page_a[0:C_END, 512:512 + P]
        cols = sb("cols", [P, C_END])
        c_col = sb("c_col", [P, KT])
        c_sig = sb("c_sig", [P, KT])
        c_act = sb("c_act", [P, KT])
        c_rep = sb("c_rep", [P, KT, 32])
        mod_add = sb("mod_add", [P, 3, 512])
        mod_mul = sb("mod_mul", [P, 3, 512])
        mod_one = sb("mod_one", [P, 3])
        ab = sb("ab", [P, 16])
        stat = sb("stat", [P, 20])
        eps = sb("eps", [P, 1])
        kz = sb("kz", [P, 4, CHUNK + S])
        v_tok = sb("v_tok", [P, TH, P])
        v_prev = sb("v_prev", [CHUNK, P])
        bv_b = sb("bv_b", [P, P])
        sinks_b = sb("sinks_b", [P, HEADS])
        sink8 = sb("sink8", [P, HEADS])
        dist_i = page_a[:, 0:TH * KEYS].bitcast(I32).rearrange("p (h k) -> p h k", h=TH)
        dist = sb("dist", [P, TH, KEYS])
        sc = sb("sc", [P, 2, TH, KEYS])
        soft = sb("soft", [P, 2, 8, TH])
        pT = sb("pT", [P, 2, 3, P])
        neg8sp = sb("neg8sp", [P, KT])
        sp_t = sb("sp_t", [P, 6, KT])
        def carve(flat):
            at = [0]

            def take(*shape, rows=P, dt=F32):
                n = 1
                for w in shape:
                    n *= w
                part = flat[0:rows, at[0]:at[0] + n]
                at[0] += n
                assert at[0] <= flat.shape[1]
                if dt != F32:
                    part = part.bitcast(dt)
                return part.rearrange("p (a b) -> p a b", a=shape[0]) if len(shape) == 2 else part
            return take

        of_x = carve(page_x[:, :, :].rearrange("p k t -> p (k t)"))
        of_kz = carve(kz[:, :, :].rearrange("p k t -> p (k t)"))
        of_sc = carve(sc[:, :, :, :].rearrange("p a b c -> p (a b c)"))
        w_router_sb = of_x(KT, E)
        b_down_sb = of_x(D, rows=E)
        lg, gt, eq, eq_n, mask, gate, posm = (of_x(TH, E) for _ in range(7))
        top8 = of_x(TH, 8)
        allow = of_x(TH, 4)
        b_router_b = sb("b_router_b", [P, E])
        gateT = of_kz(S, rows=E)
        posT = of_kz(S, rows=E)
        iota_i = of_kz(TH, P, dt=I32)
        iota_s = of_kz(TH, P)
        iota_n = of_kz(ITEMS, rows=E)
        item_t = of_kz(2, ITEMS, rows=E)
        w_target = sb("w_target", [E, 2])
        blocks = sb("blocks", [E, 8])
        item_sel = sb("item_sel", [3 * E, ITEMS])
        item_off = of_kz(ITEMS, rows=E)
        pos_item = sb("pos_item", [P, TH, ITEMS])
        gate_item = sb("gate_item", [P, TH, ITEMS])
        tab = sb("tab", [1, 96], I32)
        oh = of_sc(TH, CAP)
        ohg = of_sc(TH, P)
        ohg_h = of_sc(TH, P)
        bsel = of_sc(CAP // 2, rows=3 * E, dt=BF16)
        xgT_flat = bd_a[:, 0:4, :].rearrange("p a b -> p (a b)")
        xgT = xgT_flat.rearrange("p (b j s) -> p b j s", b=4, j=2)
        actT = bd_a[:, 4:8, :].rearrange("p a b -> p (a b)")
        glu = bd_x[:, 0:4, :].rearrange("p a b -> p (a b)")
        lin = bd_x[:, 4:8, :].rearrange("p a b -> p (a b)")
        sig = mod_add[:, 0, :]
        act_sb = mod_add[:, 1, :]
        rows = mod_add[:, 2, :]
        ohgT = mod_mul[:, 0, 0:S]
        b_up_parts = mod_mul[0:3 * E, 1:3, :].rearrange("p a b -> p (a b)").bitcast(BF16)
        xg_tok = page_n[:, 0:512]
        scrap = halves(page_q)

        bank = [ctx.enter_context(nc.psum_tensor(f"bank{i}", [P, 512], F32)) for i in range(8)]
        proj = [bank[j][:, 0:256] for j in range(2)]

        small_in = sem("small_in")
        late_in = sem("late_in")
        x_in = sem("x_in")
        c_in = sem("c_in")
        bay_in = [sem(f"bay_in{b}") for b in range(BAYS)]
        load_used = sem("load_used")
        consts = sem("consts")
        g_chain = sem("g_chain")
        v_chain = sem("v_chain")
        a_chain = sem("a_chain")
        route_in = sem("route_in")
        numbers = sem("numbers")
        c_ready = sem("c_ready")
        csig_ready = sem("csig_ready")
        xn_ready = sem("xn_ready")
        sq_ready = sem("sq_ready")
        eps_ready = sem("eps_ready")
        root_ready = sem("root_ready")
        xT_done = sem("xT_done")
        cols_ps = sem("cols_ps")
        cols_ready = sem("cols_ready")
        mod_vec = sem("mod_vec")
        ab_ps = sem("ab_ps")
        ab_ready = sem("ab_ready")
        uT_ready = sem("uT_ready")
        proj_done = sem("proj_done")
        proj_evac = sem("proj_evac")
        v_evac = sem("v_evac")
        kz_ready = sem("kz_ready")
        s_done = sem("s_done")
        negm_ready = sem("negm_ready")
        exp_done = sem("exp_done")
        p_ready = sem("p_ready")
        pt_done = sem("pt_done")
        pt_ready = sem("pt_ready")
        pv_done = sem("pv_done")
        attn_ready = sem("attn_ready")
        xc_ready = sem("xc_ready")
        ri_done = sem("ri_done")
        ri_ready = sem("ri_ready")
        lam_exp = sem("lam_exp")
        lam_in = sem("lam_in")
        log_a = sem("log_a")
        a_tab = sem("a_tab")
        lru_w = sem("lru_w")
        lru_root = sem("lru_root")
        hg_ready = sem("hg_ready")
        br_done = sem("br_done")
        br_evac = sem("br_evac")
        merged = sem("merged")
        mix_done = sem("mix_done")
        sum_ready = sem("sum_ready")
        spread_done = sem("spread_done")
        spread_copied = sem("spread_copied")
        sq1_ready = sem("sq1_ready")
        sq2_ready = sem("sq2_ready")
        x1_ready = sem("x1_ready")
        sq3_ready = sem("sq3_ready")
        yacc_done = sem("yacc_done")
        u2_ready = sem("u2_ready")
        u2T_done = sem("u2T_done")
        u2T_ready = sem("u2T_ready")
        lg_done = sem("lg_done")
        top_ready = sem("top_ready")
        gexp_ready = sem("gexp_ready")
        mask_ready = sem("mask_ready")
        pos_done = sem("pos_done")
        posm_ready = sem("posm_ready")
        posT_done = sem("posT_done")
        posT_ready = sem("posT_ready")
        blocks_ready = sem("blocks_ready")
        cum_done = sem("cum_done")
        sel_ready = sem("sel_ready")
        item_done = sem("item_done")
        tab_ready = sem("tab_ready")
        b_up_in = sem("b_up_in")
        b_up_ready = sem("b_up_ready")
        yinit_done = sem("yinit_done")
        yinit_ready = sem("yinit_ready")
        w_slot = [sem(f"w_slot{k}") for k in range(12)]
        slot_used = [sem(f"slot_used{k}") for k in range(12)]
        oh_ready = sem("oh_ready")
        ohg_half = sem("ohg_half")
        ohg_ready = sem("ohg_ready")
        bsel_ready = sem("bsel_ready")
        gather_done = sem("gather_done")
        xg_copied = sem("xg_copied")
        xgT_done = sem("xgT_done")
        xg_ready = sem("xg_ready")
        ohgT_done = sem("ohgT_done")
        ohgT_ready = sem("ohgT_ready")
        glu_ready = sem("glu_ready")
        lin_ready = sem("lin_ready")
        gl_ready = sem("gl_ready")
        sig_ready = sem("sig_ready")
        act_ready = sem("act_ready")
        actT_done = sem("actT_done")
        actT_ready = sem("actT_ready")
        rows_ready = sem("rows_ready")
        comb_done = sem("comb_done")
        y_added = sem("y_added")
        out_done = sem("out_done")

        x_v = x.rearrange("b (h p) d -> (b p) h d", p=P)
        out_v = out.rearrange("b (h p) d -> (b p) h d", p=P)
        ada_v = w_ada.rearrange("l (p k) (m n) -> (l m) p k n", k=KT, m=3)
        in_v = w_in.rearrange("l (k p) n -> (l p) k n", p=P)
        square_v = {n: w.rearrange("l (k p) (c n) -> (l c) p k n", p=P, c=2)
                    for n, w in (("attn", w_br_attn), ("lru", w_br_lru), ("mix", w_mix_out))}
        up_v = w_up.rearrange("l e (k p) f -> (l e) p k f", p=P)
        down_v = w_down.rearrange("l e (q a p) f -> (l e) p q a f", p=P, a=2)
        row = lambda v: v.rearrange("l (k p) -> (l k) p", p=P)

        def loads():
            res = []

            def ada(m, b):
                res.append((bay[len(res) % BAYS].rearrange("p (k n) -> p k n", k=2), ada_v[m, :, 2 * b:2 * b + 2, :]))

            for b in range(4):
                ada(0, b)
            for g in range(IN_GROUPS):
                w = min(512, T_END * P - 512 * g)
                dst = bay[len(res) % BAYS].rearrange("p (k n) -> p k n", k=KT)[:, :, 0:w]
                res.append((dst, in_v[:, :, 512 * g:512 * g + w]))
                if g >= RIDE:
                    ada(1 + (g - RIDE) // 4, (g - RIDE) % 4)
            for n in ("attn", "lru", "mix"):
                for half in range(2):
                    res.append((bay[len(res) % BAYS].rearrange("p (k n) -> p k n", k=KT), square_v[n][half]))
            return res

        def in_load(g):
            return L_IN + g + max(0, g - RIDE)

        plan = loads()
        assert len(plan) == L_END
        block = ctx.enter_context(nc.Block())

        @block.sync
        def _(sp):
            sp.dma_start(c_col[:, :], c.rearrange("b (p k) -> (b p) k", k=KT)).then_inc(c_in, 16)
            sp.dma_start(x_tok[:, :, :], x_v).then_inc(x_in, 16)
            for n, (dst, src) in enumerate(plan):
                if n == 1:
                    sp.wait_ge(small_in, 16 * 9)
                if n >= BAYS:
                    sp.wait_ge(load_used, n - BAYS + 1)
                sp.dma_start(dst, src).then_inc(bay_in[n % BAYS], 16)
            for n in (1, 2, 3, 0):
                b = n
                last = max(q for q in range(L_END) if q % BAYS == b)
                sp.wait_ge(load_used, last + 1)
                for k in (2 * b, 2 * b + 1):
                    sp.dma_start(ring[:, k, :], up_v[0, :, k, :]).then_inc(w_slot[k], 16)
            sp.wait_ge(hg_ready, 1)
            for q in range(4):
                sp.dma_start(ring[:, 8 + q, :].rearrange("p (a f) -> p a f", a=2),
                             down_v[0, :, q, :, :]).then_inc(w_slot[8 + q], 16)
            sp.wait_ge(tab_ready, 1)
            with sp.Fori(1, E) as e:
                ahead = sp.value_load(tab[0:1, bass.ds(e, 1)], min_val=1, max_val=ITEMS)
                for k in range(KT):
                    sp.wait_ge(slot_used[k], ahead)
                    sp.dma_start(ring[:, k, :], up_v[bass.ds(e, 1), :, k, :].rearrange("e p f -> (e p) f"))\
                      .then_inc(w_slot[k], 16)
                for q in range(4):
                    sp.wait_ge(slot_used[8 + q], ahead)
                    sp.dma_start(ring[:, 8 + q, :].rearrange("p (a f) -> p a f", a=2),
                                 down_v[bass.ds(e, 1), :, q, :, :].rearrange("e p a f -> (e p) a f"))\
                      .then_inc(w_slot[8 + q], 16)

        @block.gpsimd
        def _(g):
            done = [0]

            def link(ins):
                done[0] += 1
                ins.then_inc(g_chain, 1)
                g.wait_ge(g_chain, done[0])

            link(g.memset(ident[:, :], 0.0))
            g.affine_select(out=ident[:, :], in_=ident[:, :], compare_op=ALU.not_equal, fill=1.0, base=0,
                            pattern=[[-1, P]], channel_multiplier=1).then_inc(consts, 1)
            g.memset(ones[:, :], 1.0).then_inc(consts, 1)
            link(g.memset(mod_add[:, :, :], 0.0))
            link(g.memset(mod_mul[:, :, :], 1.0))
            g.dma_start(mod_add[0:P:32, :, :], b_ada.rearrange("l (m j n) -> (l j) m n", m=3, j=4)).then_inc(late_in, 16)
            for j, m, gain in ((2, 0, g_pre_mix), (0, 1, g_post_mix), (0, 2, g_pre_moe), (2, 2, g_post_moe)):
                g.dma_start(mod_mul[32 * j:32 * j + 33:32, m, :], gain.rearrange("l (a n) -> (l a) n", a=2))\
                 .then_inc(late_in, 16)
            link(g.memset(mod_one[:, :], 0.0))
            link(g.memset(mod_one[64:128, 0:1], 1.0))
            g.memset(mod_one[0:64, 2:3], 1.0).then_inc(consts, 1)
            for bd, w in ((bd_a, w_rg_a), (bd_x, w_rg_x)):
                link(g.memset(bd[:, :, :], 0.0))
                pair = w.rearrange("l (k two) i j -> two (l i) k j", two=2)
                for f in range(2):
                    g.dma_start(bd[64 * f:64 * f + 64, :, 64 * f:64 * f + 64], pair[f]).then_inc(late_in, 16)
            g.memset(kz[:, :, :], 0.0).then_inc(consts, 1)
            g.memset(page_x[:, :, 0:3], 0.0).then_inc(consts, 1)
            link(g.memset(before[:, :], 1.0))
            g.affine_select(out=before[:, :], in_=before[:, :], compare_op=ALU.is_gt, fill=0.0, base=0,
                            pattern=[[1, P]], channel_multiplier=-1).then_inc(consts, 1)
            link(g.iota(dist_i[:, :, :], pattern=[[0, TH], [-1, KEYS]], base=CHUNK, channel_multiplier=1))
            g.tensor_copy(dist[:, :, :], dist_i[:, :, :]).then_inc(consts, 1)
            g.memset(item_sel[:, :], 0.0).then_inc(consts, 1)

            g.wait_ge(attn_ready, HEADS // 2)
            link(g.iota(iota_i[:, :, :], pattern=[[0, TH], [0, 2], [1, CAP]], base=0, channel_multiplier=0))
            link(g.tensor_copy(iota_s[:, :, :], iota_i[:, :, :]))
            link(g.iota(iota_i[0:E, 0, 0:ITEMS], pattern=[[1, ITEMS]], base=0, channel_multiplier=0))
            link(g.tensor_copy(iota_n[:, :], iota_i[0:E, 0, 0:ITEMS]))
            link(g.iota(iota_i[0:E, 1, 0:2], pattern=[[0, 2]], base=16, channel_multiplier=16))
            g.tensor_copy(w_target[:, :], iota_i[0:E, 1, 0:2]).then_inc(numbers, 1)
            def pick_bias(i):
                return g.tensor_copy(bsel, item_sel[:, bass.ds(i, 1)].to_broadcast([3 * E, CAP]))

            g.wait_ge(tab_ready, 1)
            n_items = g.value_load(tab[0:1, E:E + 1], min_val=E, max_val=ITEMS - 1)
            pick_bias(0).then_inc(bsel_ready, 1)
            with g.Fori(0, n_items) as i:
                g.wait_ge(slot_used[7], i + 1)
                pick_bias(i + 1).then_inc(bsel_ready, 1)

        @block.scalar
        def _(a):
            for r0, src in ((C_BIN, row(b_in)), (C_BCONV, row(b_conv)),
                            (C_WCONV, w_conv.rearrange("l j (k p) -> (l j k) p", p=P)),
                            (C_BA, b_rg_a.rearrange("l (k a) j -> (l k) (a j)", a=2)),
                            (C_BX, b_rg_x.rearrange("l (k a) j -> (l k) (a j)", a=2)), (C_LAM, row(lru_lambda))):
                a.dma_start(vec_rows[r0:r0 + src.shape[0], :], src).then_inc(small_in, 16)
            a.dma_start(bv_b[:, :], b_in[:, T_V * P:T_V * P + P].to_broadcast([P, P])).then_inc(small_in, 16)
            a.dma_start(sinks_b[:, :], attn_sinks.to_broadcast([P, HEADS])).then_inc(small_in, 16)
            a.dma_start(b_router_b[:, :], b_router.to_broadcast([P, E])).then_inc(small_in, 16)
            def root(src, dst, w=1):
                a.activation(stat[:, dst:dst + w], stat[:, src:src + w], ACT.Sqrt, scale=1.0 / D, bias=eps[:, :])\
                 .then_inc(root_ready, 1)

            a.wait_ge(eps_ready, 1)
            a.wait_ge(c_in, 16)
            a.activation(c_sig[:, :], c_col[:, :], ACT.Sigmoid).then_inc(csig_ready, 1)
            a.wait_ge(x_in, 16)
            for h in range(TH):
                a.activation(page_g[:, D * h:D * h + D], x_tok[:, h, :], ACT.Square,
                             accum_out=stat[:, h:h + 1]).then_inc(sq_ready, 1)
            a.wait_ge(sq_ready, TH)
            root(0, 2, TH)
            a.wait_ge(cols_ready, 1)
            a.wait_ge(lam_in, 1)
            a.activation(sp_t[:, 0, :], sp_t[:, 1, :], ACT.Exp).then_inc(lam_exp, 1)
            a.wait_ge(xT_done, 1)
            a.wait_ge(ab_ready, 1)
            for k in range(KT):
                a.activation(uT[:, k, :], bank[4 + k // 2][:, 256 * (k % 2):256 * (k % 2) + 256], ACT.Identity,
                             bias=ab[:, k:k + 1], scale=ab[:, 8 + k:9 + k]).then_inc(uT_ready, 1)

            def evac(t):
                a.wait_ge(proj_done, t + 1)
                src, bias = proj[t % 2], cols[:, C_BIN + t:C_BIN + t + 1]
                if t < T_K:
                    ins = a.activation(qT[:, t, :], src, ACT.Identity, bias=bias)
                elif t == T_K:
                    a.wait_ge(consts, 8)
                    for f in range(2):
                        half = slice(64 * f, 64 * f + 64)
                        ins = a.activation(kz[half, 3 * f, CHUNK:CHUNK + S], src[half, :], ACT.Identity,
                                           bias=cols[half, C_BIN + t:C_BIN + t + 1])
                        if f == 0:
                            ins.then_inc(kz_ready, 1)
                elif t < T_G:
                    ins = a.activation(page_x[:, t - T_X, 3:3 + S], src, ACT.Identity, bias=bias)
                elif t < T_GA:
                    ins = a.activation(geluT[:, t - T_G, :], src, ACT.Gelu_apprx_tanh, bias=bias)
                elif t < T_GL:
                    ins = a.activation(gaT[:, t - T_GA, :], src, ACT.Sigmoid, bias=bias)
                else:
                    ins = a.activation(glT[:, t - T_GL, :], src, ACT.Sigmoid, bias=bias)
                ins.then_inc(proj_evac, 1)

            for t in range(T_END):
                if t != T_V:
                    evac(t)
                h = t - T_S
                if 0 <= h < HEADS:
                    a.wait_ge(negm_ready, h + 1)
                    for m in range(TH):
                        a.activation(sc[:, h % 2, m, :], sc[:, h % 2, m, :], ACT.Exp, scale=0.125,
                                     bias=soft[:, h % 2, 1, m:m + 1], accum_out=soft[:, h % 2, 2, m:m + 1])\
                         .then_inc(exp_done, 1)
                    a.activation(soft[:, h % 2, 3, :], soft[:, h % 2, 6, :], ACT.Exp).then_inc(exp_done, 1)
                h = t - T_PT
                if 0 <= h < HEADS:
                    a.wait_ge(pt_done, h + 1)
                    a.activation(pT[:, h % 2, 0:2, :].rearrange("p a b -> p (a b)"), bank[3][:, 0:256],
                                 ACT.Copy).then_inc(pt_ready, 1)
                    a.activation(pT[0:CHUNK, h % 2, 2, :], bank[3][0:CHUNK, 256:384], ACT.Copy).then_inc(pt_ready, 1)
                h = t - T_PV
                if 0 <= h < HEADS and h % 2:
                    a.wait_ge(pv_done, h + 1)
                    a.activation(attnT[:, h // 2, :], bank[4][:, 0:256], ACT.Copy).then_inc(attn_ready, 1)
                k = t - T_RI
                if 0 <= k < KT:
                    a.wait_ge(ri_done, k + 1)
                    a.activation(rT[:, k, :], bank[5 + k % 2][:, 0:256], ACT.Sigmoid,
                                 bias=cols[:, C_BA + k:C_BA + k + 1]).then_inc(ri_ready, 1)
                    a.activation(iT[:, k, :], bank[5 + k % 2][:, 256:512], ACT.Sigmoid,
                                 bias=cols[:, C_BX + k:C_BX + k + 1]).then_inc(ri_ready, 1)
            def evac_attn(tiles_d):
                for d in tiles_d:
                    a.wait_ge(br_done, d + 1)
                    a.activation(qT[:, d, :], proj[d % 2], ACT.Copy).then_inc(br_evac, 1)

            for half in range(2):
                ks = slice(4 * half, 4 * half + 4)
                a.wait_ge(log_a, half + 1)
                a.activation(zT[:, ks, :], rT[:, ks, :], ACT.Exp).then_inc(a_tab, 1)
                if half == 1:
                    evac_attn(range(4))
                a.wait_ge(lru_w, half + 1)
                a.activation(zT[:, ks, :], zT[:, ks, :], ACT.Sqrt, scale=-1.0).then_inc(lru_root, 1)
            a.wait_ge(proj_done, T_END)
            a.dma_start(b_up_raw, b_up.rearrange("l e f -> (l e) f")).then_inc(b_up_in, 16)
            evac_attn(range(4, KT))
            a.wait_ge(hg_ready, 1)
            a.dma_start(w_router_sb, w_router.rearrange("l (k p) e -> (l p) k e", p=P)).then_inc(route_in, 16)
            a.dma_start(b_down_sb, b_down.rearrange("l e d -> (l e) d")).then_inc(route_in, 16)

            for n, dst in enumerate((gate1_b, shift2_b, scale2_b, gate2_b)):
                a.wait_ge(spread_done, n // 2 + 1)
                for cc in range(2):
                    a.activation(dst[:, 512 * cc:512 * cc + 512], bank[2 + 2 * (n % 2) + cc][:, :], ACT.Copy)\
                     .then_inc(spread_copied, 1)
            for h in range(TH):
                c0 = 4 + 6 * h
                for cc in range(2):
                    a.wait_ge(mix_done, 2 * h + cc + 1)
                    a.activation(scrap[:, h, 512 * cc:512 * cc + 512], bank[2 * h + cc][:, :], ACT.Square,
                                 accum_out=stat[:, c0 + cc:c0 + cc + 1]).then_inc(sq1_ready, 1)
                a.wait_ge(sum_ready, h + 1)
                root(c0 + 2, c0 + 3)
                a.wait_ge(x1_ready, h + 1)
                a.activation(scrap[:, h, :], x_tok[:, h, :], ACT.Square,
                             accum_out=stat[:, c0 + 4:c0 + 5]).then_inc(sq2_ready, 1)
                a.wait_ge(sq2_ready, h + 1)
                root(c0 + 4, c0 + 5)
                a.wait_ge(u2T_done, h + 1)
                a.activation(u2T[:, 0:4, P * h:P * h + P], bank[4 + 2 * h][:, :].rearrange("p (k t) -> p k t", t=P),
                             ACT.Copy).then_inc(u2T_ready, 1)
            a.wait_ge(top_ready, 1)
            for h in range(TH):
                a.activation(gate[:, h, :], lg[:, h, :], ACT.Exp, bias=allow[:, h, 2:3]).then_inc(gexp_ready, 1)

            a.wait_ge(tab_ready, 1)
            n_items = a.value_load(tab[0:1, E:E + 1], min_val=E, max_val=ITEMS - 1)
            a.wait_ge(gather_done, 1)
            a.activation(xg_tok, bank[2][:, :], ACT.Copy).then_inc(xg_copied, 1)
            with a.Fori(0, n_items) as i:
                a.wait_ge(glu_ready, i + 1)
                a.activation(sig, glu, ACT.Sigmoid, scale=ALPHA).then_inc(sig_ready, 1)
                a.wait_ge(gather_done, i + 2)
                a.activation(xg_tok, bank[2][:, :], ACT.Copy).then_inc(xg_copied, 1)
                a.wait_ge(actT_done, i + 1)
                a.activation(actT, bank[3][:, :], ACT.Copy).then_inc(actT_ready, 1)
                a.wait_ge(slot_used[11], i + 1)
                a.activation(rows, bank[4][:, :], ACT.Copy).then_inc(rows_ready, 1)
            for h in range(TH):
                a.wait_ge(yacc_done, h + 1)
                a.activation(u2[:, h, :], y_acc[:, h, :], ACT.Square,
                             accum_out=stat[:, 16 + 2 * h:17 + 2 * h]).then_inc(sq3_ready, 1)
                a.wait_ge(sq3_ready, h + 1)
                root(16 + 2 * h, 17 + 2 * h)
            for h in range(TH):
                a.wait_ge(x1_ready, TH + h + 1)
                a.dma_start(out_v[:, h, :], x_tok[:, h, :]).then_inc(out_done, 16)
            a.wait_ge(out_done, 16 * TH)

        @block.tensor
        def _(pe):
            def landed(n):
                pe.wait_ge(bay_in[n % BAYS], 16 * (n // BAYS + 1))

            pe.wait_ge(consts, 1)
            pe.wait_ge(small_in, 16 * 9)
            pe.transpose(bank[2][:, 0:C_END], vec_rows[:, :], ident[0:C_END, 0:C_END]).then_inc(cols_ps, 1)
            pe.wait_ge(xn_ready, TH)
            for k in range(KT):
                for h in range(TH):
                    ins = pe.transpose(bank[4 + k // 2][:, 256 * (k % 2) + P * h:256 * (k % 2) + P * h + P],
                                       xn[:, h, P * k:P * k + P], ident[:, :])
            ins.then_inc(xT_done, 1)

            def modulation(b, n, ps):
                landed(n)
                w = bay[n % BAYS].rearrange("p (k n) -> p k n", k=2)
                for k in (0, 1):
                    for j in range(4):
                        ins = pe.matmul(ps[32 * j:32 * j + 32, :], c_rep[:, 2 * b + k, :],
                                        w[:, k, 512 * j:512 * j + 512], start=(b == 0 and k == 0),
                                        stop=(b == 3 and k == 1), tile_position=(0, 32 * j))
                ins.then_inc(load_used, 1)

            pe.wait_ge(c_ready, 1)
            for b in range(4):
                modulation(b, L_ADA0 + b, bank[3])
            pe.wait_ge(cols_ready, 1)
            pe.wait_ge(mod_vec, 1)
            for b in range(4):
                ins = pe.transpose(bank[2][:, P * b:P * b + P], mod_add[:, 0, P * b:P * b + P], ident[:, :])
            ins.then_inc(ab_ps, 1)

            def column_tile(t):
                n = in_load(t // 4)
                if t % 4 == 0:
                    landed(n)
                if t == 0:
                    pe.wait_ge(uT_ready, KT)
                if t - 2 == T_V:
                    pe.wait_ge(v_evac, 3)
                elif t >= 2:
                    pe.wait_ge(proj_evac, t - 1 if t - 2 < T_V else t - 2)
                w = bay[n % BAYS].rearrange("p (k n) -> p k n", k=KT)[:, :, P * (t % 4):P * (t % 4) + P]
                if t == T_V:
                    for m in range(TH):
                        for k in range(KT):
                            pe.matmul(proj[t % 2][:, P * m:P * m + P], uT[:, k, P * m:P * m + P], w[:, k, :],
                                      start=(k == 0), stop=(k == KT - 1))
                    for k in range(KT):
                        ins = pe.matmul(bank[2][0:CHUNK, 0:P], uT[:, k, CHUNK:P], w[:, k, :],
                                        start=(k == 0), stop=(k == KT - 1))
                else:
                    for k in range(KT):
                        ins = pe.matmul(proj[t % 2], w[:, k, :], uT[:, k, :], start=(k == 0), stop=(k == KT - 1))
                ins.then_inc(proj_done, 1)

            def scores(h):
                kv, f = h // 8, h % 2
                if h == 0:
                    pe.wait_ge(v_evac, 3)
                    pe.wait_ge(kz_ready, 3)
                    pe.wait_ge(proj_evac, T_K + 1)
                else:
                    pe.wait_ge(negm_ready, h)
                for m in range(TH):
                    ins = pe.matmul(bank[2][:, KEYS * m:KEYS * m + KEYS], qT[:, h // 2, P * m:P * m + P],
                                    kz[:, 2 * kv + f, P * m:P * m + KEYS], start=True, stop=True)
                ins.then_inc(s_done, 1)

            def turn_probs(h):
                pe.wait_ge(p_ready, h + 1)
                if h >= 1:
                    pe.wait_ge(pt_ready, 2 * h)
                for m in range(TH):
                    pe.transpose(bank[3][:, P * m:P * m + P], sc[:, h % 2, m, CHUNK:KEYS], ident[:, :])
                pe.transpose(bank[3][0:CHUNK, 2 * P:3 * P], sc[:, h % 2, 1, 0:CHUNK], ident[:, :])\
                  .then_inc(pt_done, 1)

            def values(h):
                kv, f = h // 8, h % 2
                pe.wait_ge(pt_ready, 2 * h + 2)
                if h >= 2:
                    pe.wait_ge(attn_ready, h // 2)
                o, v = bank[4][64 * f:64 * f + 64, :], slice(64 * kv, 64 * kv + 64)
                pe.matmul(o[:, 0:P], v_tok[:, 0, v], pT[:, h % 2, 0, :], start=True, stop=True)
                pe.matmul(o[:, P:2 * P], v_tok[:, 1, v], pT[:, h % 2, 1, :], start=True, stop=False)
                pe.matmul(o[:, P:2 * P], v_prev[:, v], pT[0:CHUNK, h % 2, 2, :], start=False, stop=True)\
                  .then_inc(pv_done, 1)

            def lru_gates(k):
                pe.wait_ge(xc_ready, k + 1)
                if k == 0:
                    pe.wait_ge(late_in, 16 * 9)
                if k >= 2:
                    pe.wait_ge(ri_ready, 2 * (k - 1))
                ps = bank[5 + k % 2]
                pe.matmul(ps[:, 0:256], bd_a[:, k, :], xcT[:, k, :], start=True, stop=True)
                pe.matmul(ps[:, 256:512], bd_x[:, k, :], xcT[:, k, :], start=True, stop=True).then_inc(ri_done, 1)

            for t in range(T_END):
                column_tile(t)
                if t % 4 == 3 or t == T_END - 1:
                    pe.wait_ge(proj_done, t + 1)
                    pe.nop().then_inc(load_used, 1)
                if 0 <= t - T_S < HEADS:
                    scores(t - T_S)
                if 0 <= t - T_PT < HEADS:
                    turn_probs(t - T_PT)
                if 0 <= t - T_PV < HEADS:
                    values(t - T_PV)
                if 0 <= t - T_RI < KT:
                    lru_gates(t - T_RI)
                if (t % 4 == 3 or t == T_END - 1) and t // 4 >= RIDE:
                    g = t // 4
                    m, b = 1 + (g - RIDE) // 4, (g - RIDE) % 4
                    if (m, b) == (2, 0):
                        pe.wait_ge(ri_ready, 2 * KT)
                    modulation(b, in_load(g) + 1, bank[8 - m])

            def branch(first, src, base):
                for d in range(KT):
                    n = first + d // 4
                    if d % 4 == 0:
                        landed(n)
                    q = base + d
                    if q >= 2:
                        pe.wait_ge(br_evac, q - 1)
                    elif q == 0:
                        pe.wait_ge(proj_evac, T_END - 1)
                    w = bay[n % BAYS].rearrange("p (k n) -> p k n", k=KT)[:, :, P * (d % 4):P * (d % 4) + P]
                    for k in range(KT):
                        ins = pe.matmul(proj[q % 2], w[:, k, :], src[:, k, :], start=(k == 0), stop=(k == KT - 1))
                    ins.then_inc(br_done, 1)
                    if d % 4 == 3:
                        pe.wait_ge(br_done, q + 1)
                        pe.nop().then_inc(load_used, 1)

            pe.wait_ge(attn_ready, HEADS // 2)
            branch(L_ATTN, attnT, 0)
            pe.wait_ge(hg_ready, 1)
            branch(L_LRU, geluT, KT)

            def spread(m, ps):
                pe.wait_ge(mod_vec, m + 1)
                for j in range(4):
                    ins = pe.matmul(ps[j][:, :], ones[32 * j:32 * j + 1, :], mod_add[32 * j:32 * j + 1, m, :],
                                    start=True, stop=True, tile_position=(32 * j, 0))
                ins.then_inc(spread_done, 1)

            spread(1, bank[2:6])
            pe.wait_ge(spread_copied, 4)
            spread(2, bank[2:6])
            pe.wait_ge(merged, KT)
            pe.wait_ge(spread_copied, 8)
            for cc in range(2):
                landed(L_MIX + cc)
            for h in range(TH):
                for cc in range(2):
                    w = bay[(L_MIX + cc) % BAYS].rearrange("p (k n) -> p k n", k=KT)
                    for k in range(KT):
                        ins = pe.matmul(bank[2 * h + cc][:, :], glT[:, k, P * h:P * h + P], w[:, k, :],
                                        start=(k == 0), stop=(k == KT - 1))
                    ins.then_inc(mix_done, 1)
            pe.wait_ge(mix_done, 4)
            pe.nop().then_inc(load_used, 1)
            pe.nop().then_inc(load_used, 1)

            pe.wait_ge(route_in, 32)
            for h in range(TH):
                pe.wait_ge(u2_ready, h + 1)
                for k in range(KT):
                    ins = pe.transpose(bank[4 + 2 * h + k // 4][:, P * (k % 4):P * (k % 4) + P],
                                       u2[:, h, P * k:P * k + P], ident[:, :])
                ins.then_inc(u2T_done, 1)
                pe.wait_ge(u2T_ready, 2 * h + 2)
                for k in range(KT):
                    ins = pe.matmul(bank[0][:, E * h:E * h + E], u2T[:, k, P * h:P * h + P], w_router_sb[:, k, :],
                                    start=(k == 0), stop=(k == KT - 1))
            ins.then_inc(lg_done, 1)
            pe.wait_ge(mask_ready, 1)
            pe.wait_ge(consts, 8)
            pe.matmul(bank[1][:, 0:E], before[:, :], mask[:, 0, :], start=True, stop=True)
            pe.matmul(bank[1][:, E:2 * E], before[:, :], mask[:, 1, :], start=True, stop=False)
            pe.matmul(bank[1][:, E:2 * E], ones[:, :], mask[:, 0, :], start=False, stop=True)
            pe.matmul(bank[2][0:E, 0:2], mask[:, 0, :], ones[:, 0:2], start=True, stop=False)
            pe.matmul(bank[2][0:E, 0:2], mask[:, 1, :], ones[:, 0:2], start=False, stop=True).then_inc(pos_done, 1)
            pe.wait_ge(posm_ready, 2)
            for h in range(TH):
                pe.transpose(bank[3][0:E, P * h:P * h + P], posm[:, h, :], ident[:, :])
            for h in range(TH):
                ins = pe.transpose(bank[3][0:E, S + P * h:S + P * h + P], gate[:, h, :], ident[:, :])
            ins.then_inc(posT_done, 1)
            pe.wait_ge(blocks_ready, 1)
            pe.matmul(bank[2][0:E, 4:6], before[0:E, 0:E], blocks[:, 0:2], start=True, stop=True)
            pe.matmul(bank[2][0:1, 8:8 + E + 2], blocks[:, 0:1], before[0:E, 0:E + 2], start=True, stop=True)\
              .then_inc(cum_done, 1)
            pe.wait_ge(sel_ready, 1)
            pe.wait_ge(posT_ready, 2)
            for h in range(TH):
                pe.matmul(bank[1][:, 64 + ITEMS * h:64 + ITEMS * h + ITEMS], posT[:, P * h:P * h + P],
                          item_sel[0:E, :], start=True, stop=False)
                pe.matmul(bank[1][:, 64 + ITEMS * h:64 + ITEMS * h + ITEMS], ones[0:E, :], item_off[:, :],
                          start=False, stop=True)
            for h in range(TH):
                pe.matmul(bank[1][:, 160 + ITEMS * h:160 + ITEMS * h + ITEMS], gateT[:, P * h:P * h + P],
                          item_sel[0:E, :], start=True, stop=True)
            pe.matmul(bank[2][0:1, 64:64 + ITEMS], w_target[:, 0:1], item_sel[0:E, :], start=True, stop=True)\
              .then_inc(item_done, 1)
            pe.wait_ge(u2T_ready, 2 * TH)
            for h in range(TH):
                for cc in range(2):
                    ins = pe.matmul(bank[4 + 2 * h + cc][:, :], gateT[:, P * h:P * h + P],
                                    b_down_sb[:, 512 * cc:512 * cc + 512], start=True, stop=True)
            ins.then_inc(yinit_done, 1)

            def gather():
                for h in range(TH):
                    for j in range(2):
                        ins = pe.matmul(bank[2][64 * j:64 * j + 64, :], oh[:, h, :], u2[:, h, 512 * j:512 * j + 512],
                                        start=(h == 0), stop=(h == TH - 1))
                ins.then_inc(gather_done, 1)

            def turn_gathered():
                for b in range(4):
                    ins = pe.transpose(bank[2][:, P * b:P * b + P], xg_tok[:, P * b:P * b + P], ident[:, :])
                ins.then_inc(xgT_done, 1)

            def combine(h):
                for cc in range(2):
                    half = slice(64 * cc, 64 * cc + 64)
                    ins = pe.matmul(bank[6 + cc][:, :], ohgT[half, P * h:P * h + P], rows[half, :],
                                    start=True, stop=True)
                ins.then_inc(comb_done, 1)

            pe.wait_ge(tab_ready, 1)
            n_items = pe.value_load(tab[0:1, E:E + 1], min_val=E, max_val=ITEMS - 1)
            pe.wait_ge(oh_ready, 1)
            gather()
            pe.wait_ge(xg_copied, 1)
            turn_gathered()
            pe.wait_ge(yinit_ready, 4)
            pe.wait_ge(b_up_ready, 1)
            with pe.Fori(0, n_items) as i:
                w_landed = pe.value_load(tab[0:1, bass.ds(i + 48, 1)], min_val=16, max_val=16 * E)
                pe.wait_ge(xg_ready, i + 1)
                pe.wait_ge(bsel_ready, i + 1)
                for cc in range(4):
                    f = cc // 2
                    pe.matmul(bank[cc % 2][64 * f:64 * f + 64, :], bsel[:, :], b_up_parts[:, 512 * cc:512 * cc + 512],
                              start=True, stop=False, skip_group_check=True)
                for k in range(KT):
                    pe.wait_ge(w_slot[k], w_landed)
                    for cc in (0, 2, 1, 3):
                        f = cc // 2
                        ins = pe.matmul(bank[cc % 2][64 * f:64 * f + 64, :], xgT[:, k % 4, k // 4, :],
                                        ring[:, k, 512 * cc:512 * cc + 512], start=False, stop=(k == KT - 1),
                                        skip_group_check=True)
                    ins.then_inc(slot_used[k], 1)
                pe.wait_ge(ohg_ready, i + 1)
                for h in range(TH):
                    ins = pe.transpose(bank[5][:, P * h:P * h + P], ohg[:, h, :], ident[:, :])
                ins.then_inc(ohgT_done, 1)
                pe.wait_ge(oh_ready, i + 2)
                gather()
                pe.wait_ge(rows_ready, i + 1)
                pe.wait_ge(ohgT_ready, i + 1)
                pe.wait_ge(y_added, 2 * i + 1)
                combine(0)
                pe.wait_ge(act_ready, i + 1)
                for j in range(4):
                    ins = pe.transpose(bank[3][:, P * j:P * j + P], act_sb[:, P * j:P * j + P], ident[:, :])
                ins.then_inc(actT_done, 1)
                pe.wait_ge(y_added, 2 * i + 2)
                combine(1)
                pe.wait_ge(actT_ready, i + 1)
                for j in range(KT):
                    q = 8 + j // 2
                    if j % 2 == 0:
                        pe.wait_ge(w_slot[q], w_landed)
                    off = P * (j % 4) + CAP * (j // 4)
                    for cc in range(2):
                        ins = pe.matmul(bank[4][64 * cc:64 * cc + 64, :], actT[:, off:off + CAP],
                                        ring[:, q, D * (j % 2) + 512 * cc:D * (j % 2) + 512 * cc + 512],
                                        start=(j == 0), stop=(j == KT - 1))
                    if j % 2:
                        ins.then_inc(slot_used[q], 1)
                    if j == 4:
                        pe.wait_ge(xg_copied, i + 2)
                        turn_gathered()
            pe.wait_ge(rows_ready, n_items + 1)
            pe.wait_ge(ohgT_ready, n_items + 1)
            pe.wait_ge(y_added, 2 * n_items + 1)
            combine(0)
            pe.wait_ge(yacc_done, 1)
            combine(1)

        @block.vector
        def _(v):
            done = [0]

            def link(ins):
                done[0] += 1
                ins.then_inc(v_chain, 1)
                v.wait_ge(v_chain, done[0])

            stt = v.scalar_tensor_tensor

            def rstd(n, at, w=1):
                v.wait_ge(root_ready, n)
                link(v.reciprocal(stat[:, at:at + w], stat[:, at:at + w]))

            v.memset(eps[:, :], EPS).then_inc(eps_ready, 1)
            v.wait_ge(csig_ready, 1)
            link(v.tensor_tensor(c_act[:, :], c_col[:, :], c_sig[:, :], ALU.mult))
            v.tensor_copy(c_rep[:, :, :], c_act[:, :].rearrange("p (k o) -> p k o", o=1).to_broadcast([P, KT, 32]))\
             .then_inc(c_ready, 1)
            rstd(1, 2, TH)
            for h in range(TH):
                v.tensor_scalar(xn[:, h, :], x_tok[:, h, :], stat[:, 2 + h:3 + h], None, ALU.mult).then_inc(xn_ready, 1)
            v.wait_ge(cols_ps, 1)
            v.tensor_copy(cols[:, :], bank[2][:, 0:C_END]).then_inc(cols_ready, 1)
            v.wait_ge(cols_ready, 1)
            v.wait_ge(consts, 8)
            dist_f = dist[:, :, :].rearrange("p m k -> p (m k)")
            link(stt(out=dist_f, in0=dist_f, scalar=-1.0, in1=dist_f, op0=ALU.mult, op1=ALU.max))
            link(v.memset(dist[0:64, :, 2 * CHUNK:KEYS], MASKED))
            link(v.memset(dist[64:128, :, 0:CHUNK], MASKED))
            link(v.memset(dist[:, 0, 0:CHUNK], MASKED))
            v.wait_ge(small_in, 16 * 9)
            link(v.tensor_scalar(sink8[:, :], sinks_b[:, :], 8.0, None, ALU.mult))
            lam = cols[:, C_LAM:C_LAM + KT]
            z, w, y, y2, acc, pos = (sp_t[:, j, :] for j in range(6))
            stt(out=w, in0=lam, scalar=-1.0, in1=lam, op0=ALU.mult, op1=ALU.min).then_inc(lam_in, 1)
            v.wait_ge(lam_exp, 1)
            link(v.tensor_scalar(pos, lam, -1.0, 0.0, ALU.mult, ALU.max))
            link(v.tensor_scalar(w, z, 2.0, None, ALU.add))
            link(v.reciprocal(w, w))
            link(v.tensor_tensor(y, z, w, ALU.mult))
            link(v.tensor_tensor(y2, y, y, ALU.mult))
            link(v.tensor_scalar(acc, y2, 1.0 / 15, 1.0 / 13, ALU.mult, ALU.add))
            for n in (11, 9, 7, 5, 3, 1):
                link(v.tensor_tensor(acc, acc, y2, ALU.mult))
                link(v.tensor_scalar(acc, acc, 1.0 / n, None, ALU.add))
            link(v.tensor_tensor(acc, acc, y, ALU.mult))
            link(stt(out=acc, in0=acc, scalar=2.0, in1=pos, op0=ALU.mult, op1=ALU.add))
            link(v.tensor_scalar(neg8sp[:, :], acc, -8.0, None, ALU.mult))

            def mod_group(m, ps):
                link(stt(out=mod_add[:, m, :], in0=ps, scalar=mod_one[:, m:m + 1], in1=mod_add[:, m, :],
                         op0=ALU.add, op1=ALU.add))
                v.tensor_tensor(mod_add[:, m, :], mod_add[:, m, :], mod_mul[:, m, :], ALU.mult).then_inc(mod_vec, 1)

            v.wait_ge(late_in, 16 * 9)
            v.wait_ge(load_used, 4)
            mod_group(0, bank[3][:, :])
            v.wait_ge(ab_ps, 1)
            v.tensor_copy(ab[:, :].rearrange("p (j b) -> p b j", j=4),
                          bank[2][:, :].rearrange("p (b c) -> p b c", b=4)[:, :, 0:P:32]).then_inc(ab_ready, 1)

            v.wait_ge(proj_evac, T_K + 1)
            v.wait_ge(kz_ready, 1)
            v.tensor_copy(kz[64:128, 1, CHUNK:CHUNK + S], kz[0:64, 0, CHUNK:CHUNK + S]).then_inc(kz_ready, 1)
            v.tensor_copy(kz[0:64, 2, CHUNK:CHUNK + S], kz[64:128, 3, CHUNK:CHUNK + S]).then_inc(kz_ready, 1)
            v.wait_ge(proj_done, T_V + 1)
            for m in range(TH):
                v.tensor_tensor(v_tok[:, m, :], proj[T_V % 2][:, P * m:P * m + P], bv_b[:, :], ALU.add)\
                 .then_inc(v_evac, 1)
            v.tensor_tensor(v_prev[:, :], bank[2][0:CHUNK, 0:P], bv_b[0:CHUNK, :], ALU.add).then_inc(v_evac, 1)

            for k in range(KT):
                v.wait_ge(proj_evac, T_X + k)
                tap = lambda j: (page_x[:, k, j:j + S], cols[:, C_WCONV + 8 * j + k:C_WCONV + 8 * j + k + 1])
                src, wj = tap(0)
                link(v.tensor_scalar(xcT[:, k, :], src, wj, cols[:, C_BCONV + k:C_BCONV + k + 1], ALU.mult, ALU.add))
                for j in (1, 2, 3):
                    src, wj = tap(j)
                    ins = stt(out=xcT[:, k, :], in0=src, scalar=wj, in1=xcT[:, k, :], op0=ALU.mult, op1=ALU.add)
                    if j < 3:
                        link(ins)
                    else:
                        ins.then_inc(xc_ready, 1)

            def soften(h):
                b = h % 2
                v.wait_ge(s_done, h + 1)
                if h >= 2:
                    v.wait_ge(pt_done, h - 1)
                link(stt(out=sc[:, b, :, :].rearrange("p m k -> p (m k)"),
                         in0=dist[:, :, :].rearrange("p m k -> p (m k)"), scalar=NEG_SLOPE8[h],
                         in1=bank[2][:, 0:TH * KEYS], op0=ALU.mult, op1=ALU.add))
                link(v.tensor_reduce(soft[:, b, 0, :], sc[:, b, :, :], AX, ALU.max))
                link(v.tensor_scalar(soft[:, b, 1, :], soft[:, b, 0, :], sink8[:, h:h + 1], -0.125, ALU.max, ALU.mult))
                v.tensor_scalar(soft[:, b, 6, :], soft[:, b, 1, :], sinks_b[:, h:h + 1], None, ALU.add)\
                 .then_inc(negm_ready, 1)

            def normalise(h):
                b = h % 2
                v.wait_ge(exp_done, 3 * h + 3)
                link(v.tensor_tensor(soft[:, b, 4, :], soft[:, b, 2, :], soft[:, b, 3, :], ALU.add))
                link(v.reciprocal(soft[:, b, 5, :], soft[:, b, 4, :]))
                for m in range(TH):
                    ins = v.tensor_scalar(sc[:, b, m, :], sc[:, b, m, :], soft[:, b, 5, m:m + 1], None, ALU.mult)
                    if m == 0:
                        link(ins)
                    else:
                        ins.then_inc(p_ready, 1)

            for h in range(HEADS + 1):
                if h < HEADS:
                    soften(h)
                if h >= 1:
                    normalise(h - 1)

            v.wait_ge(ri_ready, 2 * KT)
            for half in range(2):
                ks = slice(4 * half, 4 * half + 4)
                la, e, zz, ii, xx = rT[:, ks, :], eT[:, ks, :], zT[:, ks, :], iT[:, ks, :], xcT[:, ks, :]
                v.tensor_tensor(la, la, neg8sp[:, ks].rearrange("p (k o) -> p k o", o=1).to_broadcast([P, 4, S]),
                                ALU.mult).then_inc(log_a, 1)
                v.wait_ge(log_a, half + 1)
                yy = page_x[:, ks, 3:3 + S]
                v.wait_ge(proj_evac, T_G)
                link(v.tensor_scalar(yy, la, 0.125, None, ALU.mult))
                link(v.tensor_scalar(e, yy, 1.0 / 120, None, ALU.mult))
                for coef in (1.0 / 24, 1.0 / 6, 0.5, 1.0):
                    link(stt(out=e, in0=e, scalar=coef, in1=yy, op0=ALU.add, op1=ALU.mult))
                for _ in range(3):
                    link(stt(out=e, in0=e, scalar=2.0, in1=e, op0=ALU.add, op1=ALU.mult))
                v.wait_ge(a_tab, half + 1)
                link(v.tensor_scalar(zz, zz, -1.0, None, ALU.add))
                link(v.tensor_scalar(la, la, LRU_SMALL, None, ALU.is_lt))
                link(v.copy_predicated(e, la.bitcast(I32), zz))
                v.tensor_scalar(la, e, 2.0, None, ALU.add).then_inc(v_chain, 1)
                done[0] += 1
                v.wait_ge(v_chain, done[0])
                v.tensor_tensor(zz, la, e, ALU.mult).then_inc(lru_w, 1)
                link(v.tensor_tensor(ii, ii, xx, ALU.mult))
                link(v.tensor_scalar(e, e, 1.0, None, ALU.add))
                v.wait_ge(lru_root, half + 1)
                link(v.tensor_tensor(ii, ii, zz, ALU.mult))
                for k in range(4 * half, 4 * half + 4):
                    link(v.tensor_tensor_scan(hT[:, k, :], eT[:, k, :], iT[:, k, :], 0.0, ALU.mult, ALU.add))
                ins = v.tensor_tensor(geluT[:, ks, :], geluT[:, ks, :], hT[:, ks, :], ALU.mult)
                if half == 0:
                    v.wait_ge(proj_evac, T_GA - 1)
                    link(ins)
                else:
                    ins.then_inc(hg_ready, 1)
            v.wait_ge(load_used, in_load(RIDE + 3) + 2)
            mod_group(1, bank[7][:, :])
            v.wait_ge(load_used, in_load(RIDE + 7) + 2)
            mod_group(2, bank[6][:, :])
            v.wait_ge(proj_evac, T_END - 1)
            v.wait_ge(br_evac, KT)
            link(v.tensor_tensor(gaT, gaT, qT, ALU.mult))
            for q in range(KT, 2 * KT):
                v.wait_ge(br_done, q + 1)
                d = q - KT
                v.tensor_tensor(glT[:, d, :], glT[:, d, :], proj[q % 2], ALU.mult).then_inc(br_evac, 1)
                v.wait_ge(br_evac, q + 1)
                v.tensor_tensor(glT[:, d, :], glT[:, d, :], gaT[:, d, :], ALU.add).then_inc(merged, 1)
            v.wait_ge(mod_vec, 3)
            v.wait_ge(b_up_in, 16)
            for j in range(3):
                part = b_up_parts[E * j:E * j + E, :]
                if j < 2:
                    link(v.tensor_copy(part, b_up_raw))
                    link(v.tensor_tensor(b_up_raw, b_up_raw, part, ALU.subtract))
                else:
                    v.tensor_copy(part, b_up_raw).then_inc(b_up_ready, 1)

            v.wait_ge(spread_copied, 8)
            for h in range(TH):
                c0 = 4 + 6 * h
                v.wait_ge(sq1_ready, 2 * h + 2)
                v.tensor_tensor(stat[:, c0 + 2:c0 + 3], stat[:, c0:c0 + 1], stat[:, c0 + 1:c0 + 2], ALU.add)\
                 .then_inc(sum_ready, 1)
                rstd(2 * h + 2, c0 + 3)
                for cc in range(2):
                    part = slice(512 * cc, 512 * cc + 512)
                    link(stt(out=scrap[:, h, part], in0=bank[2 * h + cc][:, :], scalar=stat[:, c0 + 3:c0 + 4],
                             in1=gate1_b[:, part], op0=ALU.mult, op1=ALU.mult))
                v.tensor_tensor(x_tok[:, h, :], x_tok[:, h, :], scrap[:, h, :], ALU.add).then_inc(x1_ready, 1)
                rstd(2 * h + 3, c0 + 5)
                link(stt(out=u2[:, h, :], in0=x_tok[:, h, :], scalar=stat[:, c0 + 5:c0 + 6], in1=scale2_b,
                         op0=ALU.mult, op1=ALU.mult))
                v.tensor_tensor(u2[:, h, :], u2[:, h, :], shift2_b, ALU.add).then_inc(u2_ready, 1)
                v.wait_ge(u2T_done, h + 1)
                v.tensor_copy(u2T[:, 4:8, P * h:P * h + P], bank[5 + 2 * h][:, :].rearrange("p (k t) -> p k t", t=P))\
                 .then_inc(u2T_ready, 1)

            both = lambda col: col.to_broadcast([P, TH, E])
            v.wait_ge(lg_done, 1)
            link(v.tensor_tensor(lg, bank[0][:, 0:TH * E].rearrange("p (h e) -> p h e", h=TH),
                                 b_router_b[:, :].rearrange("p (o e) -> p o e", o=1).to_broadcast([P, TH, E]), ALU.add))
            for h in range(TH):
                link(v.max(top8[:, h, :], lg[:, h, :]))
            v.tensor_scalar(allow[:, :, 2], top8[:, :, 0], -1.0, None, ALU.mult).then_inc(top_ready, 1)
            link(v.tensor_tensor(gt, lg, both(top8[:, :, TOPK - 1:TOPK]), ALU.is_gt))
            link(v.tensor_tensor(eq, lg, both(top8[:, :, TOPK - 1:TOPK]), ALU.is_equal))
            link(v.tensor_reduce(allow[:, :, 0], gt, AX, ALU.add))
            for h in range(TH):
                link(v.tensor_tensor_scan(eq_n[:, h, :], ones[:, 0:E], eq[:, h, :], allow[:, h, 0:1],
                                          ALU.mult, ALU.add))
            link(stt(out=eq, in0=eq_n, scalar=float(TOPK), in1=eq, op0=ALU.is_le, op1=ALU.mult))
            v.tensor_tensor(mask, gt, eq, ALU.add).then_inc(mask_ready, 1)
            v.wait_ge(mask_ready, 1)
            v.wait_ge(gexp_ready, TH)
            link(v.tensor_tensor(gate[:, :, :], gate[:, :, :], mask[:, :, :], ALU.mult))
            link(v.tensor_reduce(allow[:, :, 0], gate[:, :, :], AX, ALU.add))
            link(v.reciprocal(allow[:, :, 1], allow[:, :, 0]))
            v.tensor_tensor(gate, gate, both(allow[:, :, 1:2]), ALU.mult).then_inc(posm_ready, 1)
            v.wait_ge(pos_done, 1)
            flat = lambda t: t[:, :, :].rearrange("p h e -> p (h e)")
            link(stt(out=flat(posm), in0=bank[1][:, 0:2 * E], scalar=BIG, in1=flat(mask), op0=ALU.add, op1=ALU.mult))
            v.tensor_scalar(flat(posm), flat(posm), -BIG, None, ALU.add).then_inc(posm_ready, 1)
            link(v.tensor_copy(blocks[:, 4:6], bank[2][0:E, 0:2]))
            link(v.tensor_scalar(blocks[:, 0:2], blocks[:, 4:6], float(CAP), 1.0, ALU.is_gt, ALU.add))
            link(stt(out=blocks[:, 0:2], in0=blocks[:, 4:6], scalar=2.0 * CAP, in1=blocks[:, 0:2],
                     op0=ALU.is_gt, op1=ALU.add))
            stt(out=blocks[:, 0:2], in0=blocks[:, 4:6], scalar=3.0 * CAP, in1=blocks[:, 0:2],
                op0=ALU.is_gt, op1=ALU.add).then_inc(blocks_ready, 1)
            v.wait_ge(blocks_ready, 1)
            v.wait_ge(posT_done, 1)
            v.tensor_copy(posT[:, :], bank[3][0:E, 0:S]).then_inc(posT_ready, 1)
            v.tensor_copy(gateT[:, :], bank[3][0:E, S:2 * S]).then_inc(posT_ready, 1)
            v.wait_ge(cum_done, 1)
            link(v.tensor_copy(blocks[:, 2:4], bank[2][0:E, 4:6]))
            link(v.tensor_tensor(blocks[:, 6:8], blocks[:, 2:4], blocks[:, 0:2], ALU.add))
            v.wait_ge(numbers, 1)
            link(v.tensor_scalar(item_t[:, 0, :], iota_n[:, :], blocks[:, 2:3], None, ALU.is_ge))
            link(v.tensor_scalar(item_t[:, 1, :], iota_n[:, :], blocks[:, 6:7], None, ALU.is_lt))
            for j in range(3):
                link(v.tensor_tensor(item_sel[E * j:E * j + E, :], item_t[:, 0, :], item_t[:, 1, :], ALU.mult))
            link(v.tensor_scalar(item_t[:, 0, :], iota_n[:, :], blocks[:, 2:3], -float(CAP), ALU.subtract, ALU.mult))
            stt(out=item_off[:, :], in0=item_t[:, 0, :], scalar=BIG, in1=item_sel[0:E, :],
                op0=ALU.add, op1=ALU.mult).then_inc(sel_ready, 1)
            v.wait_ge(item_done, 1)
            link(v.tensor_scalar(pos_item[:, :, :].rearrange("p h i -> p (h i)"), bank[1][:, 64:64 + TH * ITEMS],
                                 -BIG, None, ALU.add))
            link(v.tensor_copy(gate_item[:, :, :].rearrange("p h i -> p (h i)"), bank[1][:, 160:160 + TH * ITEMS]))
            link(v.tensor_copy(tab[:, 0:E + 2], bank[2][0:1, 8:8 + E + 2]))
            v.tensor_copy(tab[:, 48:96], bank[2][0:1, 64:64 + ITEMS]).then_inc(tab_ready, 1)
            v.wait_ge(yinit_done, 1)
            for h in range(TH):
                for cc in range(2):
                    v.tensor_copy(y_acc[:, h, 512 * cc:512 * cc + 512], bank[4 + 2 * h + cc][:, :])\
                     .then_inc(yinit_ready, 1)
            v.memset(rows, 0.0).then_inc(rows_ready, 1)
            v.memset(ohgT, 0.0).then_inc(ohgT_ready, 1)
            v.wait_ge(yinit_ready, 4)
            v.memset(lin[:, 0:1], 0.0).then_inc(y_added, 1)
            v.wait_ge(tab_ready, 1)
            v.wait_ge(y_added, 1)
            n_items = v.value_load(tab[0:1, E:E + 1], min_val=E, max_val=ITEMS - 1)

            def add_half(h, n):
                v.wait_ge(comb_done, n)
                for cc in range(2):
                    part = y_acc[:, h, 512 * cc:512 * cc + 512]
                    ins = v.tensor_tensor(part, part, bank[6 + cc][:, :], ALU.add)
                return ins

            def same_slot(dst, width, i):
                return v.tensor_tensor(dst, iota_s[:, :, 0:width],
                                       pos_item[:, :, bass.ds(i, 1)].to_broadcast([P, TH, width]), ALU.is_equal)

            same_slot(oh, CAP, 0).then_inc(oh_ready, 1)
            v.wait_ge(xgT_done, 1)
            v.tensor_copy(xgT_flat, bank[2][:, :]).then_inc(xg_ready, 1)
            two = lambda b, o: b[:, o:512:2]
            with v.Fori(0, n_items) as i:
                same_slot(oh, CAP, i + 1).then_inc(oh_ready, 1)
                same_slot(ohg_h, P, i).then_inc(ohg_half, 1)
                v.wait_ge(ohg_half, i + 1)
                v.tensor_tensor(ohg, ohg_h, gate_item[:, :, bass.ds(i, 1)].to_broadcast([P, TH, P]), ALU.mult)\
                 .then_inc(ohg_ready, 1)
                v.wait_ge(slot_used[7], i + 1)
                for b in range(2):
                    ins = v.tensor_scalar(glu[:, 256 * b:256 * b + 256], two(bank[b], 0), LIMIT, None, ALU.min)
                ins.then_inc(glu_ready, 1)
                for b in range(2):
                    ins = v.tensor_scalar(lin[:, 256 * b:256 * b + 256], two(bank[b], 1), LIMIT, -LIMIT,
                                          ALU.min, ALU.max)
                ins.then_inc(lin_ready, 1)
                v.wait_ge(glu_ready, i + 1)
                v.wait_ge(lin_ready, i + 1)
                stt(out=lin, in0=lin, scalar=1.0, in1=glu, op0=ALU.add, op1=ALU.mult).then_inc(gl_ready, 1)
                v.wait_ge(gl_ready, i + 1)
                v.wait_ge(sig_ready, i + 1)
                v.tensor_tensor(act_sb, lin, sig, ALU.mult).then_inc(act_ready, 1)
                for h in range(TH):
                    add_half(h, 2 * i + h + 1).then_inc(y_added, 1)
                v.wait_ge(ohgT_done, i + 1)
                v.tensor_copy(ohgT, bank[5][:, 0:S]).then_inc(ohgT_ready, 1)
                v.wait_ge(xgT_done, i + 2)
                v.tensor_copy(xgT_flat, bank[2][:, :]).then_inc(xg_ready, 1)
            for h in range(TH):
                add_half(h, 2 * n_items + h + 1).then_inc(yacc_done, 1)
            for h in range(TH):
                rstd(6 + h, 17 + 2 * h)
                link(stt(out=y_acc[:, h, :], in0=y_acc[:, h, :], scalar=stat[:, 17 + 2 * h:18 + 2 * h], in1=gate2_b,
                         op0=ALU.mult, op1=ALU.mult))
                v.tensor_tensor(x_tok[:, h, :], x_tok[:, h, :], y_acc[:, h, :], ALU.add).then_inc(x1_ready, 1)


_INS = ["x", "c", "w_ada", "b_ada", "g_pre_mix", "g_post_mix", "w_in", "b_in", "w_conv", "b_conv", "w_rg_a", "b_rg_a",
        "w_rg_x", "b_rg_x", "lru_lambda", "attn_sinks", "w_br_attn", "w_br_lru", "w_mix_out", "g_pre_moe",
        "g_post_moe", "w_router", "b_router", "w_up", "b_up", "w_down", "b_down"]
_OUTS = [((1, S, D), "float32")]


def kernel(**inputs):
    import numpy as _np
    import concourse.bacc as _bacc
    from concourse import mybir as _mybir
    from concourse.bass_utils import run_bass_kernel_spmd as _run

    nc = _bacc.Bacc("TRN2", target_bir_lowering=False, num_devices=1)
    arrays, args = {}, []
    for name in _INS:
        a = _np.ascontiguousarray(inputs[name])
        arrays[f"in_{name}_dram"] = a
        args.append(nc.dram_tensor(f"in_{name}_dram", a.shape, _mybir.dt.from_np(a.dtype), kind="ExternalInput").ap())
    for i, (shape, dtype) in enumerate(_OUTS):
        dt = _mybir.dt.from_np(_np.dtype(dtype))
        args.append(nc.dram_tensor(f"out_{i}_dram", shape, dt, kind="ExternalOutput").ap())
    hybrid_block(nc, *args)
    r = _run(nc, [arrays], core_ids=[0])
    return r.results[0]["out_0_dram"]
```

```python
from contextlib import ExitStack

import concourse.bass as bass
from concourse import mybir

F32 = mybir.dt.float32
BF16 = mybir.dt.bfloat16
I32 = mybir.dt.int32
ALU = mybir.AluOpType
ACT = mybir.ActivationFunctionType
AX = mybir.AxisListType.X

P = 128
D = 1024
KT = D // P
S = 256
TH = S // P
HEADS, HD, CHUNK = 16, 64, 64
KEYS = 3 * CHUNK
E = 32
TOPK = 4
CAP = 64
ITEMS = 48
EPS = 1e-6
ALPHA, LIMIT = 1.702, 7.0
MASKED = 1e30
BIG = 8192.0
NEG_SLOPE8 = [-8.0 * 2.0 ** (-8.0 * (h + 1) / HEADS) for h in range(HEADS)]

T_K, T_V, T_X, T_G, T_GA, T_GL, T_END = 8, 9, 10, 18, 26, 34, 42
C_BIN, C_BCONV, C_WCONV, C_BA, C_BX, C_LAM, C_END = 0, 42, 50, 82, 90, 98, 106
L_ADA0, L_IN, L_ATTN, L_LRU, L_MIX, L_END = 0, 4, 23, 25, 27, 29
IN_GROUPS = 11
RIDE = 3
BAYS = 4
SLOTS = 16
GROUPS = SLOTS // 4
T_S, T_PT, T_PV, T_RI = 18, 20, 21, 20
SPREAD = 5
LRU_SMALL = -0.85


def hybrid_block(nc, x, c, w_ada, b_ada, g_pre_mix, g_post_mix, w_in, b_in, w_conv, b_conv, w_rg_a, b_rg_a,
                 w_rg_x, b_rg_x, lru_lambda, attn_sinks, w_br_attn, w_br_lru, w_mix_out, g_pre_moe, g_post_moe,
                 w_router, b_router, w_up, b_up, w_down, b_down, out):
    with ExitStack() as ctx:
        def sb(name, shape, dt=F32):
            return ctx.enter_context(nc.sbuf_tensor(name, shape, dt))

        def sem(name):
            return ctx.enter_context(nc.semaphore(name))

        ring = sb("ring", [P, SLOTS, 2048])
        bay = [ring[:, 2 * b:2 * b + 2, :].rearrange("p s n -> p (s n)") for b in range(BAYS)]
        xcT, rT, iT, eT = [ring[:, 8 + j, :].rearrange("p (k t) -> p k t", k=KT) for j in range(4)]

        x_tok = sb("x_tok", [P, TH, D])
        page_u = ring[:, 12, :]
        page_q = sb("page_q", [P, 2048])
        page_x = sb("page_x", [P, KT, 3 + S])
        page_g = sb("page_g", [P, 2048])
        page_ga = ring[:, 13, :]
        page_gl = ring[:, 14, :]
        page_a = ring[:, 15, :]
        page_n = sb("page_n", [P, 2048])
        tiles = lambda page: page[:, :].rearrange("p (k t) -> p k t", k=KT)
        halves = lambda page: page[:, :].rearrange("p (h d) -> p h d", h=TH)
        uT, qT, geluT, gaT, glT, attnT = map(tiles, (page_u, page_q, page_g, page_ga, page_gl, page_a))
        zT = tiles(page_n)
        xn = halves(page_n)
        hT = page_x[:, :, 3:3 + S]
        y_acc, u2 = halves(page_q), halves(page_g)
        u2T = tiles(page_u)
        scale2_b, shift2_b = page_a[:, 0:D], page_a[:, D:2 * D]
        gate1_b, gate2_b = page_n[:, 0:D], page_n[:, D:2 * D]
        b_up_raw = page_u[0:E, :]

        ident = sb("ident", [P, P])
        before = sb("before", [P, P])
        ones = sb("ones", [P, P])
        bd_a = sb("bd_a", [P, KT, P])
        bd_x = sb("bd_x", [P, KT, P])
        vec_rows = page_a[0:C_END, 512:512 + P]
        cols = sb("cols", [P, C_END])
        c_col = sb("c_col", [P, KT])
        c_sig = sb("c_sig", [P, KT])
        c_act = sb("c_act", [P, KT])
        c_rep = sb("c_rep", [P, KT, 32])
        mod_add = sb("mod_add", [P, 3, 512])
        mod_mul = sb("mod_mul", [P, 3, 512])
        mod_one = sb("mod_one", [P, 3])
        ab = sb("ab", [P, 16])
        stat = sb("stat", [P, 20])
        eps = sb("eps", [P, 1])
        kz = sb("kz", [P, 4, CHUNK + S])
        v_tok = sb("v_tok", [P, TH, P])
        v_prev = sb("v_prev", [CHUNK, P])
        bv_b = sb("bv_b", [P, P])
        sinks_b = sb("sinks_b", [P, HEADS])
        sink8 = sb("sink8", [P, HEADS])
        dist_i = page_a[:, 0:TH * KEYS].bitcast(I32).rearrange("p (h k) -> p h k", h=TH)
        dist = sb("dist", [P, TH, KEYS])
        sc = sb("sc", [P, 2, TH, KEYS])
        soft = sb("soft", [P, 2, 8, TH])
        pT = sb("pT", [P, 2, 3, P])
        neg8sp = sb("neg8sp", [P, KT])
        sp_t = sb("sp_t", [P, 6, KT])
        def carve(flat):
            at = [0]

            def take(*shape, rows=P, dt=F32):
                n = 1
                for w in shape:
                    n *= w
                part = flat[0:rows, at[0]:at[0] + n]
                at[0] += n
                assert at[0] <= flat.shape[1]
                if dt != F32:
                    part = part.bitcast(dt)
                return part.rearrange("p (a b) -> p a b", a=shape[0]) if len(shape) == 2 else part
            return take

        of_x = carve(page_x[:, :, :].rearrange("p k t -> p (k t)"))
        of_kz = carve(kz[:, :, :].rearrange("p k t -> p (k t)"))
        of_ga = carve(page_ga[:, :])
        of_sc = carve(sc[:, :, :, :].rearrange("p a b c -> p (a b c)"))
        w_router_sb = of_x(KT, E)
        b_down_sb = of_x(D, rows=E)
        lg, gt, eq, eq_n, mask, gate, posm = (of_x(TH, E) for _ in range(7))
        top8 = of_x(TH, 8)
        allow = of_x(TH, 4)
        b_router_b = sb("b_router_b", [P, E])
        posT = of_kz(S, rows=E)
        iota_i = of_kz(TH, P, dt=I32)
        iota_s = of_kz(TH, P)
        iota_n = of_kz(ITEMS, rows=E)
        item_t = of_kz(2, ITEMS, rows=E)
        key_row = of_ga(E, rows=E)
        key_col = of_ga(2, rows=E)
        place_of = of_ga(E, rows=E)
        wraps = of_ga(E, rows=E)
        expert_id = of_ga(2, rows=E)
        keys = of_ga(E, rows=E)
        rank_t = of_ga(E, rows=E)
        rank_hot = of_ga(E, rows=E)
        at_place = of_ga(E + 2, rows=E)
        ahead_of = of_ga(E + 2, rows=E)
        ahead_t = of_ga(E, rows=E)
        place = of_ga(4, rows=E)
        blocks_b = of_ga(E, rows=E)
        blocks = sb("blocks", [E, 8])
        item_sel = sb("item_sel", [3 * E, ITEMS])
        item_off = of_kz(ITEMS, rows=E)
        pos_item = sb("pos_item", [P, TH, ITEMS])
        gate_item = sb("gate_item", [P, TH, ITEMS])
        T_ID = E + 2
        tab = cols[0:1, 0:T_ID + E].bitcast(I32)
        oh = of_sc(TH, CAP)
        ohg = of_sc(TH, P)
        ohg_h = of_sc(TH, P)
        bsel = of_sc(CAP // 2, rows=3 * E, dt=BF16)
        xgT_flat = bd_a[:, 0:4, :].rearrange("p a b -> p (a b)")
        xgT = xgT_flat.rearrange("p (b j s) -> p b j s", b=4, j=2)
        actT = bd_a[:, 4:8, :].rearrange("p a b -> p (a b)")
        glu = bd_x[:, 0:4, :].rearrange("p a b -> p (a b)")
        lin = bd_x[:, 4:8, :].rearrange("p a b -> p (a b)")
        sig = mod_add[:, 0, :]
        act_sb = mod_add[:, 1, :]
        pair_rows = [mod_add[:, 2, :], page_n[:, 512:1024]]
        pair_hot = [mod_mul[:, 0, 0:S], mod_mul[:, 0, S:2 * S]]
        rows = pT[:, :, :, :].rearrange("p a b c -> p (a b c)")[:, 0:512]
        ohgT = of_kz(S)
        gateT = pair_hot[1][0:E, :]
        b_up_parts = mod_mul[0:3 * E, 1:3, :].rearrange("p a b -> p (a b)").bitcast(BF16)
        act_kept = page_x[:, :, :].rearrange("p k t -> p (k t)")[:, 0:2048].rearrange("p (b n) -> p b n", b=4)
        xg_tok = page_n[:, 0:512]
        scrap = halves(page_q)

        bank = [ctx.enter_context(nc.psum_tensor(f"bank{i}", [P, 512], F32)) for i in range(8)]
        proj = [bank[j][:, 0:256] for j in range(2)]

        small_in = sem("small_in")
        late_in = sem("late_in")
        x_in = sem("x_in")
        c_in = sem("c_in")
        bay_in = [sem(f"bay_in{b}") for b in range(BAYS)]
        load_used = sem("load_used")
        consts = sem("consts")
        g_chain = sem("g_chain")
        v_chain = sem("v_chain")
        route_in = sem("route_in")
        numbers = sem("numbers")
        c_ready = sem("c_ready")
        csig_ready = sem("csig_ready")
        xn_ready = sem("xn_ready")
        sq_ready = sem("sq_ready")
        eps_ready = sem("eps_ready")
        root_ready = sem("root_ready")
        xT_done = sem("xT_done")
        cols_ps = sem("cols_ps")
        cols_ready = sem("cols_ready")
        mod_vec = sem("mod_vec")
        ab_ps = sem("ab_ps")
        ab_ready = sem("ab_ready")
        uT_ready = sem("uT_ready")
        uT_ready_v = sem("uT_ready_v")
        proj_done = sem("proj_done")
        proj_evac = sem("proj_evac")
        v_evac = sem("v_evac")
        kz_ready = sem("kz_ready")
        s_done = sem("s_done")
        negm_ready = sem("negm_ready")
        exp_done = sem("exp_done")
        p_ready = sem("p_ready")
        pt_done = sem("pt_done")
        pt_ready = sem("pt_ready")
        pv_done = sem("pv_done")
        attn_ready = sem("attn_ready")
        xc_ready = sem("xc_ready")
        ri_done = sem("ri_done")
        ri_ready = sem("ri_ready")
        lam_exp = sem("lam_exp")
        lam_in = sem("lam_in")
        log_a = sem("log_a")
        a_tab = sem("a_tab")
        lru_w = sem("lru_w")
        lru_root = sem("lru_root")
        hg_ready = sem("hg_ready")
        br_done = sem("br_done")
        br_evac = sem("br_evac")
        merged = sem("merged")
        mix_done = sem("mix_done")
        sum_ready = sem("sum_ready")
        spread_done = sem("spread_done")
        spread_copied = sem("spread_copied")
        sq1_ready = sem("sq1_ready")
        sq2_ready = sem("sq2_ready")
        x1_ready = sem("x1_ready")
        sq3_ready = sem("sq3_ready")
        yacc_done = sem("yacc_done")
        u2_ready = sem("u2_ready")
        u2T_done = sem("u2T_done")
        u2T_ready = sem("u2T_ready")
        lg_done = sem("lg_done")
        top_ready = sem("top_ready")
        gexp_ready = sem("gexp_ready")
        mask_ready = sem("mask_ready")
        pos_done = sem("pos_done")
        posm_ready = sem("posm_ready")
        posT_done = sem("posT_done")
        posT_ready = sem("posT_ready")
        blocks_ready = sem("blocks_ready")
        cum_done = sem("cum_done")
        sel_ready = sem("sel_ready")
        item_done = sem("item_done")
        tab_ready = sem("tab_ready")
        b_up_in = sem("b_up_in")
        b_up_ready = sem("b_up_ready")
        out_scaled = sem("out_scaled")
        out_ready = [sem(f"out_ready{h}") for h in range(TH)]
        hot_zeroed = sem("hot_zeroed")
        w_slot = [sem(f"w_slot{k}") for k in range(12)]
        slot_used = [sem(f"slot_used{k}") for k in range(12)]
        oh_ready = sem("oh_ready")
        ohg_half = sem("ohg_half")
        ohg_ready = sem("ohg_ready")
        bsel_ready = sem("bsel_ready")
        act_stored = sem("act_stored")
        gather_done = sem("gather_done")
        xg_copied = sem("xg_copied")
        xgT_done = sem("xgT_done")
        xg_ready = sem("xg_ready")
        ohgT_done = sem("ohgT_done")
        ohgT_ready = sem("ohgT_ready")
        glu_ready = sem("glu_ready")
        lin_ready = sem("lin_ready")
        gl_ready = sem("gl_ready")
        sig_ready = sem("sig_ready")
        act_ready = sem("act_ready")
        actT_done = sem("actT_done")
        actT_ready = sem("actT_ready")
        rows_ready = sem("rows_ready")
        comb_done = sem("comb_done")
        y_added = sem("y_added")
        out_done = sem("out_done")

        x_v = x.rearrange("b (h p) d -> (b p) h d", p=P)
        out_v = out.rearrange("b (h p) d -> (b p) h d", p=P)
        ada_v = w_ada.rearrange("l (p k) (m n) -> (l m) p k n", k=KT, m=3)
        in_v = w_in.rearrange("l (k p) n -> (l p) k n", p=P)
        square_v = {n: w.rearrange("l (k p) (c n) -> (l c) p k n", p=P, c=2)
                    for n, w in (("attn", w_br_attn), ("lru", w_br_lru), ("mix", w_mix_out))}
        up_v = w_up.rearrange("l e (k p) f -> (l e) p k f", p=P)
        down_v = w_down.rearrange("l e (q a p) f -> (l e) p q a f", p=P, a=2)
        row = lambda v: v.rearrange("l (k p) -> (l k) p", p=P)

        def loads():
            res = []

            def ada(m, b):
                res.append((bay[len(res) % BAYS].rearrange("p (k n) -> p k n", k=2), ada_v[m, :, 2 * b:2 * b + 2, :]))

            for b in range(4):
                ada(0, b)
            for g in range(IN_GROUPS):
                w = min(512, T_END * P - 512 * g)
                dst = bay[len(res) % BAYS].rearrange("p (k n) -> p k n", k=KT)[:, :, 0:w]
                res.append((dst, in_v[:, :, 512 * g:512 * g + w]))
                if g >= RIDE:
                    ada(1 + (g - RIDE) // 4, (g - RIDE) % 4)
            for n in ("attn", "lru", "mix"):
                for half in range(2):
                    res.append((bay[len(res) % BAYS].rearrange("p (k n) -> p k n", k=KT), square_v[n][half]))
            return res

        def in_load(g):
            return L_IN + g + max(0, g - RIDE)

        def items_at(engine, p):
            return (engine.value_load(tab[0:1, bass.ds(p, 1)], min_val=0, max_val=ITEMS - 2),
                    engine.value_load(tab[0:1, bass.ds(p + 1, 1)], min_val=1, max_val=ITEMS - 1))

        def group(p, r):
            return ((3 * p + r) & (GROUPS - 1)) * 4

        plan = loads()
        assert len(plan) == L_END
        block = ctx.enter_context(nc.Block())

        @block.sync
        def _(sp):
            sp.dma_start(c_col[:, :], c.rearrange("b (p k) -> (b p) k", k=KT)).then_inc(c_in, 16)
            sp.dma_start(x_tok[:, :, :], x_v).then_inc(x_in, 16)
            for n, (dst, src) in enumerate(plan):
                if n == 3:
                    sp.wait_ge(small_in, 16 * 9)
                if n >= BAYS:
                    sp.wait_ge(load_used, n - BAYS + 1)
                sp.dma_start(dst, src).then_inc(bay_in[n % BAYS], 16)
            for n in (1, 2, 3, 0):
                b = n
                last = max(q for q in range(L_END) if q % BAYS == b)
                sp.wait_ge(load_used, last + 1)
                for k in (2 * b, 2 * b + 1):
                    sp.dma_start(ring[:, k, :], up_v[0, :, k, :]).then_inc(w_slot[k], 16)
            sp.wait_ge(hg_ready, 1)
            for q in range(4):
                sp.dma_start(ring[:, 8 + q, :].rearrange("p (a f) -> p a f", a=2),
                             down_v[0, :, q, :, :]).then_inc(w_slot[8 + q], 16)
            sp.wait_ge(tab_ready, 1)
            def load_third(r, p, turn, ahead):
                e = sp.value_load(tab[0:1, bass.ds(p + T_ID, 1)], min_val=1, max_val=E - 1)
                for j in range(4):
                    k = 4 * r + j
                    sp.wait_ge(w_slot[k], 16 * p)
                    if ahead is not None:
                        sp.wait_ge(slot_used[(k - 4) % 12], ahead)
                    if r < 2:
                        src = up_v[bass.ds(e, 1), :, k, :].rearrange("e p f -> (e p) f")
                        dst = ring[:, group(turn, r) + j, :]
                    else:
                        src = down_v[bass.ds(e, 1), :, j, :, :].rearrange("e p a f -> (e p) a f")
                        dst = ring[:, group(turn, r) + j, :].rearrange("p (a f) -> p a f", a=2)
                    sp.dma_start(dst, src).then_inc(w_slot[k], 16)

            def load_step(p, turn, last=False):
                ahead = sp.value_load(tab[0:1, bass.ds(p, 1)], min_val=1, max_val=ITEMS)
                load_third(1, p, turn, ahead)
                load_third(2, p, turn, ahead)
                if not last:
                    load_third(0, p + 1, (turn + 1) % GROUPS, ahead)

            load_third(0, 1, 1, None)
            rounds = (E - 2) // GROUPS
            with sp.Fori(0, rounds) as turns:
                for j in range(1, GROUPS + 1):
                    load_step(GROUPS * turns + j, j % GROUPS)
            for p in range(GROUPS * rounds + 1, E):
                load_step(p, p % GROUPS, last=(p == E - 1))

        @block.gpsimd
        def _(g):
            done = [0]

            def link(ins):
                done[0] += 1
                ins.then_inc(g_chain, 1)
                g.wait_ge(g_chain, done[0])

            link(g.memset(ident[:, :], 0.0))
            g.affine_select(out=ident[:, :], in_=ident[:, :], compare_op=ALU.not_equal, fill=1.0, base=0,
                            pattern=[[-1, P]], channel_multiplier=1).then_inc(consts, 1)
            g.memset(ones[:, :], 1.0).then_inc(consts, 1)
            link(g.memset(mod_add[:, :, :], 0.0))
            link(g.memset(mod_mul[:, :, :], 1.0))
            g.dma_start(mod_add[0:P:32, :, :], b_ada.rearrange("l (m j n) -> (l j) m n", m=3, j=4)).then_inc(late_in, 16)
            for j, m, gain in ((2, 0, g_pre_mix), (0, 1, g_post_mix), (0, 2, g_pre_moe), (2, 2, g_post_moe)):
                g.dma_start(mod_mul[32 * j:32 * j + 33:32, m, :], gain.rearrange("l (a n) -> (l a) n", a=2))\
                 .then_inc(late_in, 16)
            link(g.memset(mod_one[:, :], 0.0))
            link(g.memset(mod_one[64:128, 0:1], 1.0))
            g.memset(mod_one[0:64, 2:3], 1.0).then_inc(consts, 1)
            for bd, w in ((bd_a, w_rg_a), (bd_x, w_rg_x)):
                link(g.memset(bd[:, :, :], 0.0))
                pair = w.rearrange("l (k two) i j -> two (l i) k j", two=2)
                for f in range(2):
                    g.dma_start(bd[64 * f:64 * f + 64, :, 64 * f:64 * f + 64], pair[f]).then_inc(late_in, 16)
            g.memset(kz[:, :, :], 0.0).then_inc(consts, 1)
            g.memset(page_x[:, :, 0:3], 0.0).then_inc(consts, 1)
            link(g.memset(before[:, :], 1.0))
            g.affine_select(out=before[:, :], in_=before[:, :], compare_op=ALU.is_gt, fill=0.0, base=0,
                            pattern=[[1, P]], channel_multiplier=-1).then_inc(consts, 1)
            link(g.iota(dist_i[:, :, :], pattern=[[0, TH], [-1, KEYS]], base=CHUNK, channel_multiplier=1))
            g.tensor_copy(dist[:, :, :], dist_i[:, :, :]).then_inc(consts, 1)
            g.memset(item_sel[:, :], 0.0).then_inc(consts, 1)

            g.wait_ge(attn_ready, HEADS // 2)
            link(g.iota(iota_i[:, :, :], pattern=[[0, TH], [0, 2], [1, CAP]], base=0, channel_multiplier=0))
            link(g.tensor_copy(iota_s[:, :, :], iota_i[:, :, :]))
            link(g.iota(iota_i[0:E, 0, 0:ITEMS], pattern=[[1, ITEMS]], base=0, channel_multiplier=0))
            link(g.tensor_copy(iota_n[:, :], iota_i[0:E, 0, 0:ITEMS]))
            g.wait_ge(merged, KT)
            for dst, n, pattern, base, per in ((key_row, E, [[-1, E]], E - 1, 0), (key_col[:, 0:1], 1, [[0, 1]], E - 1, -1),
                                               (place_of, E, [[SPREAD, E]], SPREAD, 0),
                                               (expert_id, 2, [[0, 2]], 0, 1)):
                link(g.iota(iota_i[0:E, 1, 0:n], pattern=pattern, base=base, channel_multiplier=per))
                link(g.tensor_copy(dst, iota_i[0:E, 1, 0:n]))
            link(g.memset(key_row[:, 0:1], -1e5))
            link(g.memset(key_col[:, 1:2], 1.0))
            link(g.memset(key_col[0:1, 1:2], 0.0))
            link(g.iota(iota_i[0:E, 1, 0:E], pattern=[[SPREAD, E]], base=SPREAD, channel_multiplier=0))
            link(g.tensor_copy(rank_t, iota_i[0:E, 1, 0:E]))
            for j in range(1, SPREAD * E // (E - 1) + 1):
                link(g.tensor_scalar(wraps, rank_t, float(j * (E - 1)), -float(E - 1), ALU.is_ge, ALU.mult))
                link(g.tensor_tensor(place_of, place_of, wraps, ALU.add))
            g.tensor_scalar(place_of, place_of, 1.0, None, ALU.add).then_inc(numbers, 1)
            g.wait_ge(mod_vec, 3)
            g.memset(mod_mul[:, 0, :], 0.0).then_inc(hot_zeroed, 1)
            g.wait_ge(spread_copied, 8)
            link(g.memset(pair_rows[0], 0.0))
            g.wait_ge(route_in, 32)
            link(g.tensor_copy(pair_rows[0][64:64 + E, :], b_down_sb[:, 0:512]))
            g.wait_ge(u2_ready, TH)
            link(g.memset(pair_rows[1], 0.0))
            g.tensor_copy(pair_rows[1][0:E, :], b_down_sb[:, 512:D]).then_inc(rows_ready, 1)
            g.wait_ge(rows_ready, 1)
            g.memset(y_acc, 0.0).then_inc(y_added, 1)
            g.wait_ge(y_added, 1)
            g.wait_ge(posT_ready, 2)
            g.tensor_copy(pair_hot[0][64:64 + E, :], gateT).then_inc(ohgT_ready, 1)
            g.wait_ge(ohgT_ready, 1)

            def pick_bias(i):
                return g.tensor_copy(bsel, item_sel[:, bass.ds(i, 1)].to_broadcast([3 * E, CAP]))

            g.wait_ge(tab_ready, 1)
            n_items = g.value_load(tab[0:1, E:E + 1], min_val=E, max_val=ITEMS - 1)
            pick_bias(0).then_inc(bsel_ready, 1)
            with g.Fori(0, n_items) as i:
                g.wait_ge(slot_used[7], i + 1)
                pick_bias(i + 1).then_inc(bsel_ready, 1)
            for h in range(TH):
                g.wait_ge(out_scaled, h + 1)
                g.tensor_tensor(x_tok[:, h, 0:384], x_tok[:, h, 0:384], y_acc[:, h, 0:384], ALU.add)\
                 .then_inc(out_ready[h], 1)

        @block.scalar
        def _(a):
            for r0, src in ((C_BIN, row(b_in)), (C_BCONV, row(b_conv)),
                            (C_WCONV, w_conv.rearrange("l j (k p) -> (l j k) p", p=P)),
                            (C_BA, b_rg_a.rearrange("l (k a) j -> (l k) (a j)", a=2)),
                            (C_BX, b_rg_x.rearrange("l (k a) j -> (l k) (a j)", a=2)), (C_LAM, row(lru_lambda))):
                a.dma_start(vec_rows[r0:r0 + src.shape[0], :], src).then_inc(small_in, 16)
            a.dma_start(bv_b[:, :], b_in[:, T_V * P:T_V * P + P].to_broadcast([P, P])).then_inc(small_in, 16)
            a.dma_start(sinks_b[:, :], attn_sinks.to_broadcast([P, HEADS])).then_inc(small_in, 16)
            a.dma_start(b_router_b[:, :], b_router.to_broadcast([P, E])).then_inc(small_in, 16)
            def root(src, dst, w=1):
                a.activation(stat[:, dst:dst + w], stat[:, src:src + w], ACT.Sqrt, scale=1.0 / D, bias=eps[:, :])\
                 .then_inc(root_ready, 1)

            a.wait_ge(eps_ready, 1)
            a.wait_ge(c_in, 16)
            a.activation(c_sig[:, :], c_col[:, :], ACT.Sigmoid).then_inc(csig_ready, 1)
            a.wait_ge(x_in, 16)
            for h in range(TH):
                a.activation(page_g[:, D * h:D * h + D], x_tok[:, h, :], ACT.Square,
                             accum_out=stat[:, h:h + 1]).then_inc(sq_ready, 1)
            a.wait_ge(sq_ready, TH)
            root(0, 2, TH)
            a.wait_ge(cols_ready, 1)
            a.wait_ge(lam_in, 1)
            a.activation(sp_t[:, 0, :], sp_t[:, 1, :], ACT.Exp).then_inc(lam_exp, 1)
            a.wait_ge(xT_done, 1)
            a.wait_ge(ab_ready, 1)
            for k in range(KT // 2):
                a.activation(uT[:, k, :], bank[4 + k // 2][:, 256 * (k % 2):256 * (k % 2) + 256], ACT.Identity,
                             bias=ab[:, k:k + 1], scale=ab[:, 8 + k:9 + k]).then_inc(uT_ready, 1)

            def evac(t):
                a.wait_ge(proj_done, t + 1)
                src, bias = proj[t % 2], cols[:, C_BIN + t:C_BIN + t + 1]
                if t < T_K:
                    ins = a.activation(qT[:, t, :], src, ACT.Identity, bias=bias)
                elif t == T_K:
                    a.wait_ge(consts, 8)
                    for f in range(2):
                        half = slice(64 * f, 64 * f + 64)
                        ins = a.activation(kz[half, 3 * f, CHUNK:CHUNK + S], src[half, :], ACT.Identity,
                                           bias=cols[half, C_BIN + t:C_BIN + t + 1])
                        if f == 0:
                            ins.then_inc(kz_ready, 1)
                elif t < T_G:
                    ins = a.activation(page_x[:, t - T_X, 3:3 + S], src, ACT.Identity, bias=bias)
                elif t < T_GA:
                    ins = a.activation(geluT[:, t - T_G, :], src, ACT.Gelu_apprx_tanh, bias=bias)
                elif t < T_GL:
                    ins = a.activation(gaT[:, t - T_GA, :], src, ACT.Sigmoid, bias=bias)
                else:
                    ins = a.activation(glT[:, t - T_GL, :], src, ACT.Sigmoid, bias=bias)
                ins.then_inc(proj_evac, 1)

            def evac_attn(tiles_d):
                for d in tiles_d:
                    a.wait_ge(br_done, d + 1)
                    a.activation(qT[:, d, :], proj[d % 2], ACT.Copy).then_inc(br_evac, 1)

            def lru_exp(half):
                ks = slice(4 * half, 4 * half + 4)
                a.wait_ge(log_a, half + 1)
                a.activation(zT[:, ks, :], rT[:, ks, :], ACT.Exp).then_inc(a_tab, 1)

            def lru_sqrt(half):
                ks = slice(4 * half, 4 * half + 4)
                a.wait_ge(lru_w, half + 1)
                a.activation(zT[:, ks, :], zT[:, ks, :], ACT.Sqrt, scale=-1.0).then_inc(lru_root, 1)

            for t in range(T_END):
                if t != T_V:
                    evac(t)
                if t == T_S + HEADS + 2:
                    lru_exp(0)
                if t == T_S + HEADS + 5:
                    lru_sqrt(0)
                h = t - T_S
                if 0 <= h < HEADS:
                    a.wait_ge(negm_ready, h + 1)
                    for m in range(TH):
                        a.activation(sc[:, h % 2, m, :], sc[:, h % 2, m, :], ACT.Exp, scale=0.125,
                                     bias=soft[:, h % 2, 1, m:m + 1], accum_out=soft[:, h % 2, 2, m:m + 1])\
                         .then_inc(exp_done, 1)
                    a.activation(soft[:, h % 2, 3, :], soft[:, h % 2, 6, :], ACT.Exp).then_inc(exp_done, 1)
                h = t - T_PT
                if 0 <= h < HEADS:
                    a.wait_ge(pt_done, h + 1)
                    a.activation(pT[:, h % 2, 0:2, :].rearrange("p a b -> p (a b)"), bank[3][:, 0:256],
                                 ACT.Copy).then_inc(pt_ready, 1)
                    a.activation(pT[0:CHUNK, h % 2, 2, :], bank[3][0:CHUNK, 256:384], ACT.Copy).then_inc(pt_ready, 1)
                h = t - T_PV
                if 0 <= h < HEADS and h % 2:
                    a.wait_ge(pv_done, h + 1)
                    a.activation(attnT[:, h // 2, :], bank[4][:, 0:256], ACT.Copy).then_inc(attn_ready, 1)
                k = t - T_RI
                if 0 <= k < KT:
                    a.wait_ge(ri_done, k + 1)
                    a.activation(rT[:, k, :], bank[5 + k % 2][:, 0:256], ACT.Sigmoid,
                                 bias=cols[:, C_BA + k:C_BA + k + 1]).then_inc(ri_ready, 1)
                    a.activation(iT[:, k, :], bank[5 + k % 2][:, 256:512], ACT.Sigmoid,
                                 bias=cols[:, C_BX + k:C_BX + k + 1]).then_inc(ri_ready, 1)
            lru_exp(1)
            evac_attn(range(2))
            lru_sqrt(1)
            a.wait_ge(proj_done, T_END)
            a.dma_start(b_up_raw, b_up.rearrange("l e f -> (l e) f")).then_inc(b_up_in, 16)
            evac_attn(range(2, KT))
            a.wait_ge(hg_ready, 1)
            a.dma_start(w_router_sb, w_router.rearrange("l (k p) e -> (l p) k e", p=P)).then_inc(route_in, 16)
            a.dma_start(b_down_sb, b_down.rearrange("l e d -> (l e) d")).then_inc(route_in, 16)

            for n, dst in enumerate((gate1_b, shift2_b, scale2_b, gate2_b)):
                a.wait_ge(spread_done, n // 2 + 1)
                for cc in range(2):
                    a.activation(dst[:, 512 * cc:512 * cc + 512], bank[2 + 2 * (n % 2) + cc][:, :], ACT.Copy)\
                     .then_inc(spread_copied, 1)
            for h in range(TH):
                c0 = 4 + 6 * h
                for cc in range(2):
                    a.wait_ge(mix_done, 2 * h + cc + 1)
                    a.activation(scrap[:, h, 512 * cc:512 * cc + 512], bank[2 * h + cc][:, :], ACT.Square,
                                 accum_out=stat[:, c0 + cc:c0 + cc + 1]).then_inc(sq1_ready, 1)
                a.wait_ge(sum_ready, h + 1)
                root(c0 + 2, c0 + 3)
                a.wait_ge(x1_ready, h + 1)
                a.activation(scrap[:, h, :], x_tok[:, h, :], ACT.Square,
                             accum_out=stat[:, c0 + 4:c0 + 5]).then_inc(sq2_ready, 1)
                a.wait_ge(sq2_ready, h + 1)
                root(c0 + 4, c0 + 5)
                a.wait_ge(u2T_done, h + 1)
                a.activation(u2T[:, 0:4, P * h:P * h + P], bank[4 + 2 * h][:, :].rearrange("p (k t) -> p k t", t=P),
                             ACT.Copy).then_inc(u2T_ready, 1)
            a.wait_ge(top_ready, 1)
            for h in range(TH):
                a.activation(gate[:, h, :], lg[:, h, :], ACT.Exp, bias=allow[:, h, 2:3]).then_inc(gexp_ready, 1)

            a.wait_ge(tab_ready, 1)
            a.wait_ge(gather_done, 1)
            a.activation(xg_tok, bank[2][:, :], ACT.Copy).then_inc(xg_copied, 1)

            def sigmoid(i):
                a.wait_ge(glu_ready, i + 1)
                a.activation(sig, glu, ACT.Sigmoid, scale=ALPHA).then_inc(sig_ready, 1)

            def copy_gathered(i):
                a.wait_ge(gather_done, i + 1)
                a.activation(xg_tok, bank[2][:, :], ACT.Copy).then_inc(xg_copied, 1)

            def copy_rows(i):
                a.wait_ge(slot_used[11], i + 1)
                a.activation(rows, bank[4][:, :], ACT.Copy).then_inc(rows_ready, 1)

            def expert(p, odd):
                first, end = items_at(a, p)
                sigmoid(first)
                copy_gathered(first + 1)
                a.wait_ge(actT_done, first + 1)
                a.activation(actT, bank[3][:, :], ACT.Copy).then_inc(actT_ready, 1)
                a.activation(c_act[:, 0:1], eps[:, 0:1], ACT.Copy).then_inc(act_stored, 1)
                with a.If(first + 1 < end):
                    with a.Fori(first + 1, end) as i:
                        sigmoid(i)
                        copy_gathered(i + 1)
                        a.wait_ge(actT_done, i + 1)
                        a.activation(act_kept[:, bass.ds(i & 3, 1), :],
                                     bank[3][:, :].rearrange("p (o n) -> p o n", o=1), ACT.Copy).then_inc(act_stored, 1)
                a.wait_ge(slot_used[11], first + 1)
                for g in range(2):
                    part = slice(64 * g, 64 * g + 64)
                    ins = a.activation(pair_rows[g ^ odd][part, :], bank[4][part, :], ACT.Copy)
                ins.then_inc(rows_ready, 1)
                with a.If(first + 1 < end):
                    with a.Fori(first + 1, end) as i:
                        a.wait_ge(act_stored, i + 1)
                        a.activation(actT[:, :].rearrange("p (o n) -> p o n", o=1), act_kept[:, bass.ds(i & 3, 1), :],
                                     ACT.Copy).then_inc(actT_ready, 1)
                        copy_rows(i)

            with a.Fori(0, E // 2) as pairs:
                for odd in range(2):
                    expert(2 * pairs + odd, odd)
            a.activation(c_sig[:, 0:1], eps[:, 0:1], ACT.Sqrt)
            for h in range(TH):
                a.wait_ge(yacc_done, h + 1)
                a.activation(u2[:, h, :], y_acc[:, h, :], ACT.Square,
                             accum_out=stat[:, 16 + 2 * h:17 + 2 * h]).then_inc(sq3_ready, 1)
                a.wait_ge(sq3_ready, h + 1)
                root(16 + 2 * h, 17 + 2 * h)
            for h in range(TH):
                a.wait_ge(out_ready[h], 2)
                a.dma_start(out_v[:, h, :], x_tok[:, h, :]).then_inc(out_done, 16)
            a.wait_ge(out_done, 16 * TH)

        @block.tensor
        def _(pe):
            def landed(n):
                pe.wait_ge(bay_in[n % BAYS], 16 * (n // BAYS + 1))

            pe.wait_ge(consts, 1)
            pe.wait_ge(small_in, 16 * 9)
            pe.transpose(bank[2][:, 0:C_END], vec_rows[:, :], ident[0:C_END, 0:C_END]).then_inc(cols_ps, 1)
            pe.wait_ge(xn_ready, TH)
            for k in range(KT):
                for h in range(TH):
                    ins = pe.transpose(bank[4 + k // 2][:, 256 * (k % 2) + P * h:256 * (k % 2) + P * h + P],
                                       xn[:, h, P * k:P * k + P], ident[:, :])
            ins.then_inc(xT_done, 1)

            def modulation(b, n, ps):
                landed(n)
                w = bay[n % BAYS].rearrange("p (k n) -> p k n", k=2)
                for k in (0, 1):
                    for j in range(4):
                        ins = pe.matmul(ps[32 * j:32 * j + 32, :], c_rep[:, 2 * b + k, :],
                                        w[:, k, 512 * j:512 * j + 512], start=(b == 0 and k == 0),
                                        stop=(b == 3 and k == 1), tile_position=(0, 32 * j))
                ins.then_inc(load_used, 1)

            pe.wait_ge(c_ready, 1)
            for b in range(4):
                modulation(b, L_ADA0 + b, bank[3])
            pe.wait_ge(cols_ready, 1)
            pe.wait_ge(mod_vec, 1)
            for b in range(4):
                ins = pe.transpose(bank[2][:, P * b:P * b + P], mod_add[:, 0, P * b:P * b + P], ident[:, :])
            ins.then_inc(ab_ps, 1)

            def column_tile(t):
                n = in_load(t // 4)
                if t % 4 == 0:
                    landed(n)
                if t - 2 == T_V:
                    pe.wait_ge(v_evac, 3)
                elif t >= 2:
                    pe.wait_ge(proj_evac, t - 1 if t - 2 < T_V else t - 2)
                w = bay[n % BAYS].rearrange("p (k n) -> p k n", k=KT)[:, :, P * (t % 4):P * (t % 4) + P]
                if t == T_V:
                    for m in range(TH):
                        for k in range(KT):
                            pe.matmul(proj[t % 2][:, P * m:P * m + P], uT[:, k, P * m:P * m + P], w[:, k, :],
                                      start=(k == 0), stop=(k == KT - 1))
                    for k in range(KT):
                        ins = pe.matmul(bank[2][0:CHUNK, 0:P], uT[:, k, CHUNK:P], w[:, k, :],
                                        start=(k == 0), stop=(k == KT - 1))
                else:
                    for k in range(KT):
                        if t == 0 and k < KT // 2:
                            pe.wait_ge(uT_ready, k + 1)
                        elif t == 0:
                            pe.wait_ge(uT_ready_v, k - KT // 2 + 1)
                        ins = pe.matmul(proj[t % 2], w[:, k, :], uT[:, k, :], start=(k == 0), stop=(k == KT - 1))
                ins.then_inc(proj_done, 1)

            def scores(h):
                kv, f = h // 8, h % 2
                if h == 0:
                    pe.wait_ge(v_evac, 3)
                    pe.wait_ge(kz_ready, 3)
                    pe.wait_ge(proj_evac, T_K + 1)
                else:
                    pe.wait_ge(negm_ready, h)
                for m in range(TH):
                    ins = pe.matmul(bank[2][:, KEYS * m:KEYS * m + KEYS], qT[:, h // 2, P * m:P * m + P],
                                    kz[:, 2 * kv + f, P * m:P * m + KEYS], start=True, stop=True)
                ins.then_inc(s_done, 1)

            def turn_probs(h):
                pe.wait_ge(p_ready, h + 1)
                if h >= 1:
                    pe.wait_ge(pt_ready, 2 * h)
                for m in range(TH):
                    pe.transpose(bank[3][:, P * m:P * m + P], sc[:, h % 2, m, CHUNK:KEYS], ident[:, :])
                pe.transpose(bank[3][0:CHUNK, 2 * P:3 * P], sc[:, h % 2, 1, 0:CHUNK], ident[:, :])\
                  .then_inc(pt_done, 1)

            def values(h):
                kv, f = h // 8, h % 2
                pe.wait_ge(pt_ready, 2 * h + 2)
                if h >= 2:
                    pe.wait_ge(attn_ready, h // 2)
                o, v = bank[4][64 * f:64 * f + 64, :], slice(64 * kv, 64 * kv + 64)
                pe.matmul(o[:, 0:P], v_tok[:, 0, v], pT[:, h % 2, 0, :], start=True, stop=True)
                pe.matmul(o[:, P:2 * P], v_tok[:, 1, v], pT[:, h % 2, 1, :], start=True, stop=False)
                pe.matmul(o[:, P:2 * P], v_prev[:, v], pT[0:CHUNK, h % 2, 2, :], start=False, stop=True)\
                  .then_inc(pv_done, 1)

            def lru_gates(k):
                pe.wait_ge(xc_ready, k + 1)
                if k == 0:
                    pe.wait_ge(late_in, 16 * 9)
                if k >= 2:
                    pe.wait_ge(ri_ready, 2 * (k - 1))
                ps = bank[5 + k % 2]
                pe.matmul(ps[:, 0:256], bd_a[:, k, :], xcT[:, k, :], start=True, stop=True)
                pe.matmul(ps[:, 256:512], bd_x[:, k, :], xcT[:, k, :], start=True, stop=True).then_inc(ri_done, 1)

            for t in range(T_END):
                column_tile(t)
                if t % 4 == 3 or t == T_END - 1:
                    pe.wait_ge(proj_done, t + 1)
                    pe.nop().then_inc(load_used, 1)
                if 0 <= t - T_S < HEADS:
                    scores(t - T_S)
                if 0 <= t - T_PT < HEADS:
                    turn_probs(t - T_PT)
                if 0 <= t - T_PV < HEADS:
                    values(t - T_PV)
                if 0 <= t - T_RI < KT:
                    lru_gates(t - T_RI)
                if (t % 4 == 3 or t == T_END - 1) and t // 4 >= RIDE:
                    g = t // 4
                    m, b = 1 + (g - RIDE) // 4, (g - RIDE) % 4
                    if (m, b) == (2, 0):
                        pe.wait_ge(ri_ready, 2 * KT)
                    modulation(b, in_load(g) + 1, bank[8 - m])

            def branch(first, src, base):
                for d in range(KT):
                    n = first + d // 4
                    if d % 4 == 0:
                        landed(n)
                    q = base + d
                    if q >= 2:
                        pe.wait_ge(br_evac, q - 1)
                    elif q == 0:
                        pe.wait_ge(proj_evac, T_END - 1)
                    w = bay[n % BAYS].rearrange("p (k n) -> p k n", k=KT)[:, :, P * (d % 4):P * (d % 4) + P]
                    for k in range(KT):
                        ins = pe.matmul(proj[q % 2], w[:, k, :], src[:, k, :], start=(k == 0), stop=(k == KT - 1))
                    ins.then_inc(br_done, 1)
                    if d % 4 == 3:
                        pe.wait_ge(br_done, q + 1)
                        pe.nop().then_inc(load_used, 1)

            pe.wait_ge(attn_ready, HEADS // 2)
            branch(L_ATTN, attnT, 0)

            def spread(m):
                pe.wait_ge(mod_vec, m + 1)
                for j in range(4):
                    ins = pe.matmul(bank[2 + j][:, :], ones[32 * j:32 * j + 1, :], mod_add[32 * j:32 * j + 1, m, :],
                                    start=True, stop=True, tile_position=(32 * j, 0))
                ins.then_inc(spread_done, 1)

            pe.wait_ge(hg_ready, 1)
            spread(1)
            branch(L_LRU, geluT, KT)
            pe.wait_ge(spread_copied, 4)
            spread(2)
            pe.wait_ge(merged, KT)
            for cc in range(2):
                landed(L_MIX + cc)
            for h in range(TH):
                if h == 1:
                    pe.wait_ge(spread_copied, 8)
                for cc in range(2):
                    w = bay[(L_MIX + cc) % BAYS].rearrange("p (k n) -> p k n", k=KT)
                    for k in range(KT):
                        ins = pe.matmul(bank[2 * h + cc][:, :], glT[:, k, P * h:P * h + P], w[:, k, :],
                                        start=(k == 0), stop=(k == KT - 1))
                    ins.then_inc(mix_done, 1)
            pe.wait_ge(mix_done, 4)
            pe.nop().then_inc(load_used, 1)
            pe.nop().then_inc(load_used, 1)

            pe.wait_ge(route_in, 32)
            for h in range(TH):
                pe.wait_ge(u2_ready, h + 1)
                for k in range(KT):
                    ins = pe.transpose(bank[4 + 2 * h + k // 4][:, P * (k % 4):P * (k % 4) + P],
                                       u2[:, h, P * k:P * k + P], ident[:, :])
                ins.then_inc(u2T_done, 1)
                pe.wait_ge(u2T_ready, 2 * h + 2)
                for k in range(KT):
                    ins = pe.matmul(bank[0][:, E * h:E * h + E], u2T[:, k, P * h:P * h + P], w_router_sb[:, k, :],
                                    start=(k == 0), stop=(k == KT - 1))
            ins.then_inc(lg_done, 1)
            pe.wait_ge(mask_ready, 1)
            pe.wait_ge(consts, 8)
            pe.matmul(bank[1][:, 0:E], before[:, :], mask[:, 0, :], start=True, stop=True)
            pe.matmul(bank[1][:, E:2 * E], before[:, :], mask[:, 1, :], start=True, stop=False)
            pe.matmul(bank[1][:, E:2 * E], ones[:, :], mask[:, 0, :], start=False, stop=True)
            pe.matmul(bank[2][0:E, 0:2], mask[:, 0, :], ones[:, 0:2], start=True, stop=False)
            pe.matmul(bank[2][0:E, 0:2], mask[:, 1, :], ones[:, 0:2], start=False, stop=True)
            pe.matmul(bank[2][0:E, E:2 * E], ones[:, 0:E], mask[:, 0, :], start=True, stop=False)
            pe.matmul(bank[2][0:E, E:2 * E], ones[:, 0:E], mask[:, 1, :], start=False, stop=True).then_inc(pos_done, 1)
            pe.wait_ge(posm_ready, 2)
            for h in range(TH):
                pe.transpose(bank[3][0:E, P * h:P * h + P], posm[:, h, :], ident[:, :])
            for h in range(TH):
                ins = pe.transpose(bank[3][0:E, S + P * h:S + P * h + P], gate[:, h, :], ident[:, :])
            ins.then_inc(posT_done, 1)
            pe.wait_ge(blocks_ready, 2)
            pe.matmul(bank[2][0:E, 2 * E:3 * E + 2], blocks_b, ahead_of, start=True, stop=True)
            pe.matmul(bank[2][0:1, 4 * E:5 * E], expert_id[:, 0:1], at_place[:, 0:E], start=True, stop=True)\
              .then_inc(cum_done, 1)
            pe.wait_ge(posT_ready, 2)
            pe.wait_ge(sel_ready, 1)
            for h in range(TH):
                pe.matmul(bank[1][:, 64 + ITEMS * h:64 + ITEMS * h + ITEMS], posT[:, P * h:P * h + P],
                          item_sel[0:E, :], start=True, stop=False)
                pe.matmul(bank[1][:, 64 + ITEMS * h:64 + ITEMS * h + ITEMS], ones[0:E, :], item_off[:, :],
                          start=False, stop=True)
            for h in range(TH):
                ins = pe.matmul(bank[1][:, 160 + ITEMS * h:160 + ITEMS * h + ITEMS], gateT[:, P * h:P * h + P],
                                item_sel[0:E, :], start=True, stop=True)
            ins.then_inc(item_done, 1)

            def gather():
                for h in range(TH):
                    for j in range(2):
                        ins = pe.matmul(bank[2][64 * j:64 * j + 64, :], oh[:, h, :], u2[:, h, 512 * j:512 * j + 512],
                                        start=(h == 0), stop=(h == TH - 1))
                ins.then_inc(gather_done, 1)

            def turn_gathered():
                for b in range(4):
                    ins = pe.transpose(bank[2][:, P * b:P * b + P], xg_tok[:, P * b:P * b + P], ident[:, :])
                ins.then_inc(xgT_done, 1)

            def combine_pair(h):
                for cc in range(2):
                    ins = pe.matmul(bank[6 + cc][:, :], pair_hot[cc][:, P * h:P * h + P], pair_rows[cc],
                                    start=True, stop=True)
                return ins

            def combine(h, banks, hot, row_of, swap):
                for cc in range(2):
                    half = slice(64 * (cc ^ swap), 64 * (cc ^ swap) + 64)
                    ins = pe.matmul(bank[banks[cc]][:, :], hot[cc][half, P * h:P * h + P], row_of[cc][half, :],
                                    start=True, stop=True)
                ins.then_inc(comb_done, 1)

            def bias(i):
                pe.wait_ge(bsel_ready, i + 1)
                for cc in range(4):
                    f = cc // 2
                    pe.matmul(bank[cc % 2][64 * f:64 * f + 64, :], bsel[:, :], b_up_parts[:, 512 * cc:512 * cc + 512],
                              start=True, stop=False, skip_group_check=True)

            def up(k, p, at):
                pe.wait_ge(w_slot[k], 16 * p + 16)
                for cc in (0, 2, 1, 3):
                    f = cc // 2
                    ins = pe.matmul(bank[cc % 2][64 * f:64 * f + 64, :], xgT[:, k % 4, k // 4, :],
                                    ring[:, at, 512 * cc:512 * cc + 512], start=False, stop=(k == KT - 1),
                                    skip_group_check=True)
                ins.then_inc(slot_used[k], 1)

            def turn_act(i):
                pe.wait_ge(act_ready, i + 1)
                for j in range(4):
                    ins = pe.transpose(bank[3][:, P * j:P * j + P], act_sb[:, P * j:P * j + P], ident[:, :])
                ins.then_inc(actT_done, 1)

            def down(j, p, at, odd=0):
                q = 8 + j // 2
                if j % 2 == 0:
                    pe.wait_ge(w_slot[q], 16 * p + 16)
                off = P * (j % 4) + CAP * (j // 4)
                for cc in range(2):
                    to = 64 * (cc ^ odd)
                    ins = pe.matmul(bank[4][to:to + 64, :], actT[:, off:off + CAP],
                                    ring[:, at, D * (j % 2) + 512 * cc:D * (j % 2) + 512 * cc + 512],
                                    start=(j == 0), stop=(j == KT - 1))
                if j % 2:
                    ins.then_inc(slot_used[q], 1)

            def turn_hot(i):
                pe.wait_ge(ohg_ready, i + 1)
                for h in range(TH):
                    ins = pe.transpose(bank[5][:, P * h:P * h + P], ohg[:, h, :], ident[:, :])
                ins.then_inc(ohgT_done, 1)

            def expert(p, turn):
                first, end = items_at(pe, p)
                up_at, down_at = [group(turn, r) for r in range(2)], group(turn, 2)
                odd = turn % 2
                bias(first)
                pe.wait_ge(xg_ready, first + 1)
                for k in range(KT):
                    up(k, p, up_at[k // 4] + k % 4)
                pe.wait_ge(oh_ready, first + 2)
                gather()
                pe.wait_ge(rows_ready, first + 1)
                pe.wait_ge(ohgT_ready, first + 1)
                pe.wait_ge(y_added, 2 * first + 1)
                combine_pair(odd).then_inc(comb_done, 2)
                turn_act(first)
                pe.wait_ge(xg_copied, first + 2)
                turn_gathered()
                with pe.If(first + 1 < end):
                    with pe.Fori(first + 1, end) as i:
                        bias(i)
                        pe.wait_ge(xg_ready, i + 1)
                        for k in range(KT):
                            up(k, p, up_at[k // 4] + k % 4)
                        pe.wait_ge(oh_ready, i + 2)
                        gather()
                        pe.wait_ge(xg_copied, i + 2)
                        turn_gathered()
                        turn_act(i)
                pe.wait_ge(actT_ready, first + 1)
                for j in range(KT):
                    down(j, p, down_at + j // 2, odd)
                    if j == 5:
                        turn_hot(first)
                with pe.If(first + 1 < end):
                    with pe.Fori(first + 1, end) as i:
                        pe.wait_ge(rows_ready, i + 1)
                        pe.wait_ge(actT_ready, i + 1)
                        for j in range(KT):
                            down(j, p, down_at + j // 2)
                            if j == 5:
                                pe.wait_ge(ohgT_ready, i + 1)
                                pe.wait_ge(y_added, 2 * i + 1)
                                turn_hot(i)
                        pe.wait_ge(rows_ready, i + 2)
                        pe.wait_ge(ohgT_ready, i + 2)
                        combine(0, (6, 7), (ohgT, ohgT), (rows, rows), 0)
                        combine(1, (5, 3), (ohgT, ohgT), (rows, rows), 0)

            pe.wait_ge(tab_ready, 1)
            n_items = pe.value_load(tab[0:1, E:E + 1], min_val=E, max_val=ITEMS - 1)
            pe.wait_ge(oh_ready, 1)
            gather()
            pe.wait_ge(xg_copied, 1)
            turn_gathered()
            pe.wait_ge(b_up_ready, 1)
            with pe.Fori(0, E // GROUPS) as turns:
                for turn in range(GROUPS):
                    expert(GROUPS * turns + turn, turn)
            pe.wait_ge(rows_ready, n_items + 1)
            pe.wait_ge(ohgT_ready, n_items + 1)
            pe.wait_ge(y_added, 2 * n_items + 1)
            combine_pair(0).then_inc(comb_done, 1)
            combine(1, (4, 5), pair_hot, pair_rows, 1)

        @block.vector
        def _(v):
            done = [0]

            def link(ins):
                done[0] += 1
                ins.then_inc(v_chain, 1)
                v.wait_ge(v_chain, done[0])

            stt = v.scalar_tensor_tensor

            def rstd(n, at, w=1):
                v.wait_ge(root_ready, n)
                link(v.reciprocal(stat[:, at:at + w], stat[:, at:at + w]))

            v.memset(eps[:, :], EPS).then_inc(eps_ready, 1)
            v.wait_ge(csig_ready, 1)
            link(v.tensor_tensor(c_act[:, :], c_col[:, :], c_sig[:, :], ALU.mult))
            v.tensor_copy(c_rep[:, :, :], c_act[:, :].rearrange("p (k o) -> p k o", o=1).to_broadcast([P, KT, 32]))\
             .then_inc(c_ready, 1)
            rstd(1, 2, TH)
            for h in range(TH):
                v.tensor_scalar(xn[:, h, :], x_tok[:, h, :], stat[:, 2 + h:3 + h], None, ALU.mult).then_inc(xn_ready, 1)
            v.wait_ge(cols_ps, 1)
            v.tensor_copy(cols[:, :], bank[2][:, 0:C_END]).then_inc(cols_ready, 1)
            v.wait_ge(cols_ready, 1)
            v.wait_ge(consts, 8)
            dist_f = dist[:, :, :].rearrange("p m k -> p (m k)")
            link(stt(out=dist_f, in0=dist_f, scalar=-1.0, in1=dist_f, op0=ALU.mult, op1=ALU.max))
            link(v.memset(dist[0:64, :, 2 * CHUNK:KEYS], MASKED))
            link(v.memset(dist[64:128, :, 0:CHUNK], MASKED))
            link(v.memset(dist[:, 0, 0:CHUNK], MASKED))
            v.wait_ge(small_in, 16 * 9)
            link(v.tensor_scalar(sink8[:, :], sinks_b[:, :], 8.0, None, ALU.mult))
            lam = cols[:, C_LAM:C_LAM + KT]
            z, w, y, y2, acc, pos = (sp_t[:, j, :] for j in range(6))
            stt(out=w, in0=lam, scalar=-1.0, in1=lam, op0=ALU.mult, op1=ALU.min).then_inc(lam_in, 1)
            v.wait_ge(lam_exp, 1)
            link(v.tensor_scalar(pos, lam, -1.0, 0.0, ALU.mult, ALU.max))
            link(v.tensor_scalar(w, z, 2.0, None, ALU.add))
            link(v.reciprocal(w, w))
            link(v.tensor_tensor(y, z, w, ALU.mult))
            link(v.tensor_tensor(y2, y, y, ALU.mult))
            link(v.tensor_scalar(acc, y2, 1.0 / 15, 1.0 / 13, ALU.mult, ALU.add))
            for n in (11, 9, 7, 5, 3, 1):
                link(v.tensor_tensor(acc, acc, y2, ALU.mult))
                link(v.tensor_scalar(acc, acc, 1.0 / n, None, ALU.add))
            link(v.tensor_tensor(acc, acc, y, ALU.mult))
            link(stt(out=acc, in0=acc, scalar=2.0, in1=pos, op0=ALU.mult, op1=ALU.add))
            link(v.tensor_scalar(neg8sp[:, :], acc, -8.0, None, ALU.mult))

            def mod_group(m, ps):
                link(stt(out=mod_add[:, m, :], in0=ps, scalar=mod_one[:, m:m + 1], in1=mod_add[:, m, :],
                         op0=ALU.add, op1=ALU.add))
                v.tensor_tensor(mod_add[:, m, :], mod_add[:, m, :], mod_mul[:, m, :], ALU.mult).then_inc(mod_vec, 1)

            v.wait_ge(late_in, 16 * 9)
            v.wait_ge(load_used, 4)
            mod_group(0, bank[3][:, :])
            v.wait_ge(ab_ps, 1)
            v.tensor_copy(ab[:, :].rearrange("p (j b) -> p b j", j=4),
                          bank[2][:, :].rearrange("p (b c) -> p b c", b=4)[:, :, 0:P:32]).then_inc(ab_ready, 1)

            v.wait_ge(ab_ready, 1)
            for k in range(KT // 2, KT):
                v.tensor_scalar(uT[:, k, :], bank[4 + k // 2][:, 256 * (k % 2):256 * (k % 2) + 256],
                                ab[:, 8 + k:9 + k], ab[:, k:k + 1], ALU.mult, ALU.add).then_inc(uT_ready_v, 1)

            v.wait_ge(proj_evac, T_K + 1)
            v.wait_ge(kz_ready, 1)
            v.tensor_copy(kz[64:128, 1, CHUNK:CHUNK + S], kz[0:64, 0, CHUNK:CHUNK + S]).then_inc(kz_ready, 1)
            v.tensor_copy(kz[0:64, 2, CHUNK:CHUNK + S], kz[64:128, 3, CHUNK:CHUNK + S]).then_inc(kz_ready, 1)
            v.wait_ge(proj_done, T_V + 1)
            for m in range(TH):
                v.tensor_tensor(v_tok[:, m, :], proj[T_V % 2][:, P * m:P * m + P], bv_b[:, :], ALU.add)\
                 .then_inc(v_evac, 1)
            v.tensor_tensor(v_prev[:, :], bank[2][0:CHUNK, 0:P], bv_b[0:CHUNK, :], ALU.add).then_inc(v_evac, 1)

            for k in range(KT):
                v.wait_ge(proj_evac, T_X + k)
                tap = lambda j: (page_x[:, k, j:j + S], cols[:, C_WCONV + 8 * j + k:C_WCONV + 8 * j + k + 1])
                src, wj = tap(0)
                link(v.tensor_scalar(xcT[:, k, :], src, wj, cols[:, C_BCONV + k:C_BCONV + k + 1], ALU.mult, ALU.add))
                for j in (1, 2, 3):
                    src, wj = tap(j)
                    ins = stt(out=xcT[:, k, :], in0=src, scalar=wj, in1=xcT[:, k, :], op0=ALU.mult, op1=ALU.add)
                    if j < 3:
                        link(ins)
                    else:
                        ins.then_inc(xc_ready, 1)

            def soften(h):
                b = h % 2
                v.wait_ge(s_done, h + 1)
                if h >= 2:
                    v.wait_ge(pt_done, h - 1)
                link(stt(out=sc[:, b, :, :].rearrange("p m k -> p (m k)"),
                         in0=dist[:, :, :].rearrange("p m k -> p (m k)"), scalar=NEG_SLOPE8[h],
                         in1=bank[2][:, 0:TH * KEYS], op0=ALU.mult, op1=ALU.add))
                link(v.tensor_reduce(soft[:, b, 0, :], sc[:, b, :, :], AX, ALU.max))
                link(v.tensor_scalar(soft[:, b, 1, :], soft[:, b, 0, :], sink8[:, h:h + 1], -0.125, ALU.max, ALU.mult))
                v.tensor_scalar(soft[:, b, 6, :], soft[:, b, 1, :], sinks_b[:, h:h + 1], None, ALU.add)\
                 .then_inc(negm_ready, 1)

            def normalise(h):
                b = h % 2
                v.wait_ge(exp_done, 3 * h + 3)
                link(v.tensor_tensor(soft[:, b, 4, :], soft[:, b, 2, :], soft[:, b, 3, :], ALU.add))
                link(v.reciprocal(soft[:, b, 5, :], soft[:, b, 4, :]))
                for m in range(TH):
                    ins = v.tensor_scalar(sc[:, b, m, :], sc[:, b, m, :], soft[:, b, 5, m:m + 1], None, ALU.mult)
                    if m == 0:
                        link(ins)
                    else:
                        ins.then_inc(p_ready, 1)

            for h in range(HEADS + 1):
                if h < HEADS:
                    soften(h)
                if h >= 1:
                    normalise(h - 1)

            v.wait_ge(ri_ready, 2 * KT)
            for half in range(2):
                ks = slice(4 * half, 4 * half + 4)
                la, e, zz, ii, xx = rT[:, ks, :], eT[:, ks, :], zT[:, ks, :], iT[:, ks, :], xcT[:, ks, :]
                v.tensor_tensor(la, la, neg8sp[:, ks].rearrange("p (k o) -> p k o", o=1).to_broadcast([P, 4, S]),
                                ALU.mult).then_inc(log_a, 1)
                v.wait_ge(log_a, half + 1)
                yy = page_x[:, ks, 3:3 + S]
                v.wait_ge(proj_evac, T_G)
                link(v.tensor_scalar(yy, la, 0.125, None, ALU.mult))
                link(v.tensor_scalar(e, yy, 1.0 / 120, None, ALU.mult))
                for coef in (1.0 / 24, 1.0 / 6, 0.5, 1.0):
                    link(stt(out=e, in0=e, scalar=coef, in1=yy, op0=ALU.add, op1=ALU.mult))
                for _ in range(3):
                    link(stt(out=e, in0=e, scalar=2.0, in1=e, op0=ALU.add, op1=ALU.mult))
                v.wait_ge(a_tab, half + 1)
                link(v.tensor_scalar(zz, zz, -1.0, None, ALU.add))
                link(v.tensor_scalar(la, la, LRU_SMALL, None, ALU.is_lt))
                link(v.copy_predicated(e, la.bitcast(I32), zz))
                v.tensor_scalar(la, e, 2.0, None, ALU.add).then_inc(v_chain, 1)
                done[0] += 1
                v.wait_ge(v_chain, done[0])
                v.tensor_tensor(zz, la, e, ALU.mult).then_inc(lru_w, 1)
                link(v.tensor_tensor(ii, ii, xx, ALU.mult))
                link(v.tensor_scalar(e, e, 1.0, None, ALU.add))
                v.wait_ge(lru_root, half + 1)
                link(v.tensor_tensor(ii, ii, zz, ALU.mult))
                for k in range(4 * half, 4 * half + 4):
                    link(v.tensor_tensor_scan(hT[:, k, :], eT[:, k, :], iT[:, k, :], 0.0, ALU.mult, ALU.add))
                ins = v.tensor_tensor(geluT[:, ks, :], geluT[:, ks, :], hT[:, ks, :], ALU.mult)
                if half == 0:
                    v.wait_ge(proj_evac, T_GA - 1)
                    link(ins)
                else:
                    ins.then_inc(hg_ready, 1)
            v.wait_ge(load_used, in_load(RIDE + 3) + 2)
            mod_group(1, bank[7][:, :])
            v.wait_ge(load_used, in_load(RIDE + 7) + 2)
            mod_group(2, bank[6][:, :])
            v.wait_ge(proj_evac, T_END - 1)
            v.wait_ge(br_evac, KT)
            link(v.tensor_tensor(gaT, gaT, qT, ALU.mult))
            for q in range(KT, 2 * KT):
                v.wait_ge(br_done, q + 1)
                d = q - KT
                v.tensor_tensor(glT[:, d, :], glT[:, d, :], proj[q % 2], ALU.mult).then_inc(br_evac, 1)
                v.wait_ge(br_evac, q + 1)
                v.tensor_tensor(glT[:, d, :], glT[:, d, :], gaT[:, d, :], ALU.add).then_inc(merged, 1)
            v.wait_ge(mod_vec, 3)
            v.wait_ge(b_up_in, 16)
            for j in range(3):
                part = b_up_parts[E * j:E * j + E, :]
                if j < 2:
                    link(v.tensor_copy(part, b_up_raw))
                    link(v.tensor_tensor(b_up_raw, b_up_raw, part, ALU.subtract))
                else:
                    v.tensor_copy(part, b_up_raw).then_inc(b_up_ready, 1)

            v.wait_ge(spread_copied, 8)
            for h in range(TH):
                c0 = 4 + 6 * h
                v.wait_ge(sq1_ready, 2 * h + 2)
                v.tensor_tensor(stat[:, c0 + 2:c0 + 3], stat[:, c0:c0 + 1], stat[:, c0 + 1:c0 + 2], ALU.add)\
                 .then_inc(sum_ready, 1)
                rstd(2 * h + 2, c0 + 3)
                for cc in range(2):
                    part = slice(512 * cc, 512 * cc + 512)
                    link(stt(out=scrap[:, h, part], in0=bank[2 * h + cc][:, :], scalar=stat[:, c0 + 3:c0 + 4],
                             in1=gate1_b[:, part], op0=ALU.mult, op1=ALU.mult))
                v.tensor_tensor(x_tok[:, h, :], x_tok[:, h, :], scrap[:, h, :], ALU.add).then_inc(x1_ready, 1)
                rstd(2 * h + 3, c0 + 5)
                link(stt(out=u2[:, h, :], in0=x_tok[:, h, :], scalar=stat[:, c0 + 5:c0 + 6], in1=scale2_b,
                         op0=ALU.mult, op1=ALU.mult))
                v.tensor_tensor(u2[:, h, :], u2[:, h, :], shift2_b, ALU.add).then_inc(u2_ready, 1)
                v.wait_ge(u2T_done, h + 1)
                v.tensor_copy(u2T[:, 4:8, P * h:P * h + P], bank[5 + 2 * h][:, :].rearrange("p (k t) -> p k t", t=P))\
                 .then_inc(u2T_ready, 1)

            both = lambda col: col.to_broadcast([P, TH, E])
            v.wait_ge(lg_done, 1)
            link(v.tensor_tensor(lg, bank[0][:, 0:TH * E].rearrange("p (h e) -> p h e", h=TH),
                                 b_router_b[:, :].rearrange("p (o e) -> p o e", o=1).to_broadcast([P, TH, E]), ALU.add))
            for h in range(TH):
                link(v.max(top8[:, h, :], lg[:, h, :]))
            v.tensor_scalar(allow[:, :, 2], top8[:, :, 0], -1.0, None, ALU.mult).then_inc(top_ready, 1)
            link(v.tensor_tensor(gt, lg, both(top8[:, :, TOPK - 1:TOPK]), ALU.is_gt))
            link(v.tensor_tensor(eq, lg, both(top8[:, :, TOPK - 1:TOPK]), ALU.is_equal))
            link(v.tensor_reduce(allow[:, :, 0], gt, AX, ALU.add))
            for h in range(TH):
                link(v.tensor_tensor_scan(eq_n[:, h, :], ones[:, 0:E], eq[:, h, :], allow[:, h, 0:1],
                                          ALU.mult, ALU.add))
            link(stt(out=eq, in0=eq_n, scalar=float(TOPK), in1=eq, op0=ALU.is_le, op1=ALU.mult))
            v.tensor_tensor(mask, gt, eq, ALU.add).then_inc(mask_ready, 1)
            v.wait_ge(mask_ready, 1)
            v.wait_ge(gexp_ready, TH)
            link(v.tensor_tensor(gate[:, :, :], gate[:, :, :], mask[:, :, :], ALU.mult))
            link(v.tensor_reduce(allow[:, :, 0], gate[:, :, :], AX, ALU.add))
            link(v.reciprocal(allow[:, :, 1], allow[:, :, 0]))
            v.tensor_tensor(gate, gate, both(allow[:, :, 1:2]), ALU.mult).then_inc(posm_ready, 1)
            v.wait_ge(pos_done, 1)
            flat = lambda t: t[:, :, :].rearrange("p h e -> p (h e)")
            link(stt(out=flat(posm), in0=bank[1][:, 0:2 * E], scalar=BIG, in1=flat(mask), op0=ALU.add, op1=ALU.mult))
            v.tensor_scalar(flat(posm), flat(posm), -BIG, None, ALU.add).then_inc(posm_ready, 1)
            link(v.tensor_copy(blocks[:, 4:6], bank[2][0:E, 0:2]))
            link(v.tensor_scalar(blocks[:, 0:2], blocks[:, 4:6], float(CAP), 1.0, ALU.is_gt, ALU.add))
            link(stt(out=blocks[:, 0:2], in0=blocks[:, 4:6], scalar=2.0 * CAP, in1=blocks[:, 0:2],
                     op0=ALU.is_gt, op1=ALU.add))
            stt(out=blocks[:, 0:2], in0=blocks[:, 4:6], scalar=3.0 * CAP, in1=blocks[:, 0:2],
                op0=ALU.is_gt, op1=ALU.add).then_inc(blocks_ready, 1)
            v.wait_ge(numbers, 1)
            link(stt(out=place[:, 0:1], in0=blocks[:, 4:5], scalar=float(E), in1=key_col[:, 0:1],
                     op0=ALU.mult, op1=ALU.add))
            link(stt(out=keys, in0=bank[2][0:E, E:2 * E], scalar=float(E), in1=key_row, op0=ALU.mult, op1=ALU.add))
            link(v.tensor_scalar(rank_t, keys, place[:, 0:1], None, ALU.is_gt))
            link(v.tensor_reduce(place[:, 1:2], rank_t, AX, ALU.add))
            link(v.tensor_scalar(rank_hot, iota_n[:, 0:E], place[:, 1:2], None, ALU.is_equal))
            link(stt(out=rank_t, in0=rank_hot, scalar=key_col[:, 1:2], in1=place_of, op0=ALU.mult, op1=ALU.mult))
            link(v.tensor_reduce(place[:, 2:3], rank_t, AX, ALU.add))
            link(v.tensor_scalar(at_place, iota_n[:, 0:E + 2], place[:, 2:3], None, ALU.is_equal))
            link(v.tensor_scalar(ahead_of, iota_n[:, 0:E + 2], place[:, 2:3], None, ALU.is_gt))
            v.wait_ge(blocks_ready, 1)
            v.tensor_copy(blocks_b, blocks[:, 0:1].to_broadcast([E, E])).then_inc(blocks_ready, 1)
            v.wait_ge(posT_done, 1)
            v.tensor_copy(posT[:, :], bank[3][0:E, 0:S]).then_inc(posT_ready, 1)
            v.wait_ge(hot_zeroed, 1)
            v.tensor_copy(gateT, bank[3][0:E, S:2 * S]).then_inc(posT_ready, 1)
            v.wait_ge(cum_done, 1)
            link(v.tensor_tensor(ahead_t, at_place[:, 0:E], bank[2][0:E, 2 * E:3 * E], ALU.mult))
            link(v.tensor_reduce(blocks[:, 2:3], ahead_t, AX, ALU.add))
            link(v.tensor_tensor(blocks[:, 6:7], blocks[:, 2:3], blocks[:, 0:1], ALU.add))
            link(v.tensor_scalar(item_t[:, 0, :], iota_n[:, :], blocks[:, 2:3], None, ALU.is_ge))
            link(v.tensor_scalar(item_t[:, 1, :], iota_n[:, :], blocks[:, 6:7], None, ALU.is_lt))
            for j in range(3):
                link(v.tensor_tensor(item_sel[E * j:E * j + E, :], item_t[:, 0, :], item_t[:, 1, :], ALU.mult))
            link(v.tensor_scalar(item_t[:, 0, :], iota_n[:, :], blocks[:, 2:3], -float(CAP), ALU.subtract, ALU.mult))
            stt(out=item_off[:, :], in0=item_t[:, 0, :], scalar=BIG, in1=item_sel[0:E, :],
                op0=ALU.add, op1=ALU.mult).then_inc(sel_ready, 1)
            v.wait_ge(item_done, 1)
            link(v.tensor_scalar(pos_item[:, :, :].rearrange("p h i -> p (h i)"), bank[1][:, 64:64 + TH * ITEMS],
                                 -BIG, None, ALU.add))
            link(v.tensor_copy(gate_item[:, :, :].rearrange("p h i -> p (h i)"), bank[1][:, 160:160 + TH * ITEMS]))
            link(v.tensor_copy(tab[:, 0:E + 2], bank[2][0:1, 2 * E:3 * E + 2]))
            v.tensor_copy(tab[:, T_ID:T_ID + E], bank[2][0:1, 4 * E:5 * E]).then_inc(tab_ready, 1)
            v.wait_ge(tab_ready, 1)
            n_items = v.value_load(tab[0:1, E:E + 1], min_val=E, max_val=ITEMS - 1)

            def add_half(h, n, banks=(6, 7)):
                v.wait_ge(comb_done, n)
                for cc in range(2):
                    part = y_acc[:, h, 512 * cc:512 * cc + 512]
                    ins = v.tensor_tensor(part, part, bank[banks[cc]][:, :], ALU.add)
                return ins

            def same_slot(dst, width, i):
                return v.tensor_tensor(dst, iota_s[:, :, 0:width],
                                       pos_item[:, :, bass.ds(i, 1)].to_broadcast([P, TH, width]), ALU.is_equal)

            same_slot(oh, CAP, 0).then_inc(oh_ready, 1)
            v.wait_ge(xgT_done, 1)
            v.tensor_copy(xgT_flat, bank[2][:, :]).then_inc(xg_ready, 1)
            two = lambda b, o: b[:, o:512:2]

            def activate(i):
                same_slot(oh, CAP, i + 1).then_inc(oh_ready, 1)
                v.wait_ge(slot_used[7], i + 1)
                for b in range(2):
                    ins = v.tensor_scalar(glu[:, 256 * b:256 * b + 256], two(bank[b], 0), LIMIT, None, ALU.min)
                ins.then_inc(glu_ready, 1)
                for b in range(2):
                    ins = v.tensor_scalar(lin[:, 256 * b:256 * b + 256], two(bank[b], 1), LIMIT, -LIMIT,
                                          ALU.min, ALU.max)
                ins.then_inc(lin_ready, 1)
                v.wait_ge(glu_ready, i + 1)
                v.wait_ge(lin_ready, i + 1)
                stt(out=lin, in0=lin, scalar=1.0, in1=glu, op0=ALU.add, op1=ALU.mult).then_inc(gl_ready, 1)
                v.wait_ge(gl_ready, i + 1)
                v.wait_ge(sig_ready, i + 1)
                v.tensor_tensor(act_sb, lin, sig, ALU.mult).then_inc(act_ready, 1)
                v.wait_ge(xgT_done, i + 2)
                v.tensor_copy(xgT_flat, bank[2][:, :]).then_inc(xg_ready, 1)

            def gated_hot(i):
                same_slot(ohg_h, P, i).then_inc(ohg_half, 1)
                v.wait_ge(ohg_half, i + 1)
                v.tensor_tensor(ohg, ohg_h, gate_item[:, :, bass.ds(i, 1)].to_broadcast([P, TH, P]), ALU.mult)\
                 .then_inc(ohg_ready, 1)

            def expert(p, odd):
                first, end = items_at(v, p)
                activate(first)
                add_half(odd, 2 * first + 2).then_inc(y_added, 2)
                with v.If(first + 1 < end):
                    with v.Fori(first + 1, end) as i:
                        activate(i)
                gated_hot(first)
                v.wait_ge(ohgT_done, first + 1)
                for g in range(2):
                    part = slice(64 * g, 64 * g + 64)
                    ins = v.tensor_copy(pair_hot[g ^ odd][part, :], bank[5][part, 0:S])
                ins.then_inc(ohgT_ready, 1)
                with v.If(first + 1 < end):
                    with v.Fori(first + 1, end) as i:
                        gated_hot(i)
                        v.wait_ge(ohgT_done, i + 1)
                        v.tensor_copy(ohgT, bank[5][:, 0:S]).then_inc(ohgT_ready, 1)
                        add_half(0, 2 * i + 1).then_inc(y_added, 1)
                        add_half(1, 2 * i + 2, (5, 3)).then_inc(y_added, 1)

            with v.Fori(0, E // 2) as pairs:
                for odd in range(2):
                    expert(2 * pairs + odd, odd)
            for h in range(TH):
                add_half(h, 2 * n_items + h + 1, (6 - 2 * h, 7 - 2 * h)).then_inc(yacc_done, 1)
            for h in range(TH):
                rstd(6 + h, 17 + 2 * h)
                stt(out=y_acc[:, h, :], in0=y_acc[:, h, :], scalar=stat[:, 17 + 2 * h:18 + 2 * h], in1=gate2_b,
                    op0=ALU.mult, op1=ALU.mult).then_inc(out_scaled, 1)
                v.wait_ge(out_scaled, h + 1)
                v.tensor_tensor(x_tok[:, h, 384:D], x_tok[:, h, 384:D], y_acc[:, h, 384:D], ALU.add)\
                 .then_inc(out_ready[h], 1)


_INS = ["x", "c", "w_ada", "b_ada", "g_pre_mix", "g_post_mix", "w_in", "b_in", "w_conv", "b_conv", "w_rg_a", "b_rg_a",
        "w_rg_x", "b_rg_x", "lru_lambda", "attn_sinks", "w_br_attn", "w_br_lru", "w_mix_out", "g_pre_moe",
        "g_post_moe", "w_router", "b_router", "w_up", "b_up", "w_down", "b_down"]
_OUTS = [((1, S, D), "float32")]


def kernel(**inputs):
    import numpy as _np
    import concourse.bacc as _bacc
    from concourse import mybir as _mybir
    from concourse.bass_utils import run_bass_kernel_spmd as _run

    nc = _bacc.Bacc("TRN2", target_bir_lowering=False, num_devices=1)
    arrays, args = {}, []
    for name in _INS:
        a = _np.ascontiguousarray(inputs[name])
        arrays[f"in_{name}_dram"] = a
        args.append(nc.dram_tensor(f"in_{name}_dram", a.shape, _mybir.dt.from_np(a.dtype), kind="ExternalInput").ap())
    for i, (shape, dtype) in enumerate(_OUTS):
        dt = _mybir.dt.from_np(_np.dtype(dtype))
        args.append(nc.dram_tensor(f"out_{i}_dram", shape, dt, kind="ExternalOutput").ap())
    hybrid_block(nc, *args)
    r = _run(nc, [arrays], core_ids=[0])
    return r.results[0]["out_0_dram"]
```
